# Optimizing a Trainium2 kernel written in Bass

```python
import math, functools
import jax, jax.numpy as jnp
from jax import lax
import numpy as np

D_MODEL = 1024
BATCH = 1
SEQ = 256
DEPTH = 1
DEC_BATCH = 8
DEC_SEQ = 1
PAST_LEN = 1024
PAGE_SIZE = 128

GDN_HEADS = 8
GDN_DK = 128
GDN_DV = 128
CONV_WIDTH = 4
GDN_CHUNK = 64
GDN_QK_W = GDN_HEADS * GDN_DK
GDN_V_W = GDN_HEADS * GDN_DV
CONV_DIM = 2 * GDN_QK_W + GDN_V_W
MLA_HEADS = 8
Q_LORA = 512
KV_LORA = 512
QK_NOPE = 128
QK_ROPE = 64
V_HEAD = 128
MLA_V_W = MLA_HEADS * V_HEAD
ROPE_THETA = 10000.0
Q_BLOCK = 128
ATTN_SCALE = (QK_NOPE + QK_ROPE) ** -0.5
N_EXPERTS = 32
TOP_K = 4
D_EXPERT = 1024
SWIGLU_LIMIT = 7.0
SWIGLU_ALPHA = 1.702
EXPERT_BLOCK = 128
NORM_EPS = 1e-6
IN_SIZES = (CONV_DIM, GDN_V_W, GDN_HEADS, GDN_HEADS, Q_LORA, KV_LORA, QK_ROPE, D_MODEL, D_MODEL)
IN_COLS = CONV_DIM + GDN_V_W + 2 * GDN_HEADS + Q_LORA + KV_LORA + QK_ROPE + 2 * D_MODEL

kernel_name = 'hybrid_gdn_mla_moe_adaln_step'

def rmsnorm(x, w):
    xf = x.astype(jnp.float32)
    y = xf * lax.rsqrt(jnp.mean(xf * xf, axis=-1, keepdims=True) + NORM_EPS)
    return (y * w.astype(jnp.float32)).astype(x.dtype)

def l2norm(x):
    xf = x.astype(jnp.float32)
    return xf * lax.rsqrt(jnp.sum(xf * xf, axis=-1, keepdims=True) + NORM_EPS)

def rope(x, pos):
    half = QK_ROPE // 2
    inv = ROPE_THETA ** (-jnp.arange(half, dtype=jnp.float32) / half)
    ang = pos.astype(jnp.float32)[:, None] * inv[None, :]
    cos = jnp.cos(ang)[:, None, :]
    sin = jnp.sin(ang)[:, None, :]
    x1 = x[..., :half].astype(jnp.float32)
    x2 = x[..., half:].astype(jnp.float32)
    return jnp.concatenate([x1 * cos - x2 * sin, x1 * sin + x2 * cos], axis=-1).astype(x.dtype)

def short_conv(u, buf, w):
    T = u.shape[1]
    xp = jnp.concatenate([buf.astype(u.dtype), u], axis=1)
    y = xp[:, 0:T] * w[:, 0]
    for j in range(1, CONV_WIDTH):
        y = y + xp[:, j:j + T] * w[:, j]
    return jax.nn.silu(y), xp[:, -(CONV_WIDTH - 1):]

def delta_rule_chunked(q, k, v, beta, g, S0):
    Bn, T, H, _ = q.shape
    nc = T // GDN_CHUNK

    def blocks(x):
        x = x.astype(jnp.float32).reshape((Bn, nc, GDN_CHUNK, H) + x.shape[3:])
        return jnp.moveaxis(x, (1, 3), (0, 2))

    qc, kc, vc, bc, gc = blocks(q), blocks(k), blocks(v), blocks(beta), blocks(g)
    gam = jnp.cumsum(gc, axis=-1)
    causal = jnp.tril(jnp.ones((GDN_CHUNK, GDN_CHUNK), bool))
    strict = jnp.tril(jnp.ones((GDN_CHUNK, GDN_CHUNK), bool), -1)
    decay = jnp.exp(jnp.where(causal, gam[..., :, None] - gam[..., None, :], -jnp.inf))
    kb = kc * bc[..., None]
    a_kk = jnp.where(strict, jnp.einsum('nbhik,nbhjk->nbhij', kb, kc) * decay, 0.0)
    t_mat = a_kk + jnp.eye(GDN_CHUNK, dtype=jnp.float32)

    def solve(rhs):
        return lax.linalg.triangular_solve(t_mat, rhs, left_side=True, lower=True, unit_diagonal=True)

    u = solve(vc * bc[..., None])
    w = solve(kb * jnp.exp(gam)[..., None])
    a_qk = jnp.einsum('nbhik,nbhjk->nbhij', qc, kc) * decay

    def step(S, xs):
        q_i, k_i, u_i, w_i, gam_i, aqk_i = xs
        v_new = u_i - jnp.einsum('bhck,bhkv->bhcv', w_i, S)
        o = (jnp.einsum('bhck,bhkv->bhcv', q_i * jnp.exp(gam_i)[..., None], S)
             + jnp.einsum('bhij,bhjv->bhiv', aqk_i, v_new))
        g_last = gam_i[..., -1:]
        S = (S * jnp.exp(g_last)[..., None]
             + jnp.einsum('bhck,bhcv->bhkv', k_i * jnp.exp(g_last - gam_i)[..., None], v_new))
        return S, o

    S, o = lax.scan(step, S0.astype(jnp.float32), (qc, kc, u, w, gam, a_qk))
    o = jnp.moveaxis(o, (0, 2), (1, 3)).reshape(Bn, T, H, v.shape[-1])
    return o, S

def delta_rule_recurrent(q, k, v, beta, g, S0):
    xs = tuple(jnp.swapaxes(t.astype(jnp.float32), 0, 1) for t in (q, k, v, beta, g))

    def step(S, inp):
        qt, kt, vt, bt, gt = inp
        S = S * jnp.exp(gt)[..., None, None]
        vn = bt[..., None] * (vt - jnp.einsum('bhk,bhkv->bhv', kt, S))
        S = S + jnp.einsum('bhk,bhv->bhkv', kt, vn)
        return S, jnp.einsum('bhk,bhkv->bhv', qt, S)

    S, o = lax.scan(step, S0.astype(jnp.float32), xs)
    return jnp.swapaxes(o, 0, 1), S

def mla_causal_attention(q_lat, q_pe, lat, kpe):
    Bn, T, H, _ = q_lat.shape
    nq = T // Q_BLOCK
    qb = jnp.swapaxes(q_lat.reshape(Bn, nq, Q_BLOCK, H, KV_LORA), 0, 1)
    pb = jnp.swapaxes(q_pe.reshape(Bn, nq, Q_BLOCK, H, QK_ROPE), 0, 1)
    kpos = jnp.arange(T)

    def one_block(args):
        ql, qp, i = args
        s = (jnp.einsum('bqhc,bkc->bhqk', ql, lat)
             + jnp.einsum('bqhr,bkr->bhqk', qp, kpe)).astype(jnp.float32) * ATTN_SCALE
        qpos = i * Q_BLOCK + jnp.arange(Q_BLOCK)
        s = jnp.where(kpos[None, :] <= qpos[:, None], s, -jnp.inf)
        p = jax.nn.softmax(s, axis=-1).astype(lat.dtype)
        return jnp.einsum('bhqk,bkc->bqhc', p, lat)

    o = lax.map(one_block, (qb, pb, jnp.arange(nq)))
    return jnp.swapaxes(o, 0, 1).reshape(Bn, T, H, KV_LORA)

def mla_paged_attention(q_lat, q_pe, lat, kpe, cache_kv, cache_pe, page_table, layer):
    Bn, T, H, _ = q_lat.shape
    qf = q_lat.astype(jnp.float32)
    pf = q_pe.astype(jnp.float32)

    def scores(kv, pe):
        return (jnp.einsum('bthc,bpc->bthp', qf, kv.astype(jnp.float32))
                + jnp.einsum('bthr,bpr->bthp', pf, pe.astype(jnp.float32))) * ATTN_SCALE

    def update(carry, s, kv):
        m, l, acc = carry
        m_new = jnp.maximum(m, jnp.max(s, axis=-1))
        corr = jnp.exp(m - m_new)
        p = jnp.exp(s - m_new[..., None])
        acc = acc * corr[..., None] + jnp.einsum('bthp,bpc->bthc', p, kv.astype(jnp.float32))
        return (m_new, l * corr + jnp.sum(p, axis=-1), acc)

    def page_step(carry, phys):
        kv = cache_kv[layer, phys]
        pe = cache_pe[layer, phys]
        return update(carry, scores(kv, pe), kv), None

    init = (jnp.full((Bn, T, H), -jnp.inf, jnp.float32), jnp.zeros((Bn, T, H), jnp.float32),
            jnp.zeros((Bn, T, H, KV_LORA), jnp.float32))
    carry, _ = lax.scan(page_step, init, jnp.swapaxes(page_table, 0, 1))
    causal = jnp.tril(jnp.ones((T, T), bool))
    s_new = jnp.where(causal[None, :, None, :], scores(lat, kpe), -jnp.inf)
    m, l, acc = update(carry, s_new, lat)
    return (acc / l[..., None]).astype(q_lat.dtype)

def gdn_branch(qkv, z, b, a, conv_buf, ssm_state, lw, chunked):
    Bn, T, _ = qkv.shape
    qkv, new_buf = short_conv(qkv, conv_buf, lw['conv_w'])
    q, k, v = jnp.split(qkv, [GDN_QK_W, 2 * GDN_QK_W], axis=-1)
    q = l2norm(q.reshape(Bn, T, GDN_HEADS, GDN_DK)) * GDN_DK ** -0.5
    k = l2norm(k.reshape(Bn, T, GDN_HEADS, GDN_DK))
    v = v.reshape(Bn, T, GDN_HEADS, GDN_DV)
    beta = jax.nn.sigmoid(b.astype(jnp.float32))
    g = -jnp.exp(lw['A_log'].astype(jnp.float32)) * jax.nn.softplus(a.astype(jnp.float32) + lw['dt_bias'].astype(jnp.float32))
    if chunked:
        o, S = delta_rule_chunked(q, k, v, beta, g, ssm_state)
    else:
        o, S = delta_rule_recurrent(q, k, v, beta, g, ssm_state)
    o = rmsnorm(o.astype(z.dtype), lw['gdn_norm_w']) * jax.nn.silu(z.reshape(Bn, T, GDN_HEADS, GDN_DV))
    return o.reshape(Bn, T, GDN_V_W) @ lw['w_o_gdn'], new_buf, S

def mla_branch(cq, ckv, kpe, pos, lw, attend):
    Bn, T, _ = cq.shape
    q = (rmsnorm(cq, lw['q_norm_w']) @ lw['w_uq']).reshape(Bn, T, MLA_HEADS, QK_NOPE + QK_ROPE)
    q_nope = q[..., :QK_NOPE]
    q_pe = rope(q[..., QK_NOPE:], pos)
    lat = rmsnorm(ckv, lw['kv_norm_w'])
    kpe = rope(kpe[:, :, None, :], pos)[:, :, 0, :]
    q_lat = jnp.einsum('bthn,hcn->bthc', q_nope, lw['w_uk'])
    o_lat = attend(q_lat, q_pe, lat, kpe)
    o = jnp.einsum('bthc,hcv->bthv', o_lat, lw['w_uv'])
    return o.reshape(Bn, T, MLA_V_W) @ lw['w_o_mla'], lat, kpe

def moe_ffn(h, lw):
    N = h.shape[0]
    M = N * TOP_K
    logits = h.astype(jnp.float32) @ lw['w_router'].astype(jnp.float32) + lw['b_router'].astype(jnp.float32)
    top_v, top_e = lax.top_k(logits, TOP_K)
    gate = jax.nn.softmax(top_v, axis=-1).astype(h.dtype)
    flat_e = top_e.reshape(M)
    order = jnp.argsort(flat_e)
    e_sorted = flat_e[order]
    tok_sorted = order // TOP_K
    counts = jnp.bincount(flat_e, length=N_EXPERTS)
    padded = (counts + EXPERT_BLOCK - 1) // EXPERT_BLOCK * EXPERT_BLOCK
    pad_end = jnp.cumsum(padded)
    pad_start = pad_end - padded
    grp_start = jnp.cumsum(counts) - counts
    slot = pad_start[e_sorted] + jnp.arange(M) - grp_start[e_sorted]
    n_blocks = -(-M // EXPERT_BLOCK) + N_EXPERTS
    n_slots = n_blocks * EXPERT_BLOCK
    slot_tok = jnp.full((n_slots,), N, jnp.int32).at[slot].set(tok_sorted.astype(jnp.int32))
    h_pad = jnp.concatenate([h, jnp.zeros((1, h.shape[1]), h.dtype)], axis=0)[slot_tok]
    h_pad = h_pad.reshape(n_blocks, EXPERT_BLOCK, h.shape[1])
    blk_e = jnp.minimum(jnp.searchsorted(pad_end, jnp.arange(n_blocks) * EXPERT_BLOCK, side='right'), N_EXPERTS - 1)

    def run_block(args):
        xb, e = args
        gu = xb @ lw['w_gu'][e] + lw['b_gu'][e]
        gt = jnp.minimum(gu[:, :D_EXPERT], SWIGLU_LIMIT)
        up = jnp.clip(gu[:, D_EXPERT:], -SWIGLU_LIMIT, SWIGLU_LIMIT)
        act = (up + 1.0) * gt * jax.nn.sigmoid(SWIGLU_ALPHA * gt)
        return act @ lw['w_dn'][e] + lw['b_dn'][e]

    y_pad = lax.map(run_block, (h_pad, blk_e)).reshape(n_slots, h.shape[1])
    y_sorted = y_pad[slot] * gate.reshape(M)[order][:, None]
    return jax.ops.segment_sum(y_sorted, tok_sorted, num_segments=N)

def decoder_layer(x, c, pos, conv_buf, ssm_state, lw, chunked, attend):
    Bn, T, D = x.shape
    mod = (c @ lw['w_ada'] + lw['b_ada']).reshape(Bn, 6, D)
    sh1, sc1, g1, sh2, sc2, g2 = [mod[:, i, None, :] for i in range(6)]
    h = rmsnorm(x, lw['norm_mix_w']) * (1.0 + sc1) + sh1
    proj = h @ lw['w_in']
    offsets = [int(o) for o in np.cumsum(IN_SIZES)[:-1]]
    qkv, z, b, a, cq, ckv, kpe, gate_a, gate_b = jnp.split(proj, offsets, axis=-1)
    y_a, new_buf, new_ssm = gdn_branch(qkv, z, b, a, conv_buf, ssm_state, lw, chunked)
    y_b, lat, kpe_rot = mla_branch(cq, ckv, kpe, pos, lw, attend)
    merged = jax.nn.sigmoid(gate_a) * y_a + jax.nn.sigmoid(gate_b) * y_b
    x = x + g1 * (merged @ lw['w_out'])
    h = rmsnorm(x, lw['norm_ffn_w']) * (1.0 + sc2) + sh2
    x = x + g2 * moe_ffn(h.reshape(Bn * T, D), lw).reshape(Bn, T, D)
    return x, lat, kpe_rot, new_ssm, new_buf

def final_norm(x, c, w_ada_final, b_ada_final, norm_final_w):
    mod = (c @ w_ada_final + b_ada_final).reshape(c.shape[0], 2, x.shape[-1])
    return rmsnorm(x, norm_final_w) * (1.0 + mod[:, 1, None, :]) + mod[:, 0, None, :]

def setup_inputs(seed: int = 0) -> dict:
    key = jax.random.key(seed)
    ks = iter(jax.random.split(key, 48))
    f32 = jnp.float32
    n_pages = PAST_LEN // PAGE_SIZE
    n_phys = (DEC_BATCH * n_pages * 5) // 4

    def nrm(shape, scale=1.0):
        return scale * jax.random.normal(next(ks), shape, f32)

    def gain(shape):
        return 1.0 + nrm(shape, 0.02)

    page_table = jax.random.permutation(next(ks), n_phys)[:DEC_BATCH * n_pages]
    page_table = page_table.reshape(DEC_BATCH, n_pages).astype(jnp.int32)
    A_log = jnp.log(jax.random.uniform(next(ks), (DEPTH, GDN_HEADS), f32, 1.0, 16.0))
    dt = jnp.exp(jax.random.uniform(next(ks), (DEPTH, GDN_HEADS), f32, math.log(1e-3), math.log(1e-1)))
    dt_bias = dt + jnp.log(-jnp.expm1(-dt))
    return {
        'x_prompt': nrm((BATCH, SEQ, D_MODEL)),
        'x_sample': nrm((DEC_BATCH, DEC_SEQ, D_MODEL)),
        'c_prompt': nrm((BATCH, D_MODEL)),
        'c_sample': nrm((DEC_BATCH, D_MODEL)),
        'cache_kv': nrm((DEPTH, n_phys, PAGE_SIZE, KV_LORA)),
        'cache_pe': nrm((DEPTH, n_phys, PAGE_SIZE, QK_ROPE)),
        'state_ssm': nrm((DEPTH, DEC_BATCH, GDN_HEADS, GDN_DK, GDN_DV)),
        'state_conv': nrm((DEPTH, DEC_BATCH, CONV_WIDTH - 1, CONV_DIM)),
        'page_table': page_table,
        'norm_mix_w': gain((DEPTH, D_MODEL)),
        'norm_ffn_w': gain((DEPTH, D_MODEL)),
        'w_ada': nrm((DEPTH, D_MODEL, 6 * D_MODEL), 0.3 * D_MODEL ** -0.5),
        'b_ada': nrm((DEPTH, 6 * D_MODEL), 0.02),
        'w_in': nrm((DEPTH, D_MODEL, IN_COLS), D_MODEL ** -0.5),
        'conv_w': nrm((DEPTH, CONV_DIM, CONV_WIDTH), CONV_WIDTH ** -0.5),
        'A_log': A_log,
        'dt_bias': dt_bias,
        'gdn_norm_w': gain((DEPTH, GDN_DV)),
        'w_o_gdn': nrm((DEPTH, GDN_V_W, D_MODEL), GDN_V_W ** -0.5),
        'q_norm_w': gain((DEPTH, Q_LORA)),
        'kv_norm_w': gain((DEPTH, KV_LORA)),
        'w_uq': nrm((DEPTH, Q_LORA, MLA_HEADS * (QK_NOPE + QK_ROPE)), Q_LORA ** -0.5),
        'w_uk': nrm((DEPTH, MLA_HEADS, KV_LORA, QK_NOPE), KV_LORA ** -0.5),
        'w_uv': nrm((DEPTH, MLA_HEADS, KV_LORA, V_HEAD), KV_LORA ** -0.5),
        'w_o_mla': nrm((DEPTH, MLA_V_W, D_MODEL), MLA_V_W ** -0.5),
        'w_out': nrm((DEPTH, D_MODEL, D_MODEL), D_MODEL ** -0.5),
        'w_router': nrm((DEPTH, D_MODEL, N_EXPERTS), D_MODEL ** -0.5),
        'b_router': nrm((DEPTH, N_EXPERTS), 0.01),
        'w_gu': nrm((DEPTH, N_EXPERTS, D_MODEL, 2 * D_EXPERT), D_MODEL ** -0.5),
        'b_gu': nrm((DEPTH, N_EXPERTS, 2 * D_EXPERT), 0.01),
        'w_dn': nrm((DEPTH, N_EXPERTS, D_EXPERT, D_MODEL), D_EXPERT ** -0.5),
        'b_dn': nrm((DEPTH, N_EXPERTS, D_MODEL), 0.01),
        'w_ada_final': nrm((D_MODEL, 2 * D_MODEL), 0.3 * D_MODEL ** -0.5),
        'b_ada_final': nrm((2 * D_MODEL,), 0.02),
        'norm_final_w': gain((D_MODEL,)),
    }

def reference(x_prompt, x_sample, c_prompt, c_sample, cache_kv, cache_pe, state_ssm, state_conv, page_table,
              norm_mix_w, norm_ffn_w, w_ada, b_ada, w_in, conv_w, A_log, dt_bias, gdn_norm_w, w_o_gdn,
              q_norm_w, kv_norm_w, w_uq, w_uk, w_uv, w_o_mla, w_out, w_router, b_router, w_gu, b_gu,
              w_dn, b_dn, w_ada_final, b_ada_final, norm_final_w):
    Bp = x_prompt.shape[0]
    pos_p = jnp.arange(x_prompt.shape[1])
    past_len = page_table.shape[1] * PAGE_SIZE
    pos_s = past_len + jnp.arange(x_sample.shape[1])
    hp, hs = x_prompt, x_sample
    kv_p, pe_p, ssm_p, conv_p = [], [], [], []
    kv_s, pe_s, ssm_s, conv_s = [], [], [], []
    for l in range(DEPTH):
        lw = {
            'norm_mix_w': norm_mix_w[l], 'norm_ffn_w': norm_ffn_w[l], 'w_ada': w_ada[l], 'b_ada': b_ada[l],
            'w_in': w_in[l], 'conv_w': conv_w[l], 'A_log': A_log[l], 'dt_bias': dt_bias[l],
            'gdn_norm_w': gdn_norm_w[l], 'w_o_gdn': w_o_gdn[l], 'q_norm_w': q_norm_w[l],
            'kv_norm_w': kv_norm_w[l], 'w_uq': w_uq[l], 'w_uk': w_uk[l], 'w_uv': w_uv[l],
            'w_o_mla': w_o_mla[l], 'w_out': w_out[l], 'w_router': w_router[l], 'b_router': b_router[l],
            'w_gu': w_gu[l], 'b_gu': b_gu[l], 'w_dn': w_dn[l], 'b_dn': b_dn[l],
        }
        zero_buf = jnp.zeros((Bp, CONV_WIDTH - 1, CONV_DIM), x_prompt.dtype)
        zero_ssm = jnp.zeros((Bp, GDN_HEADS, GDN_DK, GDN_DV), jnp.float32)
        hp, lat, kpe, S, buf = decoder_layer(hp, c_prompt, pos_p, zero_buf, zero_ssm, lw, True,
                                             mla_causal_attention)
        kv_p.append(lat); pe_p.append(kpe); ssm_p.append(S.astype(state_ssm.dtype)); conv_p.append(buf)
        attend_s = functools.partial(mla_paged_attention, cache_kv=cache_kv, cache_pe=cache_pe,
                                     page_table=page_table, layer=l)
        hs, lat, kpe, S, buf = decoder_layer(hs, c_sample, pos_s, state_conv[l], state_ssm[l], lw, False, attend_s)
        kv_s.append(lat); pe_s.append(kpe); ssm_s.append(S.astype(state_ssm.dtype)); conv_s.append(buf)
    y_prompt = final_norm(hp, c_prompt, w_ada_final, b_ada_final, norm_final_w)
    y_sample = final_norm(hs, c_sample, w_ada_final, b_ada_final, norm_final_w)
    return (y_prompt, y_sample,
            jnp.stack(kv_p), jnp.stack(pe_p), jnp.stack(ssm_p), jnp.stack(conv_p),
            jnp.stack(kv_s), jnp.stack(pe_s), jnp.stack(ssm_s), jnp.stack(conv_s))


_drawn_inputs = setup_inputs


def setup_inputs(seed=0):
    import zlib

    import numpy as np

    out = dict(_drawn_inputs(seed))
    spreads = {}
    factors = {'cache_kv': 6.881,
     'cache_pe': 8.0,
     'norm_ffn_w': 3.926,
     'gdn_norm_w': 8.0,
     'q_norm_w': 8.0,
     'kv_norm_w': 2.936,
     'b_router': 5.793,
     'b_gu': 8.0,
     'b_dn': 64.0,
     'norm_final_w': 8.623,
     'b_ada_final': 2.754}
    for name, (base, spread) in spreads.items():
        noise = np.random.default_rng([zlib.crc32(name.encode()), seed]).standard_normal(out[name].shape)
        drawn = base * np.exp(spread * noise) if base else spread * noise
        out[name] = __import__('jax').numpy.asarray(drawn.astype(out[name].dtype))
    for name, factor in factors.items():
        out[name] = (out[name] * factor).astype(out[name].dtype)
    return out
```

```python
from contextlib import ExitStack

import numpy as np
import concourse.bass as bass
from concourse import mybir

F32 = mybir.dt.float32
I32 = mybir.dt.int32
ALU = mybir.AluOpType
ACT = mybir.ActivationFunctionType
AX = mybir.AxisListType.X

P = 128
D = 1024
KD = D // P
NPR = 256
NSA = 8
T = NPR + NSA
H = 8
CONVT = 3 * H
RING = 6
CH = 4096
PAGES = 8
NPHYS = 80
LORA = 4
ROPE = 64
SCALE = (128 + 64) ** -0.5
EPS = 1e-6
NEG = -1e30
NE = 32
SLOT = 64
NJ = 48
NJ1 = NJ + 1
LEVELS = 7

C_ID, C_ONE, C_U, C_STR, C_PERM = 0, 128, 256, 384, 512
C_LEV = 640
C_COS = C_LEV + LEVELS * P
C_SIN = C_COS + T
C_NEG = C_SIN + T
C_IOTA = C_NEG + 384
C_J = C_IOTA + SLOT
C_J64 = C_J + NJ1
C_E = C_J64 + NJ1
C_B8 = C_E + 1
C_EPS = C_B8 + 64
C_TWO = C_EPS + 1
NCONST = C_TWO + P

S_NMIX, S_NFFN, S_NFIN = 0, 8, 16
S_NQ, S_NKV, S_NGDN = 24, 28, 32
S_BADA = 33
S_ALOG = S_BADA + 64
S_DT = S_ALOG + 8
S_BR = S_DT + 8
S_CW = S_BR + NE
S_WSM = S_CW + CONVT * 4
WSM = 16 + 128 + 32
S_CT = S_WSM + KD * WSM
NSMALL = S_CT + KD * 9

ADA, FIN, QKV, SSM, ZZ, CQ, CKV, UQN, UQR, UK, UV, UKT, KVS = 0, 12, 16, 22, 24, 26, 27, 28, 29, 30, 31, 32, 33
UV2 = KVS + 2 * NSA
OG, GA, OM, GB, WO = UV2 + 1, UV2 + 3, UV2 + 5, UV2 + 7, UV2 + 9
NCH = WO + 2
assert NCH % RING == 0


def build_program(nc, t):
    ctx = ExitStack()
    with ctx:
        def sb(name, shape, dt=F32):
            return ctx.enter_context(nc.sbuf_tensor(name, shape, dt))

        def sem(name):
            return ctx.enter_context(nc.semaphore(name))

        ring = [sb(f"ring{i}", [P, CH]) for i in range(RING)]
        con = sb("con_sb", [P, NCONST])
        small = sb("small_sb", [P, NSMALL])
        xT = sb("xT_sb", [P, KD, T])
        hT = sb("hT", [P, KD, T])
        mod = sb("mod", [P, 64, 9])
        regA = sb("regA", [P, CONVT * T])
        regB = sb("regB", [P, H, T])
        samp = regB[:, 0:3, :].rearrange("p a b -> p (a b)")[:, 0:CONVT * 32].rearrange("p (m j b) -> p m j b", m=CONVT, j=4)
        regC = sb("regC", [P, 10240])
        pages_sb = sb("pages_sb", [1, NSA * PAGES], I32)
        banks = ctx.enter_context(nc.psum_tensor("banks", [P, 8, 512], F32))
        bank = [banks[:, i, :] for i in range(8)]

        ident = con[:, C_ID:C_ID + P]
        ones = con[:, C_ONE:C_ONE + P]
        upto = con[:, C_U:C_U + P]
        before = con[:, C_STR:C_STR + P]
        perm = con[:, C_PERM:C_PERM + P]
        cosT = con[:, C_COS:C_COS + T]
        sinT = con[:, C_SIN:C_SIN + T]
        neg384 = con[:, C_NEG:C_NEG + 384]
        cT = small[:, S_CT:S_CT + KD * 9].rearrange("p (k c) -> p k c", k=KD)
        wsm = small[:, S_WSM:S_WSM + KD * WSM].rearrange("p (k c) -> p k c", k=KD)
        convw = small[:, S_CW:S_CW + CONVT * 4].rearrange("p (m j) -> p m j", j=4)

        qkvT = regA[:, :].rearrange("p (m t) -> p m t", t=T)
        oG = regB
        def cut(reg, at, *shape):
            n = 1
            for s in shape:
                n *= s
            v = reg[:, at:at + n]
            if len(shape) == 2:
                v = v.rearrange("p (a b) -> p a b", b=shape[1])
            if len(shape) == 3:
                v = v.rearrange("p (a b c) -> p a b c", b=shape[1], c=shape[2])
            return v
        upad = cut(regC, 0, 3, 3 + NPR)
        sigb = cut(regC, 800, 2, T)
        sqb = cut(regC, 1400, 2, T)
        rsb = cut(regC, 2900, 2, T)
        modA = cut(regC, 2300, KD, 9)
        convp = sb("convp", [P, CONVT, 3])
        smt = cut(regC, 2500, 2, CONVT, NSA)
        beta_tok = sb("beta_tok", [P, 3, H])
        g_tok = sb("g_tok", [P, 3, H])
        G4 = 4 * P
        AT = cut(regC, 0, 2, G4)
        Xm = cut(regC, 1024, 2, G4)
        XTm = cut(regC, 2048, 2, G4)
        LTm = cut(regC, 3072, 2, G4)
        Aqk = cut(regC, 4096, 2, G4)
        qg = cut(regC, 5120, 2, G4)
        VB = cut(regC, 6144, 2, G4)
        KBG = cut(regC, 7168, 2, G4)
        K2 = cut(regC, 8192, 2, G4)
        Sst = cut(regC, 9216, 2, G4)
        gcol = sb("gcol", [P, 5, H])
        gsc = sb("gsc", [P, 3, 3, H])

        latT = cut(regC, 0, LORA, T)
        cqT = cut(regC, 1056, LORA, T)
        kpeT = cut(regC, 2112, T)
        vtok = cut(regC, 2376, 2, H * P)
        oM = cut(regC, 4424, H, T)
        mlat = 6536
        msc = [cut(regC, mlat + 384 * i, 384) for i in range(2)]
        mp = [cut(regC, mlat + 768 + 384 * i, 384) for i in range(2)]
        mpT = [cut(regC, mlat + 1536 + 384 * i, 384) for i in range(2)]
        msq = cut(regC, mlat, 2, T)
        mrs = cut(regC, mlat + 600, 2, T)
        mstat = cut(regC, mlat + 2304, 2, 8)
        rtmp = cut(regC, mlat, 2, T)
        qlat = cut(regC, mlat, LORA, H, NSA)
        olat = cut(regC, mlat + 256, LORA, H, NSA)
        sTs = [cut(regC, mlat + 512 + 64 * i, 64) for i in range(2)]
        ps_ = [cut(regA, 3168 + 1032 * i, 1032) for i in range(2)]
        pT = [cut(regC, mlat + 640 + 72 * i, 72) for i in range(2)]
        qpeS = cut(regC, mlat + 800, 4, 2, NSA)
        lat_tok = cut(regC, mlat + 900, 512)
        sstat = cut(regC, mlat + 1420, 2, 8)
        qnT = cut(regA, 0, H, T)
        qpeT = cut(regA, 2112, 4, T)
        knT = cut(regA, 3168, H, NPR)
        peT = [cut(regA, 5240, 1024), cut(regC, 9000, 1024)]
        yA = cut(regA, 0, KD, T)
        yB = cut(regA, 2112, KD, T)
        gsig = cut(regC, mlat, 2, T)
        h2tok = cut(regC, 0, 3, KD, P)
        acc = regB
        yout = cut(regC, 0, KD, T)
        a0 = 0
        lg = cut(regA, 0, 3, NE)
        ex = cut(regA, 96, 3, NE)
        sel = cut(regA, 192, 3, NE)
        eqm = cut(regA, 288, 3, NE)
        pre = [cut(regA, 384 + 144 * i, 3, 48) for i in range(2)]
        v8 = cut(regA, 672, 3, 8)
        rst = cut(regA, 700, 4, 3)
        gate = cut(regA, 712, 3, NE)
        maskT = cut(regA, 808, T)
        gateT = cut(regA, 1072, T)
        m1T = cut(regA, 1336, T)
        cntc = cut(regA, 1600, 8)
        e1h = cut(regA, 1608, NJ1)
        ge1 = cut(regA, 1657, NJ1)
        rr = cut(regA, 1706, 3, NJ1)
        gg = cut(regA, 1853, 3, NJ1)
        self_ = cut(regA, 2000, 3, SLOT)
        selg = cut(regA, 2192, 3, 2, SLOT)
        selT = cut(regA, 2576, T)
        gtok = cut(regA, 2840, 512)
        hg = cut(regA, 3352, 4, P)
        gmn = cut(regA, 3864, 512)
        upc = cut(regA, 4376, 512)
        sgm = cut(regA, 4888, 512)
        act_ = cut(regA, 5400, 512)
        actT = cut(regC, 7000, 4, P)
        ytok = cut(regC, 7512, 512)
        brow = cut(regC, 8100, 3 * 512)
        items = sb("items", [1, 64], I32)
        msq2 = cut(regC, 4000, KD, T)
        mrs2 = cut(regC, 6200, T)

        vnT = cut(regC, 0, H, NSA)
        kts = cut(regC, 64, H, P)
        vnm = cut(regC, 1088, 2, NSA * P)
        bgm = cut(regC, 3136, 2, 64)
        bgb = cut(regC, 3264, 2, 64)

        zsig = cut(regC, 7300, 2, T)

        rot = cut(regC, 8000, T)
        cumc = sb("cumc", [P, 2, 16])
        modA2 = cut(regC, 6500, KD, 9)

        inputs_in = sem("inputs_in")
        slot_in = [sem(f"slot_in{i}") for i in range(RING)]
        dve_line = sem("dve_line")
        act_line = sem("act_line")
        root_ready = sem("root_ready")
        sq_ready = sem("sq_ready")
        ss_ready = sem("ss_ready")
        mod_ready = sem("mod_ready")
        mod_evac = sem("mod_evac")
        h_ready = sem("h_ready")
        proj_ready = sem("proj_ready")
        proj_evac = sem("proj_evac")
        ab_ready = sem("ab_ready")
        conv_done = sem("conv_done")
        sig_done = sem("sig_done")
        silu_done = sem("silu_done")
        l2sq = sem("l2sq")
        l2ss = sem("l2ss")
        l2done = sem("l2done")
        ab_act = sem("ab_act")
        bg_done = sem("bg_done")
        tr_ready = sem("tr_ready")
        tr_evac = sem("tr_evac")
        stored = sem("stored")

        names = {}

        def stage(name):
            if name not in names:
                names[name] = sem(name)
            return names[name]

        block = ctx.enter_context(nc.Block())

        used = {}
        for n in range(FIN + 4):
            used[n] = (mod_ready, n + 1)
        for i in range(6):
            used[QKV + i] = (proj_ready, 4 * (i + 1))
        for i in range(2):
            used[SSM + i] = (stage(f"ssm_stored{i}"), 16)
        for i in range(2):
            used[ZZ + i] = (stage("z_ready"), 4 * (i + 1))
        used[CQ] = (stage("lat_ready"), 4)
        used[CKV] = (stage("lat_ready"), 8)
        used[UQN] = (stage("q_ready"), 8)
        used[UQR] = (stage("q_ready"), 12)
        used[UK] = (stage("kn_ready"), 8)
        used[UV] = (stage("vt_ready"), 4)
        used[UKT] = (stage("qlat_ready"), 1)
        for b in range(NSA):
            used[KVS + 2 * b] = (stage("st_ready"), b + 1)
            used[KVS + 2 * b + 1] = (stage("ol_ready"), b + 1)
        used[UV2] = (stage("os_ready"), 1)
        for i in range(2):
            used[OG + i] = (stage("out_ready"), 4 * (i + 1))
            used[GA + i] = (stage("out_ready"), 8 + 4 * (i + 1))
            used[OM + i] = (stage("out_ready"), 16 + 4 * (i + 1))
            used[GB + i] = (stage("out_ready"), 24 + 4 * (i + 1))
            used[WO + i] = (stage("out_ready"), 32 + 4 * (i + 1))
        arrive = {}
        count = [0] * RING
        for n in range(NCH):
            count[n % RING] += 16 * (PAGES if KVS <= n < UV2 else 1)
            arrive[n] = count[n % RING]
        moe_base = list(count)

        def weights(pe, n):
            pe.wait_ge(slot_in[n % RING], arrive[n])
            return ring[n % RING][:, :].rearrange("p (k c) -> p k c", c=512)

        pe_mm = nc.tensor.matmul

        def chunk_k(n, m, k):
            return ring[n % RING][:, k * 512 + m * P:k * 512 + (m + 1) * P]

        moe_read = sem("moe_read")
        gu_ready = sem("gu_ready")
        sel_new = sem("sel_new")
        selg_new = sem("selg_new")
        gathered = sem("gathered")
        gtok_copied = sem("gtok_copied")
        g_turned = sem("g_turned")
        hg_ready = sem("hg_ready")
        selT_turned = sem("selT_turned")
        selT_copied = sem("selT_copied")
        gmin_ready = sem("gmin_ready")
        sig_ready = sem("sig_ready")
        act_ready = sem("act_ready")
        a_turned = sem("a_turned")
        actT_ready = sem("actT_ready")
        ytok_copied = sem("ytok_copied")
        scattered = sem("scattered")
        acc_added = sem("acc_added")
        moe_line = sem("moe_line")
        brow_in = sem("brow_in")
        wgu = t["w_gu"].rearrange("e (p k) n -> e p (k n)", p=P)
        wdn = t["w_dn"].rearrange("e (m p) n -> e p m n", p=P)
        tok_tiles = ((0, P), (1, P), (2, NSA))
        HALF = D // 2
        both = con[0:2, C_TWO:C_TWO + P]

        def number_of_items(eng):
            eng.wait_ge(stage("items_ready"), 1)
            return eng.value_load(items[0:1, 0:1], min_val=1, max_val=NJ)

        def moe_loads(sp):
            K = number_of_items(sp)

            def load(c, e):
                if c < 4:
                    src = wgu[bass.ds(e, 1), :, CH * c:CH * (c + 1)].rearrange("a p n -> p (a n)")
                    sp.dma_start(ring[c][:, :], src).then_inc(slot_in[c], 16)
                else:
                    src = wdn[bass.ds(e, 1), :, 4 * (c - 4):4 * (c - 3), :].rearrange("a p m n -> p (a m) n")
                    sp.dma_start(ring[c][:, :].rearrange("p (m n) -> p m n", m=4), src).then_inc(slot_in[c], 16)

            def load_bias(e):
                sp.dma_start(brow[0:2, :], t["biases"][bass.ds(e, 1), :, :].rearrange("a h n -> h (a n)")).then_inc(brow_in, 16)

            e0 = sp.value_load(items[0:1, 1:2], min_val=0, max_val=NE - 1)
            for c in range(RING):
                sp.wait_ge(*used[NCH - RING + c])
                load(c, e0)
            load_bias(e0)
            with sp.Fori(1, NJ) as j:
                with sp.If(j < K):
                    e = sp.value_load(items[0:1, bass.ds(j + 1, 1)], min_val=0, max_val=NE - 1)
                    for c in range(RING):
                        sp.wait_ge(moe_read, j * 6 + (c - 5))
                        load(c, e)
                    load_bias(e)

        def moe_tensor(pe):
            K = number_of_items(pe)

            def gather(n):
                pe.wait_ge(sel_new, n)
                for i, r in tok_tiles:
                    for y in range(2):
                        mm = pe_mm(bank[2][SLOT * y:SLOT * (y + 1), :], lhsT=self_[0:r, i, :],
                                   rhs=h2tok[0:r, i, 4 * y:4 * y + 4, :].rearrange("p k c -> p (k c)"),
                                   start=(i == 0), stop=(i == 2), skip_group_check=True)
                mm.then_inc(gathered, 1)

            def turn_gathered(n):
                pe.wait_ge(gtok_copied, n)
                for q in range(4):
                    mm = pe_mm(bank[3][:, P * q:P * (q + 1)], lhsT=gtok[:, P * q:P * (q + 1)], rhs=ident, start=True, stop=True)
                mm.then_inc(g_turned, 1)

            def scatter(j):
                pe.wait_ge(ytok_copied, j + 1)
                pe.wait_ge(selT_copied, j + 1)
                for q in range(4):
                    b = (6, 2)[q % 2]
                    if q >= 2:
                        pe.wait_ge(acc_added, j * 4 + q)
                    for y in range(2):
                        r = slice(SLOT * y, SLOT * (y + 1))
                        mm = pe_mm(bank[b + y][:, 0:T], lhsT=ytok[r, P * q:P * (q + 1)], rhs=selT[r, :], start=True, stop=True)
                    mm.then_inc(scattered, 1)

            pe.wait_ge(stage("rg_copied"), 1)
            gather(1)
            turn_gathered(1)
            with pe.Fori(0, NJ) as j:
                with pe.If(j < K):
                    pe.wait_ge(hg_ready, j + 1)
                    for c in range(4):
                        pe.wait_ge(slot_in[c], j * 16 + (moe_base[c] + 16))
                        for kk in range(2):
                            k = 2 * c + kk
                            for x in range(4):
                                mm = pe_mm(bank[x // 2][SLOT * (x % 2):SLOT * (x % 2 + 1), :],
                                           lhsT=hg[:, k % 4, SLOT * (k // 4):SLOT * (k // 4 + 1)],
                                           rhs=ring[c][:, 2048 * kk + HALF * x:2048 * kk + HALF * (x + 1)],
                                           start=(k == 0), stop=False, skip_group_check=True)
                        mm.then_inc(moe_read, 1)
                        if c == 0:
                            scatter(j)
                            pe.wait_ge(selg_new, j + 1)
                            for i, r in tok_tiles:
                                mm = pe_mm(bank[4][:, P * i:P * i + r], lhsT=selg[0:r, i, :, :].rearrange("p a s -> p (a s)"),
                                           rhs=ident[0:r, 0:r], start=True, stop=True)
                            mm.then_inc(selT_turned, 1)
                    pe.wait_ge(brow_in, j * 16 + 16)
                    for x in range(2):
                        mm = pe_mm(bank[x][:, :], lhsT=both, rhs=brow[0:2, HALF * x:HALF * (x + 1)], start=False, stop=True, skip_group_check=True)
                    mm.then_inc(gu_ready, 1)
                    pe.wait_ge(acc_added, j * 4 + 5)
                    gather(j + 2)
                    turn_gathered(j + 2)
                    pe.wait_ge(selT_copied, j + 2)
                    pe.wait_ge(act_ready, j + 1)
                    for q in range(4):
                        if q == 2:
                            pe.wait_ge(hg_ready, j + 2)
                        mm = pe_mm(bank[4 - q // 2][:, P * q:P * (q + 1)], lhsT=act_[:, P * q:P * (q + 1)], rhs=ident, start=True, stop=True)
                        if q % 2 == 1:
                            mm.then_inc(a_turned, 1)
                    for m in range(8):
                        c = 4 + m // 4
                        if m % 4 == 0:
                            pe.wait_ge(slot_in[c], j * 16 + (moe_base[c] + 16))
                        if m == 0:
                            pe.wait_ge(actT_ready, j * 2 + 1)
                        if m == 2:
                            pe.wait_ge(actT_ready, j * 2 + 2)
                        for y in range(2):
                            mm = pe_mm(bank[5][SLOT * y:SLOT * (y + 1), :], lhsT=actT[:, m % 4, SLOT * (m // 4):SLOT * (m // 4 + 1)],
                                       rhs=ring[c][:, D * (m % 4) + HALF * y:D * (m % 4) + HALF * (y + 1)],
                                       start=(m == 0), stop=False, skip_group_check=True)
                        if m == 3:
                            mm.then_inc(moe_read, 1)
                    pe_mm(bank[5][:, :], lhsT=both, rhs=brow[0:2, 2 * HALF:3 * HALF], start=False, stop=True, skip_group_check=True).then_inc(moe_read, 1)
            scatter(K)

        def moe_scalar(act):
            A = nc.scalar.activation
            K = number_of_items(act)
            act.wait_ge(gathered, 1)
            A(gtok[:, :], bank[2][:, :], ACT.Copy).then_inc(gtok_copied, 1)
            act.wait_ge(g_turned, 1)
            A(hg[:, :, :], bank[3][:, :].rearrange("p (q s) -> p q s", q=4), ACT.Copy).then_inc(hg_ready, 1)
            with act.Fori(0, NJ) as j:
                with act.If(j < K):
                    act.wait_ge(selT_turned, j + 1)
                    A(selT[:, :], bank[4][:, 0:T], ACT.Copy).then_inc(selT_copied, 1)
                    act.wait_ge(gmin_ready, j + 1)
                    A(sgm[:, :], gmn[:, :], ACT.Sigmoid, scale=1.702).then_inc(sig_ready, 1)
                    act.wait_ge(gathered, j + 2)
                    A(gtok[:, :], bank[2][:, :], ACT.Copy).then_inc(gtok_copied, 1)
                    act.wait_ge(g_turned, j + 2)
                    A(hg[:, :, :], bank[3][:, :].rearrange("p (q s) -> p q s", q=4), ACT.Copy).then_inc(hg_ready, 1)
                    for y in range(2):
                        act.wait_ge(a_turned, j * 2 + (y + 1))
                        A(actT[:, 2 * y:2 * y + 2, :], bank[4 - y][:, 256 * y:256 * (y + 1)].rearrange("p (q s) -> p q s", q=2),
                          ACT.Copy).then_inc(actT_ready, 1)
                    act.wait_ge(moe_read, j * 6 + 6)
                    A(ytok[:, :], bank[5][:, :], ACT.Copy).then_inc(ytok_copied, 1)

        LINKS = 2

        def moe_vector(dve, link):
            V = nc.vector
            K = number_of_items(dve)
            iota = con[:, C_IOTA:C_IOTA + SLOT]
            dve.wait_ge(acc_added, 1)
            V.memset(selT[:, :], 0.0).then_inc(selT_copied, 1)
            V.memset(ytok[:, :], 0.0).then_inc(ytok_copied, 1)

            def choose(col):
                for i, r in tok_tiles:
                    ins = V.tensor_scalar(self_[0:r, i, :], iota[0:r, :], rr[0:r, i, col], None, ALU.is_equal)
                return ins

            def add(j):
                for q in range(4):
                    b = (6, 2)[q % 2]
                    dve.wait_ge(scattered, j * 4 + (q + 1))
                    pair = acc[:, q::4, :]
                    V.tensor_tensor(pair, pair, banks[:, b:b + 2, 0:T], ALU.add).then_inc(acc_added, 1)

            choose(slice(0, 1)).then_inc(sel_new, 1)
            with dve.Fori(0, NJ) as j:
                with dve.If(j < K):
                    n = [0]

                    def after(ins):
                        n[0] += 1
                        ins.then_inc(moe_line, 1)
                        dve.wait_ge(moe_line, j * LINKS + n[0])

                    dve.wait_ge(gathered, j + 1)
                    choose(bass.ds(j + 1, 1)).then_inc(sel_new, 1)
                    for i, r in tok_tiles:
                        ins = V.tensor_scalar(selg[0:r, i, :, :], iota[0:r, :].unsqueeze(1).to_broadcast([r, 2, SLOT]),
                                              rr[0:r, i, bass.ds(j, 1)], gg[0:r, i, bass.ds(j, 1)], ALU.is_equal, ALU.mult)
                    ins.then_inc(selg_new, 1)
                    add(j)
                    dve.wait_ge(gu_ready, j + 1)
                    V.tensor_scalar(gmn[:, :], bank[0][:, :], 7.0, None, ALU.min).then_inc(gmin_ready, 1)
                    after(V.tensor_scalar(upc[:, :], bank[1][:, :], 7.0, -7.0, ALU.min, ALU.max))
                    after(V.scalar_tensor_tensor(upc[:, :], upc[:, :], 1.0, gmn[:, :], ALU.add, ALU.mult))
                    dve.wait_ge(sig_ready, j + 1)
                    V.tensor_tensor(act_[:, :], upc[:, :], sgm[:, :], ALU.mult).then_inc(act_ready, 1)
                    assert n[0] == LINKS
            add(K)
            dve.wait_ge(acc_added, K * 4 + 5)

        ssm_view = [ring[(SSM + i) % RING][:, :].rearrange("p (h b v) -> p h b v", h=4, b=NSA) for i in range(2)]

        @block.sync
        def _(sp):
            sp.dma_start(small[:, :], t["small"]).then_inc(inputs_in, 16)
            sp.dma_start(xT[:, :, :], t["xT"]).then_inc(inputs_in, 16)
            sp.dma_start(con[:, :], t["con"]).then_inc(inputs_in, 16)
            sp.dma_start(samp[:, :, :, :], t["convT"]).then_inc(inputs_in, 16)
            sp.dma_start(pages_sb[:, :], t["pages"]).then_inc(stage("pages_in"), 16)
            for n in range(NCH):
                if n >= RING:
                    sp.wait_ge(*used[n - RING])
                dst = ring[n % RING]
                if KVS <= n < UV2:
                    b, what = (n - KVS) // 2, (n - KVS) % 2
                    if n == KVS:
                        sp.wait_ge(stage("pages_in"), 16)
                    src = t["kvT"] if what == 0 else t["kv"]
                    if what == 0:
                        if b >= 2:
                            sp.wait_ge(stage("st_ready"), b - 1)
                        else:
                            sp.wait_ge(stage("oss_ready"), 1)
                            sp.wait_ge(stage("ssmp_stored"), 16)
                    with sp.Fori(0, PAGES) as pg:
                        phys = sp.value_load(pages_sb[0:1, bass.ds(pg + b * PAGES, 1)], min_val=0, max_val=NPHYS - 1)
                        sp.dma_start(dst[:, bass.ds(pg * 512, 512)],
                                     src[bass.ds(phys, 1), :, :].rearrange("a p c -> p (a c)")
                                     ).then_inc(slot_in[n % RING], 16)
                        if what == 0:
                            sp.dma_start(peT[b % 2][0:ROPE, bass.ds(pg * P, P)],
                                         t["peT"][bass.ds(phys, 1), :, :].rearrange("a p c -> p (a c)")
                                         ).then_inc(stage(f"pe_in{b % 2}"), 16)
                elif n == UQR:
                    sp.dma_start(dst[:, 0:2048], t["wpre"][wp_index(n), :, 0:2048]).then_inc(slot_in[n % RING], 16)
                elif SSM <= n < SSM + 2:
                    sp.dma_start(dst[:, :], t["ssm"][n - SSM, :, :]).then_inc(slot_in[n % RING], 16)
                else:
                    sp.dma_start(dst[:, :], t["wpre"][wp_index(n), :, :]).then_inc(slot_in[n % RING], 16)
            moe_loads(sp)

        @block.tensor
        def _(pe):
            def sum_squares(out, sq, k):
                for i in range(k):
                    mm = pe_mm(out, lhsT=ones, rhs=sq(i), start=(i == 0), stop=(i == k - 1))
                return mm

            pe.wait_ge(inputs_in, 64)
            pe.wait_ge(sq_ready, 1)
            sum_squares(bank[2][:, 0:T], lambda k: hT[:, k, :], KD).then_inc(ss_ready, 1)
            for n in range(FIN + 4):
                weights(pe, n)
                if n >= 2:
                    pe.wait_ge(mod_evac, n - 1)
                for m in range(4):
                    for k in range(KD):
                        mm = pe_mm(bank[n % 2][:, 9 * m:9 * m + 9], lhsT=chunk_k(n, m, k), rhs=cT[:, k, :],
                                   start=(k == 0), stop=(k == KD - 1))
                mm.then_inc(mod_ready, 1)
            pe.wait_ge(h_ready, 1)
            for i, (a, b) in enumerate(((0, P), (P, NPR), (NPR, T))):
                for k in range(KD):
                    mm = pe_mm(bank[6][0:b - a, 16 * i:16 * i + 16], lhsT=hT[:, k, a:b], rhs=wsm[:, k, 0:16],
                               start=(k == 0), stop=(k == KD - 1))
            mm.then_inc(ab_ready, 1)
            for m in range(CONVT):
                n = QKV + m // 4
                weights(pe, n)
                if m >= 4:
                    pe.wait_ge(proj_evac, m - 3)
                for k in range(KD):
                    mm = pe_mm(bank[m % 4][:, 0:T], lhsT=chunk_k(n, m % 4, k), rhs=hT[:, k, :],
                               start=(k == 0), stop=(k == KD - 1))
                mm.then_inc(proj_ready, 1)
            for i in range(2 * H):
                pe.wait_ge(l2sq, i + 1)
                if i >= 2:
                    pe.wait_ge(l2done, i - 1)
                pe_mm(bank[4 + i % 2][:, 0:T], lhsT=ones, rhs=sqb[:, i % 2, :], start=True, stop=True).then_inc(l2ss, 1)
            pe.wait_ge(bg_done, 1)
            for c in range(2):
                pe_mm(bank[6][:, 64 + 16 * c:72 + 16 * c], lhsT=upto, rhs=g_tok[:, c, :], start=True, stop=True)
                mm = pe_mm(bank[6][:, 72 + 16 * c:80 + 16 * c], lhsT=ones, rhs=g_tok[:, c, :], start=True, stop=True)
            mm.then_inc(stage("cum_ready"), 1)
            pe.wait_ge(l2done, 2 * H)
            for c in range(2):
                tok = slice(c * P, (c + 1) * P)
                for g in range(2):
                    for w in range(2):
                        bk = bank[2 * w + g]
                        if g == 0 and w == 0 and c == 1:
                            pe.wait_ge(stage("gd_out"), 2)
                        for i in range(4):
                            mm = pe_mm(bk[:, i * P:(i + 1) * P],
                                       lhsT=qkvT[:, H * (1 + w) + 4 * g + i, tok], rhs=ident,
                                       start=True, stop=True)
                        mm.then_inc(tr_ready, 1)
                for g in range(2):
                    b0 = 4 - 4 * g
                    if g == 1:
                        pe.wait_ge(tr_evac, 4 * (c + 1))
                    for i in range(4):
                        h = 4 * g + i
                        pe_mm(bank[b0][:, i * P:(i + 1) * P], lhsT=g_tok[:, c, h:h + 1].to_broadcast([P, P]), rhs=upto, start=True, stop=True)
                    for i in range(4):
                        h = 4 * g + i
                        pe_mm(bank[b0 + 1][:, i * P:(i + 1) * P], lhsT=beta_tok[:, c, h:h + 1].to_broadcast([P, P]), rhs=ident, start=True, stop=True)
                    if g == 0 and c == 0:
                        pe.wait_ge(stage("cum_read"), 1)
                    for i in range(4):
                        h = 4 * g + i
                        pe_mm(bank[b0 + 2][:, i * P:(i + 1) * P], lhsT=qkvT[:, H + h, tok], rhs=qkvT[:, H + h, tok], start=True, stop=True)
                    for i in range(4):
                        h = 4 * g + i
                        mm = pe_mm(bank[b0 + 3][:, i * P:(i + 1) * P], lhsT=qkvT[:, H + h, tok], rhs=qkvT[:, h, tok], start=True, stop=True)
                    mm.then_inc(stage("gd_prod"), 1)
                for lv in range(LEVELS):
                    for g in range(2):
                        q = (c * LEVELS + lv) * 2 + g + 1
                        pe.wait_ge(stage("lt_done"), q)
                        if lv == 0:
                            pe.wait_ge(stage("prep_done"), 2 * c + 2)
                        for i in range(4):
                            s = slice(i * P, (i + 1) * P)
                            mm = pe_mm(bank[g][:, s], lhsT=LTm[:, g, s], rhs=Xm[:, g, s], start=True, stop=True)
                        mm.then_inc(stage("lx_done"), 1)
                    for g in range(2):
                        q = (c * LEVELS + lv) * 2 + g + 1
                        pe.wait_ge(stage("lx_copied"), q)
                        for i in range(4):
                            s = slice(i * P, (i + 1) * P)
                            pe_mm(bank[2 + g][:, s], lhsT=XTm[:, g, s], rhs=LTm[:, g, s], start=True, stop=True)
                        for i in range(4):
                            s = slice(i * P, (i + 1) * P)
                            mm = pe_mm(bank[4 + g][:, s], lhsT=LTm[:, g, s], rhs=XTm[:, g, s], start=True, stop=True)
                        mm.then_inc(stage("xlx_done"), 1)
                for g in range(2):
                    pe.wait_ge(stage("x_done"), (c + 1) * 2 * LEVELS if g == 1 else (c + 1) * 2 * LEVELS - 1)
                    for i in range(4):
                        s = slice(i * P, (i + 1) * P)
                        mm = pe_mm(bank[g][:, s], lhsT=XTm[:, g, s], rhs=VB[:, g, s], start=True, stop=True)
                    if c == 1:
                        for i in range(4):
                            s = slice(i * P, (i + 1) * P)
                            mm = pe_mm(bank[2 + g][:, s], lhsT=KBG[:, g, s], rhs=XTm[:, g, s], start=True, stop=True)
                    mm.then_inc(stage("uw_done"), 1)
                if c == 1:
                    for g in range(2):
                        pe.wait_ge(stage("wt_copied"), g + 1)
                        for i in range(4):
                            s = slice(i * P, (i + 1) * P)
                            mm = pe_mm(bank[4 + g][:, s], lhsT=Xm[:, g, s], rhs=Sst[:, g, s], start=True, stop=True)
                        mm.then_inc(stage("ws_done"), 1)
                for g in range(2):
                    pe.wait_ge(stage("vn_done"), 2 * c + g + 1)
                    for i in range(4):
                        s = slice(i * P, (i + 1) * P)
                        mm = pe_mm(bank[6 + g][:, s], lhsT=VB[:, g, s], rhs=Aqk[:, g, s], start=True, stop=(c == 0))
                        if c == 1:
                            mm = pe_mm(bank[6 + g][:, s], lhsT=Sst[:, g, s], rhs=qg[:, g, s], start=False, stop=True)
                    for i in range(4):
                        s = slice(i * P, (i + 1) * P)
                        mm = pe_mm(bank[2 + g][:, s], lhsT=K2[:, g, s], rhs=VB[:, g, s], start=True, stop=True)
                    mm.then_inc(stage("os_done"), 1)
            pe.wait_ge(stage("gd_out"), 4)
            for h in range(H):
                mm = pe_mm(bank[h // 4][0:NSA, (h % 4) * P:(h % 4 + 1) * P], lhsT=qkvT[:, H + h, NPR:T], rhs=ident, start=True, stop=True)
            mm.then_inc(stage("sample_products"), 1)
            pe.wait_ge(stage("bgm_ready"), 1)
            pe_mm(bank[2][:, 0:64], lhsT=ones[0:NSA, :], rhs=bgm[0:NSA, 0, :], start=True, stop=True)
            pe_mm(bank[2][:, 64:128], lhsT=ones[0:NSA, :], rhs=bgm[0:NSA, 1, :], start=True, stop=True).then_inc(stage("sample_products"), 1)
            for h in range(H):
                if h % 4 == 0:
                    pe.wait_ge(slot_in[(SSM + h // 4) % RING], arrive[SSM + h // 4])
                for b in range(NSA):
                    mm = pe_mm(bank[3][:, h * NSA + b:h * NSA + b + 1], lhsT=ssm_view[h // 4][:, h % 4, b, :],
                               rhs=qkvT[:, H + h, NPR + b:NPR + b + 1], start=True, stop=True)
            mm.then_inc(stage("sample_products"), 1)
            pe.wait_ge(stage("vns_ready"), 1)
            pe.wait_ge(stage("kts_copied"), 1)
            for h in range(H):
                mm = pe_mm(bank[h // 4][0:NSA, (h % 4) * P:(h % 4 + 1) * P], lhsT=vnT[:, h, :], rhs=ident, start=True, stop=True)
            mm.then_inc(stage("sample_products"), 1)
            for h in range(H):
                pe.wait_ge(stage("vnm_ready"), h + 1)
                if h >= 2:
                    pe.wait_ge(stage("snew"), h - 1)
                for y in range(2):
                    mm = pe_mm(bank[4 + 2 * (h % 2) + y][:, :], lhsT=kts[0:NSA, h, :],
                               rhs=vnm[0:NSA, h % 2, 512 * y:512 * y + 512], start=True, stop=True)
                mm.then_inc(stage("outer"), 1)
            for h in range(H):
                pe.wait_ge(stage("snew"), h + 1)
                for b in range(NSA):
                    mm = pe_mm(bank[3][:, 64 + h * NSA + b:65 + h * NSA + b], lhsT=ssm_view[h // 4][:, h % 4, b, :],
                               rhs=qkvT[:, h, NPR + b:NPR + b + 1], start=True, stop=True)
            mm.then_inc(stage("oss_ready"), 1)
            for h in range(H):
                pe.wait_ge(stage("on_sq"), h + 1)
                if h >= 2:
                    pe.wait_ge(stage("on_rs"), h - 1)
                pe_mm(bank[h % 2][:, 0:T], lhsT=ones, rhs=msq[:, h % 2, :], start=True, stop=True).then_inc(stage("on_ss"), 1)
            pe.wait_ge(stage("on_rs"), H)
            for m in range(H):
                n = ZZ + m // 4
                weights(pe, n)
                if m >= 4:
                    pe.wait_ge(stage("z_evac"), m - 3)
                for k in range(KD):
                    mm = pe_mm(bank[m % 4][:, 0:T], lhsT=chunk_k(n, m % 4, k), rhs=hT[:, k, :], start=(k == 0), stop=(k == KD - 1))
                mm.then_inc(stage("z_ready"), 1)
            for m in range(8):
                n = CQ + m // 4
                weights(pe, n)
                if m >= 4:
                    pe.wait_ge(stage("lat_evac"), m - 3)
                for k in range(KD):
                    mm = pe_mm(bank[4 + m % 4][:, 0:T], lhsT=chunk_k(n, m % 4, k), rhs=hT[:, k, :], start=(k == 0), stop=(k == KD - 1))
                mm.then_inc(stage("lat_ready"), 1)
            pe.wait_ge(stage("z_evac"), H)
            for k in range(KD):
                mm = pe_mm(bank[0][:, 0:T], lhsT=wsm[:, k, 16:144], rhs=hT[:, k, :], start=(k == 0), stop=(k == KD - 1))
            mm.then_inc(stage("kpe_ready"), 1)
            pe.wait_ge(stage("kpe_copied"), 1)
            pe_mm(bank[1][:, 0:T], lhsT=perm, rhs=kpeT[:, :], start=True, stop=True).then_inc(stage("kpe_turned"), 1)
            for w in range(2):
                for i in range(LORA):
                    pe.wait_ge(stage("lsq"), LORA * w + i + 1)
                    mm = pe_mm(bank[2 + w][:, 0:T], lhsT=ones, rhs=msq[:, i % 2, :], start=(i == 0), stop=(i == LORA - 1))
                    mm.then_inc(stage("lss"), 1)
            pe.wait_ge(stage("lat_normed"), 1)
            pe.wait_ge(stage("lat_evac"), 8)
            for m in range(12):
                n = UQN if m < 8 else UQR
                pe.wait_ge(slot_in[n % RING], arrive[n])
                if m >= 4:
                    pe.wait_ge(stage("q_evac"), m - 3)
                W = 1024 if m < 8 else 512
                c0 = (m if m < 8 else m - 8) * P
                for k in range(LORA):
                    mm = pe_mm(bank[4 + m % 4][:, 0:T], lhsT=ring[n % RING][:, k * W + c0:k * W + c0 + P], rhs=cqT[:, k, :],
                               start=(k == 0), stop=(k == LORA - 1))
                mm.then_inc(stage("q_ready"), 1)
            for i in range(4):
                pe.wait_ge(stage("q_evac"), 9 + i)
                if i >= 2:
                    pe.wait_ge(stage("q_turned"), i - 1)
                pe_mm(bank[i % 2][:, 0:T], lhsT=perm, rhs=qpeT[:, i, :], start=True, stop=True).then_inc(stage("q_turn"), 1)
            pe.wait_ge(stage("lat_normed"), 2)
            pe.wait_ge(slot_in[UK % RING], arrive[UK])
            wk = ring[UK % RING][:, :].rearrange("p (c h n) -> p c h n", c=LORA, h=H)
            for h in range(H):
                pe.wait_ge(stage("kn_evac"), h - 3) if h >= 4 else pe.wait_ge(stage("q_evac"), 12)
                for k in range(LORA):
                    mm = pe_mm(bank[4 + h % 4][:, 0:NPR], lhsT=wk[:, k, h, :], rhs=latT[:, k, 0:NPR], start=(k == 0), stop=(k == LORA - 1))
                mm.then_inc(stage("kn_ready"), 1)
            pe.wait_ge(slot_in[UV % RING], arrive[UV])
            wv = ring[UV % RING][:, :].rearrange("p (c n) -> p c n", c=LORA)
            pe.wait_ge(stage("q_turned"), 4)
            for i in range(4):
                c, y = i // 2, i % 2
                for k in range(LORA):
                    mm = pe_mm(bank[i][:, :], lhsT=latT[:, k, c * P:(c + 1) * P], rhs=wv[:, k, 512 * y:512 * y + 512], start=(k == 0), stop=(k == LORA - 1))
                mm.then_inc(stage("vt_ready"), 1)
            pe.wait_ge(stage("kn_evac"), 8)
            pe.wait_ge(stage("vt_evac"), 4)
            for h in range(H + 1):
                if h < H:
                    s = bank[h % 2]
                    half = slice(64 * (h % 2), 64 * (h % 2) + 64)
                    if h >= 2:
                        pe.wait_ge(stage("pa_masked"), h - 1)
                    pe_mm(s[:, 0:P], lhsT=qnT[:, h, 0:P], rhs=knT[:, h, 0:P], start=True, stop=False)
                    pe_mm(s[:, 0:P], lhsT=qpeT[half, h // 2, 0:P], rhs=kpeT[half, 0:P], start=False, stop=True)
                    pe_mm(s[:, P:384], lhsT=qnT[:, h, P:NPR], rhs=knT[:, h, :], start=True, stop=False)
                    pe_mm(s[:, P:384], lhsT=qpeT[half, h // 2, P:NPR], rhs=kpeT[half, 0:NPR], start=False, stop=True).then_inc(stage("pa_scores"), 1)
                if h >= 1:
                    j = h - 1
                    pe.wait_ge(stage("pa_probs"), j + 1)
                    if j >= 2:
                        pe.wait_ge(stage("pa_pcopied"), j - 1)
                    w = bank[2 + j % 2]
                    pe.transpose(w[:, 0:P], mp[j % 2][:, 0:P], ident)
                    pe.transpose(w[:, P:256], mp[j % 2][:, P:256], ident)
                    pe.transpose(w[:, 256:384], mp[j % 2][:, 256:384], ident).then_inc(stage("pa_turned"), 1)
                    pe.wait_ge(stage("pa_pcopied"), j + 1)
                    if j >= 2:
                        pe.wait_ge(stage("pa_out"), j - 1)
                    o = bank[4 + j % 2]
                    pe_mm(o[:, 0:NPR], lhsT=vtok[:, 0, j * P:(j + 1) * P], rhs=mpT[j % 2][:, 0:NPR], start=True, stop=False)
                    pe_mm(o[:, P:NPR], lhsT=vtok[:, 1, j * P:(j + 1) * P], rhs=mpT[j % 2][:, NPR:384], start=False, stop=True).then_inc(stage("pa_ready"), 1)
            pe.wait_ge(slot_in[UKT % RING], arrive[UKT])
            wkt = ring[UKT % RING][:, :].rearrange("p (h c) -> p h c", h=H)
            for h in range(H):
                for k in range(LORA):
                    pe_mm(bank[6][:, k * 64 + h * NSA:k * 64 + h * NSA + NSA], lhsT=wkt[:, h, k * P:(k + 1) * P], rhs=qnT[:, h, NPR:T], start=True, stop=True)
            pe_mm(bank[7][0:ROPE, 0:32], lhsT=ident[:, 0:ROPE], rhs=qpeT[:, :, NPR:T], start=True, stop=True)
            mm = pe_mm(bank[7][0:ROPE, 32:64], lhsT=ident[:, ROPE:P], rhs=qpeT[:, :, NPR:T], start=True, stop=True)
            mm.then_inc(stage("qlat_ready"), 1)
            pe.wait_ge(stage("pa_out"), 8)
            pe.wait_ge(stage("pa_pcopied"), 8)
            for k in range(LORA):
                mm = pe_mm(bank[5][0:NSA, k * P:(k + 1) * P], lhsT=latT[:, k, NPR:T], rhs=ident, start=True, stop=True)
            mm.then_inc(stage("ltok_ready"), 1)
            pe.wait_ge(stage("qlat_copied"), 1)

            def sample_scores(b):
                n = KVS + 2 * b
                pe.wait_ge(slot_in[n % RING], arrive[n])
                pe.wait_ge(stage(f"pe_in{b % 2}"), 16 * PAGES * (b // 2 + 1))
                if b >= 1:
                    pe.wait_ge(stage("st_copied"), b)
                kt = ring[n % RING][:, :].rearrange("p (g c s) -> p g c s", g=PAGES, c=LORA)
                for g in range(PAGES):
                    o = bank[6][:, 8 * g:8 * g + 8].rearrange("p (a i) -> p a i", i=2)
                    for k in range(LORA):
                        pe_mm(bank[6][:, 8 * g:8 * g + 8], lhsT=kt[:, g, k, :], rhs=qlat[:, k, :, b], start=(k == 0), stop=False)
                    mm = pe_mm(o, lhsT=peT[b % 2][0:ROPE, g * P:(g + 1) * P], rhs=qpeS[0:ROPE, :, :, b], start=False, stop=True)
                mm.then_inc(stage("st_ready"), 1)
                if b >= 1:
                    pe.wait_ge(stage("s_read"), b)
                for k in range(LORA):
                    pe_mm(bank[4][0:NSA, 0:NSA], lhsT=qlat[:, k, :, b], rhs=latT[:, k, NPR:T], start=(k == 0), stop=False)
                pe_mm(bank[4][0:NSA, 0:NSA], lhsT=qpeS[0:ROPE, :, :, b], rhs=kpeT[0:ROPE, NPR:T], start=False, stop=True)
                pe.wait_ge(stage("st_copied"), b + 1)
                for g in range(PAGES):
                    mm = pe_mm(bank[g // 4][0:NSA, (g % 4) * P:(g % 4 + 1) * P], lhsT=sTs[b % 2][:, 8 * g:8 * g + 8], rhs=ident, start=True, stop=True)
                mm.then_inc(stage("s_turned"), 1)

            def sample_values(b):
                pe.wait_ge(stage("p_ready"), b + 1)
                if b >= 1:
                    pe.wait_ge(stage("pT_copied"), b)
                for g in range(PAGES):
                    pe_mm(bank[2][:, 8 * g:8 * g + 8], lhsT=ps_[b % 2][0:NSA, g * P:(g + 1) * P], rhs=ident[0:NSA, 0:NSA], start=True, stop=True)
                mm = pe_mm(bank[2][0:NSA, 64:72], lhsT=ps_[b % 2][0:NSA, 1024:1032], rhs=ident[0:NSA, 0:NSA], start=True, stop=True)
                mm.then_inc(stage("p_turned"), 1)
                pe.wait_ge(stage("pT_copied"), b + 1)
                n = KVS + 2 * b + 1
                pe.wait_ge(slot_in[n % RING], arrive[n])
                if b >= 1:
                    pe.wait_ge(stage("ol_copied"), b)
                kv = ring[n % RING][:, :].rearrange("p (g c) -> p g c", g=PAGES)
                for k in range(LORA):
                    for g in range(PAGES):
                        pe_mm(bank[3][:, 8 * k:8 * k + 8], lhsT=kv[:, g, k * P:(k + 1) * P], rhs=pT[b % 2][:, 8 * g:8 * g + 8], start=(g == 0), stop=False)
                    mm = pe_mm(bank[3][:, 8 * k:8 * k + 8], lhsT=lat_tok[0:NSA, k * P:(k + 1) * P], rhs=pT[b % 2][0:NSA, 64:72], start=False, stop=True)
                mm.then_inc(stage("ol_ready"), 1)

            for b in range(NSA + 1):
                if b < NSA:
                    sample_scores(b)
                if b >= 1:
                    sample_values(b - 1)
            pe.wait_ge(slot_in[UV2 % RING], arrive[UV2])
            pe.wait_ge(stage("ol_copied"), NSA)
            wv2 = ring[UV2 % RING][:, :].rearrange("p (c n) -> p c n", c=LORA)
            for h in range(H):
                for k in range(LORA):
                    mm = pe_mm(bank[7][:, 64 + 8 * h:72 + 8 * h], lhsT=wv2[:, k, h * P:(h + 1) * P], rhs=olat[:, k, h, :], start=(k == 0), stop=(k == LORA - 1))
            mm.then_inc(stage("os_ready"), 1)
            for m in range(40):
                n = OG + m // 4
                rhs = (oG, hT, oM, hT, yA)[m // 8]
                weights(pe, n)
                if m == 0:
                    pe.wait_ge(stage("z_gated"), H)
                if m == 16:
                    pe.wait_ge(stage("os_copied"), 1)
                if m == 32:
                    pe.wait_ge(stage("merged"), KD)
                if m >= 4:
                    kind, r = (m - 4) // 8, (m - 4) % 8 + 1
                    if kind in (0, 2):
                        pe.wait_ge(stage("out_evac"), 8 * (kind // 2) + r)
                    elif kind in (1, 3):
                        pe.wait_ge(stage("gate_sig"), 8 * (kind // 2) + r)
                    else:
                        pe.wait_ge(stage("out_evac"), 16 + r)
                for k in range(KD):
                    mm = pe_mm(bank[m % 4][:, 0:T], lhsT=chunk_k(n, m % 4, k), rhs=rhs[:, k, :], start=(k == 0), stop=(k == KD - 1))
                mm.then_inc(stage("out_ready"), 1)
            pe.wait_ge(sq_ready, 2)
            sum_squares(bank[4][:, 0:T], lambda k: msq2[:, k, :], KD).then_inc(ss_ready, 1)
            pe.wait_ge(h_ready, 2)
            tiles = ((0, P), (P, NPR), (NPR, T))
            for i, (a, b) in enumerate(tiles):
                for k in range(KD):
                    mm = pe_mm(bank[5][0:b - a, NE * i:NE * i + NE], lhsT=hT[:, k, a:b], rhs=wsm[:, k, 144:176], start=(k == 0), stop=(k == KD - 1))
            mm.then_inc(stage("logits"), 1)
            for i, (a, b) in enumerate(tiles):
                for y in range(2):
                    q = 2 * i + y
                    if q >= 4:
                        pe.wait_ge(stage("h2_copied"), q - 3)
                    for k in range(4):
                        mm = pe.transpose(bank[q % 4][0:b - a, k * P:(k + 1) * P], hT[:, 4 * y + k, a:b], ident)
                    mm.then_inc(stage("h2_turned"), 1)
            pe.wait_ge(stage("sel_ready"), 1)
            pe_mm(bank[6][0:NE, 0:P], lhsT=sel[:, 0, :], rhs=before, start=True, stop=True)
            pe_mm(bank[6][0:NE, P:NPR], lhsT=sel[:, 0, :], rhs=ones, start=True, stop=False)
            pe_mm(bank[6][0:NE, P:NPR], lhsT=sel[:, 1, :], rhs=before, start=False, stop=True)
            pe_mm(bank[6][0:NE, NPR:T], lhsT=sel[:, 0, :], rhs=ones[:, 0:NSA], start=True, stop=False)
            pe_mm(bank[6][0:NE, NPR:T], lhsT=sel[:, 1, :], rhs=ones[:, 0:NSA], start=False, stop=False)
            pe_mm(bank[6][0:NE, NPR:T], lhsT=sel[0:NSA, 2, :], rhs=before[0:NSA, 0:NSA], start=False, stop=True)
            pe_mm(bank[7][0:NE, 0:1], lhsT=sel[:, 0, :], rhs=ones[:, 0:1], start=True, stop=False)
            pe_mm(bank[7][0:NE, 0:1], lhsT=sel[:, 1, :], rhs=ones[:, 0:1], start=False, stop=False)
            pe_mm(bank[7][0:NE, 0:1], lhsT=sel[0:NSA, 2, :], rhs=ones[0:NSA, 0:1], start=False, stop=True)
            pe.wait_ge(stage("sel_ready"), 2)
            for i, (a, b) in enumerate(tiles):
                pe.transpose(bank[4][0:NE, a:b], sel[0:b - a, i, :], ident[0:b - a, 0:b - a])
            pe.wait_ge(stage("h2_copied"), 6)
            for i, (a, b) in enumerate(tiles):
                mm = pe.transpose(bank[0][0:NE, a:b], gate[0:b - a, i, :], ident[0:b - a, 0:b - a])
            mm.then_inc(stage("route"), 1)
            pe.wait_ge(stage("blocks"), 1)
            pe_mm(bank[7][0:NE, 1:2], lhsT=before[0:NE, 0:NE], rhs=cntc[0:NE, 0:1], start=True, stop=True)
            pe_mm(bank[7][0:1, 2:3], lhsT=cntc[0:NE, 0:1], rhs=ones[0:NE, 0:1], start=True, stop=True).then_inc(stage("route"), 1)
            pe.wait_ge(stage("e1h_ready"), 1)
            pe_mm(bank[7][0:1, 8:8 + NJ1], lhsT=con[0:NE, C_E:C_E + 1], rhs=e1h[0:NE, :], start=True, stop=True).then_inc(stage("route"), 1)
            pe.wait_ge(stage("m1_ready"), 1)
            for i, (a, b) in enumerate(tiles):
                pe_mm(bank[1][0:b - a, NJ1 * i:NJ1 * (i + 1)], lhsT=m1T[0:NE, a:b], rhs=e1h[0:NE, :], start=True, stop=True)
            for i, (a, b) in enumerate(tiles):
                mm = pe_mm(bank[2][0:b - a, NJ1 * i:NJ1 * (i + 1)], lhsT=gateT[0:NE, a:b], rhs=e1h[0:NE, :], start=True, stop=True)
            mm.then_inc(stage("route"), 1)
            moe_tensor(pe)
            pe.wait_ge(sq_ready, 3)
            sum_squares(bank[0][:, 0:T], lambda k: msq2[:, k, :], KD).then_inc(ss_ready, 1)

        @block.scalar
        def _(act):
            line = [0]

            def link(ins):
                line[0] += 1
                ins.then_inc(act_line, 1)
                act.wait_ge(act_line, line[0])

            A = nc.scalar.activation
            act.wait_ge(inputs_in, 64)
            A(hT[:, :, :], xT[:, :, :], ACT.Square).then_inc(sq_ready, 1)

            def root(out, sums, scale):
                return A(out, sums, ACT.Sqrt, scale=scale, bias=con[:, C_EPS:C_EPS + 1])
            act.wait_ge(ss_ready, 1)
            act.wait_ge(stage("upad_zero"), 1)
            root(rsb[:, 0, :], bank[2][:, 0:T], 1.0 / D).then_inc(root_ready, 1)
            for m in range(CONVT + 1):
                if m < CONVT:
                    act.wait_ge(proj_ready, m + 1)
                    if m >= 3:
                        act.wait_ge(conv_done, m - 2)
                    elif m == 0:
                        act.wait_ge(stage("upad_zero"), 1)
                    b = bank[m % 4]
                    A(samp[:, m, 3, :], b[:, NPR:T], ACT.Copy)
                    A(convp[:, m, :], b[:, NPR - 3:NPR], ACT.Copy)
                    A(upad[:, m % 3, 3:3 + NPR], b[:, 0:NPR], ACT.Copy).then_inc(proj_evac, 1)
                if m >= 1:
                    act.wait_ge(conv_done, m)
                    if m >= 3:
                        act.wait_ge(silu_done, m - 2)
                    A(sigb[:, (m - 1) % 2, 0:NPR], qkvT[:, m - 1, 0:NPR], ACT.Sigmoid).then_inc(sig_done, 1)
            act.wait_ge(stage("conv_s"), 1)
            A(smt[:, 1, :, :], smt[:, 0, :, :], ACT.Sigmoid).then_inc(sig_done, 1)
            act.wait_ge(ab_ready, 1)
            act.wait_ge(stage("ab_copied"), 1)
            A(beta_tok[:, :, :], gsc[:, 0, :, :], ACT.Sigmoid).then_inc(ab_act, 1)
            link(A(gsc[:, 2, :, :], gsc[:, 1, :, :], ACT.Abs))
            link(A(gsc[:, 2, :, :], gsc[:, 2, :, :], ACT.Exp, scale=-1.0))
            link(A(gcol[:, 0, :], small[:, S_ALOG:S_ALOG + 8], ACT.Exp))
            A(gsc[:, 2, :, :], gsc[:, 2, :, :], ACT.Ln, bias=1.0).then_inc(ab_act, 1)
            act.wait_ge(silu_done, CONVT + 1)
            for i in range(2 * H + 1):
                if i < 2 * H:
                    if i >= 2:
                        act.wait_ge(l2ss, i - 1)
                    A(sqb[:, i % 2, :], qkvT[:, i, :], ACT.Square).then_inc(l2sq, 1)
                if i >= 1:
                    act.wait_ge(l2ss, i)
                    if i >= 3:
                        act.wait_ge(l2done, i - 2)
                    root(rsb[:, (i - 1) % 2, :], bank[4 + (i - 1) % 2][:, 0:T], 1.0).then_inc(root_ready, 1)
            for c in range(2):
                if c == 0:
                    act.wait_ge(l2done, 2 * H)
                    act.wait_ge(stage("cum_copied"), 1)
                else:
                    act.wait_ge(stage("gd_out"), 2)
                    act.wait_ge(stage("cum_copied"), 2)
                A(gcol[:, 1, :], gcol[:, 0, :], ACT.Exp).then_inc(stage("gexp"), 1)
                A(gcol[:, 4, :], gsc[:, 0, 0, :], ACT.Exp).then_inc(stage("gexp"), 1)
                A(gcol[:, 3, :], gsc[:, 0, 1, :], ACT.Exp).then_inc(stage("gexp"), 1)
                for q, (w, g) in enumerate(((0, 0), (1, 0), (0, 1), (1, 1))):
                    act.wait_ge(tr_ready, 4 * c + q + 1)
                    A((K2 if w == 0 else VB)[:, g, :], bank[2 * w + g][:, :], ACT.Copy).then_inc(tr_evac, 1)
                for g in range(2):
                    b0 = 4 - 4 * g
                    act.wait_ge(stage("gd_prod"), 2 * c + g + 1)
                    A(XTm[:, g, :], bank[b0][:, :], ACT.Exp).then_inc(stage("eg_done"), 1)
                    act.wait_ge(stage("dif_done"), 2 * c + g + 1)
                    A(LTm[:, g, :], LTm[:, g, :], ACT.Exp).then_inc(stage("dec_done"), 1)
                for lv in range(LEVELS):
                    for g in range(2):
                        act.wait_ge(stage("lx_done"), (c * LEVELS + lv) * 2 + g + 1)
                        A(LTm[:, g, :], bank[g][:, :], ACT.Copy).then_inc(stage("lx_copied"), 1)
                if c == 1:
                    for g in range(2):
                        act.wait_ge(stage("uw_done"), 2 + g + 1)
                        A(Xm[:, g, :], bank[2 + g][:, :], ACT.Copy).then_inc(stage("wt_copied"), 1)
                act.wait_ge(stored, 32)
                for g in range(2):
                    act.wait_ge(stage("os_done"), 2 * c + g + 1)
                    A(oG[:, 4 * g:4 * g + 4, c * P:(c + 1) * P], bank[6 + g][:, :].rearrange("p (h t) -> p h t", h=4),
                      ACT.Copy).then_inc(stage("o_copied"), 1)
            act.wait_ge(stage("sample_products"), 1)
            act.wait_ge(stage("gd_out"), 4)
            for y in range(2):
                A(kts[0:NSA, 4 * y:4 * y + 4, :], bank[y][0:NSA, :].rearrange("p (h t) -> p h t", h=4), ACT.Copy)
            link(A(bgb[:, 0, 0:1], ones[:, 0:1], ACT.Copy))
            act.wait_ge(stage("sample_products"), 2)
            A(bgb[:, 1, :], bank[2][:, 64:128], ACT.Exp)
            A(bgb[:, 0, :], bank[2][:, 0:64], ACT.Copy).then_inc(stage("kts_copied"), 1)
            act.wait_ge(stage("oss_ready"), 1)
            A(oG[:, :, NPR:T], bank[3][:, 64:128].rearrange("p (h b) -> p h b", h=H), ACT.Copy).then_inc(stage("o_copied"), 1)
            act.wait_ge(stage("o_copied"), 5)
            for h in range(H + 1):
                if h < H:
                    if h >= 2:
                        act.wait_ge(stage("on_ss"), h - 1)
                    A(msq[:, h % 2, :], oG[:, h, :], ACT.Square).then_inc(stage("on_sq"), 1)
                if h >= 1:
                    act.wait_ge(stage("on_ss"), h)
                    if h >= 3:
                        act.wait_ge(stage("on_rs"), h - 2)
                    root(mrs[:, (h - 1) % 2, :], bank[(h - 1) % 2][:, 0:T], 1.0 / P).then_inc(root_ready, 1)
            for m in range(H):
                act.wait_ge(stage("z_ready"), m + 1)
                if m == 0:
                    act.wait_ge(stage("on_rs"), H)
                if m >= 2:
                    act.wait_ge(stage("z_gated"), m - 1)
                A(zsig[:, m % 2, :], bank[m % 4][:, 0:T], ACT.Sigmoid).then_inc(stage("z_sig"), 1)
            for m in range(8):
                act.wait_ge(stage("lat_ready"), m + 1)
                A((cqT if m < 4 else latT)[:, m % 4, :], bank[4 + m % 4][:, 0:T], ACT.Copy).then_inc(stage("lat_evac"), 1)
            act.wait_ge(stage("kpe_ready"), 1)
            A(kpeT[:, :], bank[0][:, 0:T], ACT.Copy).then_inc(stage("kpe_copied"), 1)
            act.wait_ge(stage("lat_evac"), 8)
            act.wait_ge(stage("z_gated"), H)
            for i in range(2 * LORA):
                if i >= 2:
                    act.wait_ge(stage("lss"), i - 1)
                A(msq[:, i % 2, :], (cqT if i < 4 else latT)[:, i % 4, :], ACT.Square).then_inc(stage("lsq"), 1)
                if i % LORA == LORA - 1:
                    act.wait_ge(stage("lss"), i + 1)
                    root(mrs[:, i // LORA, :], bank[2 + i // LORA][:, 0:T], 1.0 / (LORA * P)).then_inc(root_ready, 1)
            for m in range(12):
                act.wait_ge(stage("q_ready"), m + 1)
                A(qnT[:, m, :] if m < 8 else qpeT[:, m - 8, :], bank[4 + m % 4][:, 0:T], ACT.Copy).then_inc(stage("q_evac"), 1)
            for h in range(H):
                act.wait_ge(stage("kn_ready"), h + 1)
                A(knT[:, h, :], bank[4 + h % 4][:, 0:NPR], ACT.Copy).then_inc(stage("kn_evac"), 1)
            for i in range(4):
                act.wait_ge(stage("vt_ready"), i + 1)
                A(vtok[:, i // 2, 512 * (i % 2):512 * (i % 2) + 512], bank[i][:, :], ACT.Copy).then_inc(stage("vt_evac"), 1)
            for h in range(H + 1):
                if h < H:
                    act.wait_ge(stage("pa_max"), h + 1)
                    if h >= 2:
                        act.wait_ge(stage("pa_turned"), h - 1)
                    st = mstat[:, h % 2, :]
                    A(mp[h % 2][:, 0:P], msc[h % 2][:, 0:P], ACT.Exp, bias=st[:, 2:3], scale=SCALE, accum_out=st[:, 4:5])
                    A(mp[h % 2][:, P:384], msc[h % 2][:, P:384], ACT.Exp, bias=st[:, 3:4], scale=SCALE, accum_out=st[:, 5:6]).then_inc(stage("pa_exp"), 1)
                if h >= 1:
                    j = h - 1
                    act.wait_ge(stage("pa_turned"), j + 1)
                    if j >= 2:
                        act.wait_ge(stage("pa_ready"), j - 1)
                    A(mpT[j % 2][:, :], bank[2 + j % 2][:, 0:384], ACT.Copy).then_inc(stage("pa_pcopied"), 1)
                    act.wait_ge(stage("pa_ready"), j + 1)
                    A(oM[:, j, 0:NPR], bank[4 + j % 2][:, 0:NPR], ACT.Copy).then_inc(stage("pa_out"), 1)
            act.wait_ge(stage("qlat_ready"), 1)
            A(qlat[:, :, :, :], bank[6][:, 0:256].rearrange("p (k h b) -> p k h b", k=LORA, h=H), ACT.Copy)
            A(qpeS[0:ROPE, :, 0, :], bank[7][0:ROPE, 0:32].rearrange("p (a b) -> p a b", a=4), ACT.Copy)
            A(qpeS[0:ROPE, :, 1, :], bank[7][0:ROPE, 32:64].rearrange("p (a b) -> p a b", a=4), ACT.Copy)
            act.wait_ge(stage("ltok_ready"), 1)
            A(lat_tok[0:NSA, :], bank[5][0:NSA, :], ACT.Copy).then_inc(stage("qlat_copied"), 1)
            for b in range(NSA + 1):
                if b < NSA:
                    act.wait_ge(stage("st_ready"), b + 1)
                    if b >= 2:
                        act.wait_ge(stage("s_turned"), b - 1)
                    A(sTs[b % 2][:, :], bank[6][:, 0:64], ACT.Copy).then_inc(stage("st_copied"), 1)
                    act.wait_ge(stage("s_max"), b + 1)
                    st = sstat[0:NSA, b % 2, :]
                    A(ps_[b % 2][0:NSA, :], ps_[b % 2][0:NSA, :], ACT.Exp, bias=st[:, 1:2], scale=SCALE, accum_out=st[:, 2:3]).then_inc(stage("s_exp"), 1)
                if b >= 1:
                    j = b - 1
                    act.wait_ge(stage("p_turned"), j + 1)
                    if j >= 2:
                        act.wait_ge(stage("ol_ready"), j - 1)
                    A(pT[j % 2][:, 0:64], bank[2][:, 0:64], ACT.Copy)
                    A(pT[j % 2][0:NSA, 64:72], bank[2][0:NSA, 64:72], ACT.Copy).then_inc(stage("pT_copied"), 1)
                    act.wait_ge(stage("ol_ready"), j + 1)
                    A(olat[:, :, :, j], bank[3][:, 0:32].rearrange("p (k h) -> p k h", k=LORA), ACT.Copy).then_inc(stage("ol_copied"), 1)
            act.wait_ge(stage("os_ready"), 1)
            A(oM[:, :, NPR:T], bank[7][:, 64:128].rearrange("p (h b) -> p h b", h=H), ACT.Copy).then_inc(stage("os_copied"), 1)
            for m in range(32):
                act.wait_ge(stage("out_ready"), m + 1)
                b = bank[m % 4][:, 0:T]
                if m // 8 == 0:
                    A(yA[:, m % 8, :], b, ACT.Copy).then_inc(stage("out_evac"), 1)
                elif m // 8 == 2:
                    A(yB[:, m % 8, :], b, ACT.Copy).then_inc(stage("out_evac"), 1)
                else:
                    i = (m // 16) * 8 + m % 8
                    if i >= 2:
                        act.wait_ge(stage("gated"), i - 1)
                    A(gsig[:, i % 2, :], b, ACT.Sigmoid).then_inc(stage("gate_sig"), 1)
            act.wait_ge(stage("out_evac"), 24)
            A(msq2[:, :, :], xT[:, :, :], ACT.Square).then_inc(sq_ready, 1)
            act.wait_ge(ss_ready, 2)
            root(mrs2[:, :], bank[4][:, 0:T], 1.0 / D).then_inc(root_ready, 1)
            act.wait_ge(stored, 64)
            for i in range(6):
                act.wait_ge(stage("h2_turned"), i + 1)
                n = P if i < 4 else NSA
                A(h2tok[0:n, i // 2, :, 64 * (i % 2):64 * (i % 2) + 64],
                  bank[i % 4][0:n, :].rearrange("p (x k) -> p k x", k=KD), ACT.Copy).then_inc(stage("h2_copied"), 1)
            act.wait_ge(stage("v8_ready"), 1)
            for i in range(3):
                A(ex[:, i, :], lg[:, i, :], ACT.Exp, bias=rst[:, 0, i:i + 1]).then_inc(stage("route_exp"), 1)
            moe_scalar(act)
            act.wait_ge(stage("x2_ready"), 1)
            A(msq2[:, :, :], xT[:, :, :], ACT.Square).then_inc(sq_ready, 1)
            act.wait_ge(ss_ready, 3)
            root(mrs2[:, :], bank[0][:, 0:T], 1.0 / D).then_inc(root_ready, 1)

        @block.vector
        def _(dve):
            line = [0]
            V = nc.vector

            def link(ins):
                line[0] += 1
                ins.then_inc(dve_line, 1)
                dve.wait_ge(dve_line, line[0])

            def norm_mod(r, x, out, sc, sh, nw, rs, A9):
                link(V.scalar_tensor_tensor(A9, mod[:, sc:sc + KD, :], 1.0,
                                            small[:, nw:nw + KD].unsqueeze(2).to_broadcast([P, KD, 9]), ALU.add, ALU.mult))
                dve.wait_ge(root_ready, (1, 28, 29)[r])
                link(V.reciprocal(rs, rs))
                link(V.tensor_tensor(out, x, rs.unsqueeze(1).to_broadcast([P, KD, T]), ALU.mult))
                for k in range(KD):
                    link(V.tensor_scalar(out[:, k, 0:NPR], out[:, k, 0:NPR], A9[:, k, 0:1], mod[:, sh + k, 0:1], ALU.mult, ALU.add))
                link(V.tensor_tensor(out[:, :, NPR:T], out[:, :, NPR:T], A9[:, :, 1:9], ALU.mult))
                V.tensor_tensor(out[:, :, NPR:T], out[:, :, NPR:T], mod[:, sh:sh + KD, 1:9], ALU.add).then_inc(h_ready, 1)
                dve.wait_ge(h_ready, r + 1)

            dve.wait_ge(inputs_in, 64)
            link(V.memset(upad[:, :, 0:3], 0.0))
            link(V.memset(gsc[:, :, :, :], 0.0))
            V.memset(rsb[:, :, :], 0.0).then_inc(stage("upad_zero"), 1)
            for n in range(FIN + 4):
                dve.wait_ge(mod_ready, n + 1)
                V.tensor_tensor(mod[:, 4 * n:4 * n + 4, :], bank[n % 2][:, 0:36].rearrange("p (m c) -> p m c", c=9),
                                small[:, S_BADA + 4 * n:S_BADA + 4 * n + 4].unsqueeze(2).to_broadcast([P, 4, 9]),
                                ALU.add).then_inc(mod_evac, 1)
            dve.wait_ge(mod_evac, FIN + 4)
            dve.wait_ge(stage("upad_zero"), 1)
            norm_mod(0, xT[:, :, :], hT[:, :, :], 8, 0, S_NMIX, rsb[:, 0, :], modA[:, :, :])
            for m in range(CONVT + 1):
                if m < CONVT:
                    dve.wait_ge(proj_evac, m + 1)
                    u = upad[:, m % 3, :]
                    y = qkvT[:, m, 0:NPR]
                    link(V.tensor_scalar(y, u[:, 0:NPR], convw[:, m, 0:1], None, ALU.mult))
                    for j in range(1, 3):
                        link(V.scalar_tensor_tensor(y, u[:, j:j + NPR], convw[:, m, j:j + 1], y, ALU.mult, ALU.add))
                    V.scalar_tensor_tensor(y, u[:, 3:3 + NPR], convw[:, m, 3:4], y, ALU.mult, ALU.add).then_inc(conv_done, 1)
                if m >= 1:
                    dve.wait_ge(sig_done, m)
                    V.tensor_tensor(qkvT[:, m - 1, 0:NPR], qkvT[:, m - 1, 0:NPR], sigb[:, (m - 1) % 2, 0:NPR], ALU.mult).then_inc(silu_done, 1)
            for j in range(4):
                dst = smt[:, 0, :, :] if j == 0 else smt[:, 1, :, :]
                link(V.tensor_tensor(dst, samp[:, :, j, :], convw[:, :, j:j + 1].to_broadcast([P, CONVT, NSA]), ALU.mult))
                if j:
                    ins = V.tensor_tensor(smt[:, 0, :, :], smt[:, 0, :, :], smt[:, 1, :, :], ALU.add)
                    if j < 3:
                        link(ins)
                    else:
                        ins.then_inc(stage("conv_s"), 1)
            dve.wait_ge(sig_done, CONVT + 1)
            V.tensor_tensor(qkvT[:, :, NPR:T], smt[:, 0, :, :], smt[:, 1, :, :], ALU.mult).then_inc(silu_done, 1)
            dve.wait_ge(ab_ready, 1)
            dve.wait_ge(dve_line, line[0])
            for i, n in ((0, P), (1, P), (2, NSA)):
                link(V.tensor_copy(gsc[0:n, 0, i, :], bank[6][0:n, 16 * i:16 * i + 8]))
                ins = V.tensor_tensor(gsc[0:n, 1, i, :], bank[6][0:n, 16 * i + 8:16 * i + 16], small[0:n, S_DT:S_DT + 8], ALU.add)
                if i < 2:
                    link(ins)
                else:
                    ins.then_inc(stage("ab_copied"), 1)
            dve.wait_ge(ab_act, 2)
            link(V.tensor_scalar(gsc[:, 1, :, :], gsc[:, 1, :, :], 0.0, None, ALU.max))
            link(V.tensor_tensor(gsc[:, 1, :, :], gsc[:, 1, :, :], gsc[:, 2, :, :], ALU.add))
            dve.wait_ge(act_line, 3)
            V.scalar_tensor_tensor(g_tok[:, :, :], gsc[:, 1, :, :], -1.0, gcol[:, 0, :].unsqueeze(1).to_broadcast([P, 3, H]),
                                   ALU.mult, ALU.mult).then_inc(bg_done, 1)
            for i in range(2 * H):
                dve.wait_ge(root_ready, i + 2)
                link(V.reciprocal(rsb[:, i % 2, :], rsb[:, i % 2, :]))
                V.scalar_tensor_tensor(qkvT[:, i, :], qkvT[:, i, :], P ** -0.5 if i < H else 1.0, rsb[:, i % 2, :], ALU.mult, ALU.mult).then_inc(l2done, 1)
                dve.wait_ge(l2done, i + 1)
            dve.wait_ge(stage("cum_ready"), 1)
            V.tensor_copy(cumc[:, :, :], bank[6][:, 64:96].rearrange("p (c e) -> p c e", c=2)).then_inc(stage("cum_read"), 1)
            dve.wait_ge(stage("cum_read"), 1)
            for c in range(2):
                if c == 1:
                    dve.wait_ge(stage("gd_out"), 2)
                link(V.tensor_copy(gcol[:, 0, :], cumc[:, c, 0:8]))
                link(V.tensor_copy(gsc[:, 0, 0, :], cumc[:, c, 8:16]))
                V.tensor_tensor(gsc[:, 0, 1, :], cumc[:, c, 8:16], cumc[:, c, 0:8], ALU.subtract).then_inc(stage("cum_copied"), 1)
                dve.wait_ge(stage("gexp"), 3 * c + 3)
                link(V.tensor_tensor(gcol[:, 2, :], gcol[:, 1, :], beta_tok[:, c, :], ALU.mult))
                for g in range(2):
                    b0 = 4 - 4 * g
                    hs = slice(4 * g, 4 * g + 4)

                    def heads(v):
                        return v.rearrange("p (h t) -> p h t", h=4)

                    def col(v):
                        return v.unsqueeze(2).to_broadcast([P, 4, P])

                    def row(v):
                        return v.unsqueeze(1).to_broadcast([P, 4, P])
                    dve.wait_ge(stage("gd_prod"), 2 * c + g + 1)
                    dve.wait_ge(stage("eg_done"), 2 * c + g + 1)
                    link(V.tensor_tensor(heads(LTm[:, g, :]), heads(bank[b0][:, :]), col(gcol[:, 0, hs]), ALU.subtract))
                    V.tensor_scalar(LTm[:, g, :], LTm[:, g, :], 0.0, None, ALU.min).then_inc(stage("dif_done"), 1)
                    link(V.tensor_tensor(heads(qg[:, g, :]), heads(XTm[:, g, :]), qkvT[:, hs, c * P:(c + 1) * P], ALU.mult))
                    dve.wait_ge(tr_evac, 4 * c + 4)
                    link(V.tensor_tensor(heads(VB[:, g, :]), heads(VB[:, g, :]), col(beta_tok[:, c, hs]), ALU.mult))
                    link(V.tensor_tensor(heads(KBG[:, g, :]), heads(K2[:, g, :]), col(gcol[:, 2, hs]), ALU.mult))
                    link(V.tensor_tensor(heads(K2[:, g, :]), heads(K2[:, g, :]), col(gcol[:, 3, hs]), ALU.mult))
                    dve.wait_ge(stage("dec_done"), 2 * c + g + 1)
                    link(V.tensor_tensor(heads(LTm[:, g, :]), heads(LTm[:, g, :]), row(upto), ALU.mult))
                    link(V.tensor_tensor(Aqk[:, g, :], bank[b0 + 3][:, :], LTm[:, g, :], ALU.mult))
                    link(V.tensor_tensor(AT[:, g, :], bank[b0 + 2][:, :], LTm[:, g, :], ALU.mult))
                    link(V.tensor_tensor(AT[:, g, :], bank[b0 + 1][:, :], AT[:, g, :], ALU.mult))
                    link(V.tensor_copy(heads(Xm[:, g, :]), row(ident)))
                    V.tensor_copy(heads(XTm[:, g, :]), row(ident)).then_inc(stage("prep_done"), 1)
                    dve.wait_ge(stage("prep_done"), 2 * c + g + 1)
                for lv in range(LEVELS):
                    mask = con[:, C_LEV + lv * P:C_LEV + (lv + 1) * P]
                    for g in range(2):
                        q = (c * LEVELS + lv) * 2 + g + 1
                        if lv >= 1:
                            dve.wait_ge(stage("xlx_done"), q - 2)
                            link(V.tensor_tensor(Xm[:, g, :], Xm[:, g, :], bank[2 + g][:, :], ALU.subtract))
                            V.tensor_tensor(XTm[:, g, :], XTm[:, g, :], bank[4 + g][:, :], ALU.subtract).then_inc(stage("x_done"), 1)
                            dve.wait_ge(stage("x_done"), q - 2)
                        V.tensor_tensor(heads(LTm[:, g, :]), heads(AT[:, g, :]), row(mask), ALU.mult).then_inc(stage("lt_done"), 1)
                for g in range(2):
                    q = (c * LEVELS + LEVELS) * 2 + g + 1 - 2
                    dve.wait_ge(stage("xlx_done"), q)
                    V.tensor_tensor(XTm[:, g, :], XTm[:, g, :], bank[4 + g][:, :], ALU.subtract).then_inc(stage("x_done"), 1)
                for g in range(2):
                    dve.wait_ge(stage("uw_done"), 2 * c + g + 1)
                    if c == 0:
                        V.tensor_copy(VB[:, g, :], bank[g][:, :]).then_inc(stage("vn_done"), 1)
                    else:
                        link(V.tensor_copy(VB[:, g, :], bank[g][:, :]))
                        dve.wait_ge(stage("ws_done"), g + 1)
                        V.tensor_tensor(VB[:, g, :], VB[:, g, :], bank[4 + g][:, :], ALU.subtract).then_inc(stage("vn_done"), 1)
                for g in range(2):
                    dve.wait_ge(stage("os_done"), 2 * c + g + 1)
                    dve.wait_ge(stage("o_copied"), 2 * c + g + 1)
                    if c == 1:
                        link(V.tensor_tensor(heads(Sst[:, g, :]), heads(Sst[:, g, :]), col(gcol[:, 4, 4 * g:4 * g + 4]), ALU.mult))
                        V.tensor_tensor(Sst[:, g, :], Sst[:, g, :], bank[2 + g][:, :], ALU.add).then_inc(stage("gd_out"), 1)
                    else:
                        V.tensor_copy(Sst[:, g, :], bank[2 + g][:, :]).then_inc(stage("gd_out"), 1)
                    dve.wait_ge(stage("gd_out"), 2 * c + g + 1)
            dve.wait_ge(stage("ssmp_stored"), 16)
            eye8 = ident[0:NSA, 0:NSA].unsqueeze(1).to_broadcast([NSA, H, NSA])
            link(V.tensor_tensor(bgm[0:NSA, 0, :].rearrange("p (h b) -> p h b", h=H), eye8,
                                 beta_tok[0:NSA, 2, :].unsqueeze(2).to_broadcast([NSA, H, NSA]), ALU.mult))
            V.tensor_tensor(bgm[0:NSA, 1, :].rearrange("p (h b) -> p h b", h=H), eye8,
                            g_tok[0:NSA, 2, :].unsqueeze(2).to_broadcast([NSA, H, NSA]), ALU.mult).then_inc(stage("bgm_ready"), 1)
            dve.wait_ge(stage("sample_products"), 3)
            dve.wait_ge(stage("kts_copied"), 1)
            hb = lambda v: v.rearrange("p (h b) -> p h b", h=H)
            link(V.tensor_tensor(vnT[:, :, :], hb(bank[3][:, 0:64]), hb(bgb[:, 1, :]), ALU.mult))
            link(V.tensor_tensor(vnT[:, :, :], qkvT[:, 2 * H:3 * H, NPR:T], vnT[:, :, :], ALU.subtract))
            V.tensor_tensor(vnT[:, :, :], vnT[:, :, :], hb(bgb[:, 0, :]), ALU.mult).then_inc(stage("vns_ready"), 1)
            dve.wait_ge(stage("sample_products"), 4)

            def spread(h):
                if h >= 2:
                    dve.wait_ge(stage("outer"), h - 1)
                V.tensor_tensor(vnm[0:NSA, h % 2, :].rearrange("p (b v) -> p b v", b=NSA),
                                bank[h // 4][0:NSA, (h % 4) * P:(h % 4 + 1) * P].unsqueeze(1).to_broadcast([NSA, NSA, P]),
                                ident[0:NSA, 0:NSA].unsqueeze(2).to_broadcast([NSA, NSA, P]), ALU.mult).then_inc(stage("vnm_ready"), 1)
            spread(0)
            for h in range(H):
                if h + 1 < H:
                    spread(h + 1)
                S = ssm_view[h // 4][:, h % 4, :, :]
                link(V.tensor_tensor(S, S, bgb[:, 1, h * NSA:(h + 1) * NSA].unsqueeze(2).to_broadcast([P, NSA, P]), ALU.mult))
                dve.wait_ge(stage("outer"), h + 1)
                link(V.tensor_tensor(S[:, 0:4, :], S[:, 0:4, :], bank[4 + 2 * (h % 2)][:, :].rearrange("p (b v) -> p b v", b=4), ALU.add))
                V.tensor_tensor(S[:, 4:8, :], S[:, 4:8, :], bank[5 + 2 * (h % 2)][:, :].rearrange("p (b v) -> p b v", b=4), ALU.add).then_inc(stage("snew"), 1)
            for h in range(H):
                dve.wait_ge(root_ready, 18 + h)
                link(V.reciprocal(mrs[:, h % 2, :], mrs[:, h % 2, :]))
                V.scalar_tensor_tensor(oG[:, h, :], oG[:, h, :], small[:, S_NGDN:S_NGDN + 1], mrs[:, h % 2, :], ALU.mult, ALU.mult).then_inc(stage("on_rs"), 1)
                dve.wait_ge(stage("on_rs"), h + 1)
            for m in range(H):
                dve.wait_ge(stage("z_sig"), m + 1)
                V.tensor_tensor(zsig[:, m % 2, :], zsig[:, m % 2, :], bank[m % 4][:, 0:T], ALU.mult).then_inc(stage("z_evac"), 1)
                dve.wait_ge(stage("z_evac"), m + 1)
                V.tensor_tensor(oG[:, m, :], oG[:, m, :], zsig[:, m % 2, :], ALU.mult).then_inc(stage("z_gated"), 1)

            def rotate(x, turned):
                link(V.tensor_tensor(rot[:, :], turned, sinT, ALU.mult))
                link(V.tensor_tensor(x, x, cosT, ALU.mult))
                return V.tensor_tensor(x, x, rot[:, :], ALU.add)
            dve.wait_ge(stage("kpe_turned"), 1)
            rotate(kpeT[:, :], bank[1][:, 0:T]).then_inc(stage("kpe_rot"), 1)
            for w in range(2):
                dve.wait_ge(root_ready, 26 + w)
                link(V.reciprocal(mrs[:, w, :], mrs[:, w, :]))
                for i in range(LORA):
                    v = (cqT, latT)[w][:, i, :]
                    nw = (S_NQ, S_NKV)[w] + i
                    ins = V.scalar_tensor_tensor(v, v, small[:, nw:nw + 1], mrs[:, w, :], ALU.mult, ALU.mult)
                    if i < LORA - 1:
                        link(ins)
                    else:
                        ins.then_inc(stage("lat_normed"), 1)
            dve.wait_ge(stage("kpe_rot"), 1)
            for i in range(4):
                dve.wait_ge(stage("q_turn"), i + 1)
                rotate(qpeT[:, i, :], bank[i % 2][:, 0:T]).then_inc(stage("q_turned"), 1)
                dve.wait_ge(stage("q_turned"), i + 1)
            def normalise(j):
                dve.wait_ge(stage("pa_exp"), j + 1)
                st = mstat[:, j % 2, :]
                link(V.reciprocal(st[:, 6:8], st[:, 4:6]))
                link(V.tensor_scalar(mp[j % 2][:, 0:P], mp[j % 2][:, 0:P], st[:, 6:7], None, ALU.mult))
                V.tensor_scalar(mp[j % 2][:, P:384], mp[j % 2][:, P:384], st[:, 7:8], None, ALU.mult).then_inc(stage("pa_probs"), 1)

            for h in range(H + 1):
                if h < H:
                    dve.wait_ge(stage("pa_scores"), h + 1)
                    V.tensor_tensor(msc[h % 2][:, :], bank[h % 2][:, 0:384], neg384, ALU.add).then_inc(stage("pa_masked"), 1)
                    dve.wait_ge(stage("pa_masked"), h + 1)
                    st = mstat[:, h % 2, :]
                    link(V.tensor_reduce(st[:, 0:1], msc[h % 2][:, 0:P], AX, ALU.max))
                    link(V.tensor_reduce(st[:, 1:2], msc[h % 2][:, P:384], AX, ALU.max))
                    V.tensor_scalar(st[:, 2:4], st[:, 0:2], -SCALE, None, ALU.mult).then_inc(stage("pa_max"), 1)
                if h >= 1:
                    normalise(h - 1)
            for b in range(NSA):
                dve.wait_ge(stage("s_turned"), b + 1)
                if b == 0:
                    dve.wait_ge(stage("qlat_copied"), 1)
                if b >= 2:
                    dve.wait_ge(stage("p_turned"), b - 1)
                S = ps_[b % 2]
                st = sstat[0:NSA, b % 2, :]
                link(V.tensor_copy(S[0:NSA, 0:512], bank[0][0:NSA, :]))
                link(V.tensor_copy(S[0:NSA, 512:1024], bank[1][0:NSA, :]))
                V.tensor_tensor(S[0:NSA, 1024:1032], bank[4][0:NSA, 0:NSA], con[0:NSA, C_B8 + 8 * b:C_B8 + 8 * b + 8], ALU.add).then_inc(stage("s_read"), 1)
                dve.wait_ge(stage("s_read"), b + 1)
                link(V.tensor_reduce(st[:, 0:1], S[0:NSA, :], AX, ALU.max))
                V.tensor_scalar(st[:, 1:2], st[:, 0:1], -SCALE, None, ALU.mult).then_inc(stage("s_max"), 1)
                dve.wait_ge(stage("s_exp"), b + 1)
                link(V.reciprocal(st[:, 3:4], st[:, 2:3]))
                V.tensor_scalar(S[0:NSA, :], S[0:NSA, :], st[:, 3:4], None, ALU.mult).then_inc(stage("p_ready"), 1)
            dve.wait_ge(stage("out_evac"), 8)
            for i in range(16):
                dve.wait_ge(stage("gate_sig"), i + 1)
                y = (yA, yB)[i // 8][:, i % 8, :]
                if i == 8:
                    dve.wait_ge(stage("out_evac"), 16)
                if i < 8:
                    V.tensor_tensor(y, y, gsig[:, i % 2, :], ALU.mult).then_inc(stage("gated"), 1)
                    dve.wait_ge(stage("gated"), i + 1)
                else:
                    V.tensor_tensor(y, y, gsig[:, i % 2, :], ALU.mult).then_inc(stage("gated"), 1)
                    dve.wait_ge(stage("gated"), i + 1)
                    V.tensor_tensor(yA[:, i % 8, :], yA[:, i % 8, :], y, ALU.add).then_inc(stage("merged"), 1)
            for m in range(KD):
                dve.wait_ge(stage("out_ready"), 33 + m)
                b = bank[m % 4]
                link(V.scalar_tensor_tensor(xT[:, m, 0:NPR], b[:, 0:NPR], mod[:, 16 + m, 0:1], xT[:, m, 0:NPR], ALU.mult, ALU.add))
                link(V.tensor_tensor(mrs2[:, 0:NSA], b[:, NPR:T], mod[:, 16 + m, 1:9], ALU.mult))
                V.tensor_tensor(xT[:, m, NPR:T], xT[:, m, NPR:T], mrs2[:, 0:NSA], ALU.add).then_inc(stage("out_evac"), 1)
                dve.wait_ge(stage("out_evac"), 17 + m)
            norm_mod(1, xT[:, :, :], hT[:, :, :], 32, 24, S_NFFN, mrs2[:, :], modA2[:, :, :])
            dve.wait_ge(stage("logits"), 1)
            link(V.memset(lg[:, :, :], 0.0))
            for p_ in pre:
                link(V.memset(p_[:, :, :], 0.0))
            br = small[:, S_BR:S_BR + NE]
            link(V.tensor_tensor(lg[:, 0:2, :], bank[5][:, 0:64].rearrange("p (i e) -> p i e", i=2), br.unsqueeze(1).to_broadcast([P, 2, NE]), ALU.add))
            link(V.tensor_tensor(lg[0:NSA, 2, :], bank[5][0:NSA, 64:96], br[0:NSA, :], ALU.add))
            for i in range(3):
                link(V.max(v8[:, i, :], lg[:, i, :]))
            V.tensor_scalar(rst[:, 0, :], v8[:, :, 0], -1.0, None, ALU.mult).then_inc(stage("v8_ready"), 1)
            fourth = v8[:, :, 3:4].to_broadcast([P, 3, NE])
            link(V.tensor_tensor(sel[:, :, :], lg[:, :, :], fourth, ALU.is_gt))
            link(V.tensor_tensor(eqm[:, :, :], lg[:, :, :], fourth, ALU.is_equal))
            link(V.tensor_reduce(rst[:, 1, :], sel[:, :, :], AX, ALU.add))
            link(V.tensor_scalar(rst[:, 1, :], rst[:, 1, :], -1.0, 4.0, ALU.mult, ALU.add))
            link(V.tensor_copy(pre[0][:, :, 16:48], eqm[:, :, :]))
            for i, s in enumerate((1, 2, 4, 8, 16)):
                a, b = pre[i % 2], pre[(i + 1) % 2]
                link(V.tensor_tensor(b[:, :, 16:48], a[:, :, 16:48], a[:, :, 16 - s:48 - s], ALU.add))
            link(V.tensor_tensor(pre[0][:, :, 16:48], pre[1][:, :, 16:48], rst[:, 1, :].unsqueeze(2).to_broadcast([P, 3, NE]), ALU.is_le))
            link(V.tensor_tensor(eqm[:, :, :], eqm[:, :, :], pre[0][:, :, 16:48], ALU.mult))
            V.tensor_tensor(sel[:, :, :], sel[:, :, :], eqm[:, :, :], ALU.add).then_inc(stage("sel_ready"), 1)
            dve.wait_ge(stage("sel_ready"), 1)
            dve.wait_ge(stage("route_exp"), 3)
            link(V.tensor_tensor(ex[:, :, :], ex[:, :, :], sel[:, :, :], ALU.mult))
            link(V.tensor_reduce(rst[:, 2, :], ex[:, :, :], AX, ALU.add))
            link(V.reciprocal(rst[:, 3, :], rst[:, 2, :]))
            V.tensor_tensor(gate[:, :, :], ex[:, :, :], rst[:, 3, :].unsqueeze(2).to_broadcast([P, 3, NE]), ALU.mult).then_inc(stage("sel_ready"), 1)
            dve.wait_ge(stage("route"), 1)
            link(V.tensor_copy(cntc[0:NE, 4:5], bank[7][0:NE, 0:1]))
            link(V.tensor_scalar(cntc[0:NE, 0:1], cntc[0:NE, 4:5], 0.0, None, ALU.is_gt))
            for i in range(1, 5):
                ins = V.scalar_tensor_tensor(cntc[0:NE, 0:1], cntc[0:NE, 4:5], float(SLOT * i), cntc[0:NE, 0:1], ALU.is_gt, ALU.add)
                if i < 4:
                    link(ins)
                else:
                    ins.then_inc(stage("blocks"), 1)
            dve.wait_ge(stage("blocks"), 1)
            dve.wait_ge(stage("route"), 2)
            link(V.tensor_copy(cntc[0:NE, 1:2], bank[7][0:NE, 1:2]))
            link(V.tensor_tensor(cntc[0:NE, 2:3], cntc[0:NE, 1:2], cntc[0:NE, 0:1], ALU.add))
            link(V.tensor_scalar(cntc[0:NE, 3:4], cntc[0:NE, 1:2], float(SLOT), 1.0, ALU.mult, ALU.add))
            jrow = con[0:NE, C_J:C_J + NJ1]
            link(V.tensor_scalar(ge1[0:NE, :], jrow, cntc[0:NE, 1:2], None, ALU.is_ge))
            V.scalar_tensor_tensor(e1h[0:NE, :], jrow, cntc[0:NE, 2:3], ge1[0:NE, :], ALU.is_lt, ALU.mult).then_inc(stage("e1h_ready"), 1)
            link(V.tensor_copy(maskT[0:NE, :], bank[4][0:NE, 0:T]))
            link(V.tensor_copy(gateT[0:NE, :], bank[0][0:NE, 0:T]))
            V.scalar_tensor_tensor(m1T[0:NE, :], bank[6][0:NE, 0:T], cntc[0:NE, 3:4], maskT[0:NE, :], ALU.add, ALU.mult).then_inc(stage("m1_ready"), 1)
            dve.wait_ge(stage("route"), 3)
            link(V.tensor_copy(items[0:1, 1:1 + NJ1], bank[7][0:1, 8:8 + NJ1]))
            V.tensor_copy(items[0:1, 0:1], bank[7][0:1, 2:3]).then_inc(stage("items_ready"), 1)
            dve.wait_ge(stage("route"), 4)
            for i, n in ((0, P), (1, P), (2, NSA)):
                link(V.tensor_tensor(rr[0:n, i, :], bank[1][0:n, NJ1 * i:NJ1 * (i + 1)], con[0:n, C_J64:C_J64 + NJ1], ALU.subtract))
                ins = V.tensor_copy(gg[0:n, i, :], bank[2][0:n, NJ1 * i:NJ1 * (i + 1)])
                if i < 2:
                    link(ins)
                else:
                    ins.then_inc(stage("rg_copied"), 1)
            dve.wait_ge(stage("rg_copied"), 1)
            dve.wait_ge(stage("items_ready"), 1)
            moe_vector(dve, link)
            for m in range(KD):
                link(V.scalar_tensor_tensor(xT[:, m, 0:NPR], acc[:, m, 0:NPR], mod[:, 40 + m, 0:1], xT[:, m, 0:NPR], ALU.mult, ALU.add))
            link(V.tensor_tensor(acc[:, :, NPR:T], acc[:, :, NPR:T], mod[:, 40:48, 1:9], ALU.mult))
            V.tensor_tensor(xT[:, :, NPR:T], xT[:, :, NPR:T], acc[:, :, NPR:T], ALU.add).then_inc(stage("x2_ready"), 1)
            norm_mod(2, xT[:, :, :], yout[:, :, :], 56, 48, S_NFIN, mrs2[:, :], modA2[:, :, :])

        @block.gpsimd
        def _(pool):
            pool.wait_ge(h_ready, 1)
            pool.wait_ge(silu_done, CONVT + 1)
            pool.wait_ge(proj_evac, CONVT)
            pool.dma_start(t["o_convp"], convp[:, :, :]).then_inc(stored, 16)
            pool.dma_start(t["o_convs"], samp[:, :, :, :]).then_inc(stored, 16)
            pool.wait_ge(stage("gd_out"), 4)
            pool.dma_start(t["o_ssmp"], Sst[:, :, :]).then_inc(stage("ssmp_stored"), 16)
            for i in range(2):
                pool.wait_ge(stage("snew"), 4 * i + 4)
                pool.wait_ge(stage("oss_ready"), 1)
                pool.dma_start(t["o_ssms"][i, :, :], ring[(SSM + i) % RING][:, :]).then_inc(stage(f"ssm_stored{i}"), 16)
            pool.wait_ge(stage("kpe_rot"), 1)
            pool.dma_start(t["o_kpe"], kpeT[0:ROPE, :]).then_inc(stored, 16)
            pool.wait_ge(stage("lat_normed"), 2)
            pool.dma_start(t["o_lat"], latT[:, :, :]).then_inc(stored, 16)
            pool.wait_ge(stage("out_ready"), 8)
            nc.gpsimd.memset(acc[:, :, :], 0.0).then_inc(acc_added, 1)
            pool.wait_ge(h_ready, 3)
            pool.dma_start(t["o_y"], yout[:, :, :]).then_inc(stored, 16)
            pool.wait_ge(stored, 80)
            pool.wait_ge(stage("ssm_stored0"), 16)
            pool.wait_ge(stage("ssm_stored1"), 16)
            pool.wait_ge(stage("ssmp_stored"), 16)


Q0, Z0, B0, CQ0, CKV0, KPE0, GA0, GB0 = 0, 3072, 4096, 4112, 4624, 5136, 5200, 6224


def wp_index(n):
    if n < SSM:
        return n
    if n < KVS:
        return n - 2
    return n - 2 - 2 * NSA


def lay_out(i):
    f = np.float32

    def cols(w, c0, n):
        w = w[:, c0:c0 + 512 * n].reshape(-1, P, n, 512)
        return w.transpose(2, 1, 0, 3).reshape(n, P, -1)

    def vec(v):
        return v.reshape(-1, P).T

    w_in = i["w_in"][0]
    w_uq = i["w_uq"][0].reshape(LORA, P, H, 192)
    half = np.zeros((P, 2048), f)
    uqr = w_uq[..., 128:].reshape(LORA, P, 512).transpose(1, 0, 2).reshape(P, 2048)
    uk = i["w_uk"][0].reshape(H, LORA, P, P)
    uv = i["w_uv"][0].reshape(H, LORA, P, P).transpose(2, 1, 0, 3).reshape(1, P, CH)
    wpre = np.concatenate([
        cols(i["w_ada"][0], 0, 12), cols(i["w_ada_final"], 0, 4), cols(w_in, Q0, 6), cols(w_in, Z0, 2),
        cols(w_in, CQ0, 1), cols(w_in, CKV0, 1),
        w_uq[..., :128].reshape(LORA, P, 1024).transpose(1, 0, 2).reshape(1, P, CH),
        np.concatenate([uqr, half], 1)[None],
        uk.transpose(2, 1, 0, 3).reshape(1, P, CH), uv,
        i["w_uk"][0].transpose(2, 0, 1).reshape(1, P, CH), uv,
        cols(i["w_o_gdn"][0], 0, 2), cols(w_in, GA0, 2), cols(i["w_o_mla"][0], 0, 2), cols(w_in, GB0, 2),
        cols(i["w_out"][0], 0, 2)], 0)
    n = np.arange(P)
    con = np.zeros((P, NCONST), f)
    con[:, C_ID:C_ID + P] = np.eye(P)
    con[:, C_ONE:C_ONE + P] = 1
    con[:, C_U:C_U + P] = n[:, None] <= n[None]
    con[:, C_STR:C_STR + P] = n[:, None] < n[None]
    con[:, C_PERM:C_PERM + P] = n[:, None] == (n[None] ^ 32)
    for lv in range(LEVELS):
        b = 1 << lv
        con[:, C_LEV + lv * P:C_LEV + (lv + 1) * P] = ((n[:, None] // (2 * b) == n[None] // (2 * b))
                                                     & (n[:, None] // b % 2 == 0) & (n[None] // b % 2 == 1))
    inv = f(10000.0) ** (-np.arange(32, dtype=f) / f(32))
    pos = np.concatenate([np.arange(NPR), np.full(NSA, PAGES * P)]).astype(f)
    ang = inv[n % 32][:, None] * pos[None]
    con[:, C_COS:C_COS + T] = np.cos(ang)
    con[:, C_SIN:C_SIN + T] = np.sin(ang) * np.where(n % 64 < 32, -1, 1)[:, None]
    low = np.where(n[None] <= n[:, None], 0, NEG)
    con[:, C_NEG:C_NEG + P] = low
    con[:, C_NEG + 256:C_NEG + 384] = low
    con[:, C_IOTA:C_IOTA + SLOT] = np.arange(SLOT)
    con[:, C_J:C_J + NJ1] = np.arange(NJ1)
    con[:, C_J64:C_J64 + NJ1] = SLOT * np.arange(NJ1) + 1
    con[:, C_E] = n
    con[:, C_EPS] = EPS
    con[0:2, C_TWO:C_TWO + P] = np.arange(2)[:, None] == n[None] // 64
    con[:, C_B8:C_B8 + 64] = np.where(np.eye(8) > 0, 0, NEG).reshape(64)
    small = np.empty((P, NSMALL), f)
    small[:, S_NMIX:S_NMIX + 8] = vec(i["norm_mix_w"])
    small[:, S_NFFN:S_NFFN + 8] = vec(i["norm_ffn_w"])
    small[:, S_NFIN:S_NFIN + 8] = vec(i["norm_final_w"])
    small[:, S_NQ:S_NQ + 4] = vec(i["q_norm_w"])
    small[:, S_NKV:S_NKV + 4] = vec(i["kv_norm_w"])
    small[:, S_NGDN:S_NGDN + 1] = vec(i["gdn_norm_w"])
    small[:, S_BADA:S_BADA + 64] = np.concatenate([vec(i["b_ada"]), vec(i["b_ada_final"])], 1)
    small[:, S_ALOG:S_ALOG + 8] = i["A_log"]
    small[:, S_DT:S_DT + 8] = i["dt_bias"]
    small[:, S_BR:S_BR + NE] = i["b_router"]
    small[:, S_CW:S_CW + CONVT * 4] = i["conv_w"][0].reshape(CONVT, P, 4).transpose(1, 0, 2).reshape(P, -1)
    kpe = w_in[:, KPE0:KPE0 + ROPE]
    small[:, S_WSM:S_WSM + KD * WSM] = np.concatenate([w_in[:, B0:B0 + 16], kpe, kpe, i["w_router"][0]],
                                                      1).reshape(KD, P, WSM).transpose(1, 0, 2).reshape(P, -1)
    c = np.concatenate([i["c_prompt"], i["c_sample"]], 0)
    small[:, S_CT:] = c.T.reshape(KD, P, 9).transpose(1, 0, 2).reshape(P, -1)
    x = np.concatenate([i["x_prompt"][0], i["x_sample"][:, 0]], 0)
    conv = np.zeros((P, CONVT, 4, NSA), f)
    conv[:, :, 0:3] = i["state_conv"][0].reshape(NSA, 3, CONVT, P).transpose(3, 2, 1, 0)
    kv = i["cache_kv"][0]
    return {
        "small": small,
        "biases": np.concatenate([i["b_gu"][0].reshape(NE, 2, 2, 512), i["b_dn"][0].reshape(NE, 1, 2, 512)],
                                 1).transpose(0, 2, 1, 3).reshape(NE, 2, -1),
        "con": con,
        "xT": x.T.reshape(KD, P, T).transpose(1, 0, 2),
        "convT": conv,
        "pages": i["page_table"].reshape(1, -1),
        "wpre": wpre,
        "ssm": i["state_ssm"][0].reshape(NSA, 2, 4, P, P).transpose(1, 3, 2, 0, 4).reshape(2, P, CH),
        "kvT": kv.reshape(NPHYS, P, LORA, P).transpose(0, 3, 2, 1).reshape(NPHYS, P, 512),
        "kv": kv,
        "peT": i["cache_pe"][0].transpose(0, 2, 1),
        "w_gu": i["w_gu"][0],
        "w_dn": i["w_dn"][0],
    }


OUTS = {
    "o_y": (P, KD, T), "o_lat": (P, LORA, T), "o_kpe": (ROPE, T), "o_ssmp": (P, 2, 512),
    "o_convp": (P, CONVT, 3), "o_ssms": (2, P, CH), "o_convs": (P, CONVT, 4, NSA),
}


def kernel(**inputs):
    import concourse.bacc as bacc
    from concourse.bass_utils import run_bass_kernel_spmd

    nc = bacc.Bacc("TRN2", target_bir_lowering=False, num_devices=1)
    arrays = {k: np.ascontiguousarray(v) for k, v in lay_out({k: np.asarray(v) for k, v in inputs.items()}).items()}
    t = {k: nc.dram_tensor(k, v.shape, mybir.dt.from_np(v.dtype), kind="ExternalInput").ap() for k, v in arrays.items()}
    for k, shape in OUTS.items():
        t[k] = nc.dram_tensor(k, shape, F32, kind="ExternalOutput").ap()
    build_program(nc, t)
    r = run_bass_kernel_spmd(nc, [arrays], core_ids=[0]).results[0]

    def rows(v):
        return v.transpose(2, 1, 0).reshape(v.shape[2], -1)
    y, lat, kpe = rows(r["o_y"]), rows(r["o_lat"]), r["o_kpe"].T
    ssmp = r["o_ssmp"].reshape(P, H, P).transpose(1, 0, 2)
    convp = r["o_convp"].transpose(2, 1, 0).reshape(1, 1, 3, -1)
    ssms = r["o_ssms"].reshape(2, P, 4, NSA, P).transpose(3, 0, 2, 1, 4).reshape(1, NSA, H, P, P)
    convs = r["o_convs"][:, :, 1:4, :].transpose(3, 2, 1, 0).reshape(1, NSA, 3, -1)
    c = np.ascontiguousarray
    return (c(y[None, :NPR]), c(y[NPR:, None]), c(lat[None, None, :NPR]), c(kpe[None, None, :NPR]), c(ssmp[None, None]),
            c(convp), c(lat[None, NPR:, None]), c(kpe[None, NPR:, None]), c(ssms), c(convs))
```

```python
from contextlib import ExitStack

import numpy as np
import concourse.bass as bass
from concourse import mybir

F32 = mybir.dt.float32
I32 = mybir.dt.int32
ALU = mybir.AluOpType
ACT = mybir.ActivationFunctionType
AX = mybir.AxisListType.X
AXY = mybir.AxisListType.XY

P = 128
D = 1024
KD = D // P
NPR = 256
NSA = 8
T = NPR + NSA
H = 8
CONVT = 3 * H
RING = 6
CH = 4096
PAGES = 8
NPHYS = 80
LORA = 4
ROPE = 64
SCALE = (128 + 64) ** -0.5
EPS = 1e-6
NEG = -1e30
NE = 32
SLOT = 64
NJ = 48
NJ1 = NJ + 1
LEVELS = 7

C_ID, C_ONE, C_U, C_STR, C_PERM = 0, 128, 256, 384, 512
C_LEV = 640
C_COS = C_LEV + LEVELS * P
C_SIN = C_COS + T
C_NEG = C_SIN + T
C_IOTA = C_NEG + 384
C_J = C_IOTA + SLOT
C_J64 = C_J + NJ1
C_E = C_J64 + NJ1
C_B8 = C_E + 1
C_EPS = C_B8 + 16
C_TWO = C_EPS + 1
C_OWN = C_TWO + P
NCONST = C_OWN + NSA

S_NMIX, S_NFFN, S_NFIN = 0, 8, 16
S_NQ, S_NKV, S_NGDN = 24, 28, 32
S_BADA = 33
S_ALOG = S_BADA + 64
S_DT = S_ALOG + 8
S_BR = S_DT + 8
S_CW = S_BR + NE
S_WSM = S_CW + CONVT * 4
WSM = 16 + ROPE + 32
S_CT = S_WSM + KD * WSM
NSMALL = S_CT + KD * 32

ADA, QKV, ADA2, SSM, ZZ, CQ, CKV, UQN, UQR, UK, UV, UKT = 0, 4, 10, 22, 24, 26, 27, 28, 29, 30, 31, 32
KV_AT = (UKT + 1, UKT + 7, UKT + 13, UKT + 19)
OG, GA, GB = KV_AT[0] + 4, KV_AT[1] + 4, KV_AT[2] + 4
UV2 = KV_AT[3] + 4
OM, WO = UV2 + 1, UV2 + 3
NCH = WO + 2
assert NCH % RING == 0


def ada_chunk(i):
    return ADA + i if i < 4 else ADA2 + i - 4


def kv_chunk(b, what):
    return KV_AT[2 * (b // 4) + what] + b % 4


KV_OF = {kv_chunk(b, what): (b, what) for b in range(NSA) for what in range(2)}


def build_program(nc, t):
    ctx = ExitStack()
    with ctx:
        def sb(name, shape, dt=F32):
            return ctx.enter_context(nc.sbuf_tensor(name, shape, dt))

        def sem(name):
            return ctx.enter_context(nc.semaphore(name))

        ring = [sb(f"ring{i}", [P, CH]) for i in range(RING)]
        con = sb("con_sb", [P, NCONST])
        small = sb("small_sb", [P, NSMALL])
        xT = sb("xT_sb", [P, KD, T])
        hT = sb("hT", [P, KD, T])
        mod = sb("mod", [P, 64, 9])
        regA = sb("regA", [P, CONVT * T])
        regB = sb("regB", [P, H, T])
        samp = regB[:, 0:3, :].rearrange("p a b -> p (a b)")[:, 0:CONVT * 32].rearrange("p (m j b) -> p m j b", m=CONVT, j=4)
        regC = sb("regC", [P, 10240])
        pages_sb = sb("pages_sb", [1, NSA * PAGES], I32)
        banks = ctx.enter_context(nc.psum_tensor("banks", [P, 8, 512], F32))
        bank = [banks[:, i, :] for i in range(8)]

        ident = con[:, C_ID:C_ID + P]
        ones = con[:, C_ONE:C_ONE + P]
        upto = con[:, C_U:C_U + P]
        before = con[:, C_STR:C_STR + P]
        perm = con[:, C_PERM:C_PERM + P]
        cosT = con[:, C_COS:C_COS + T]
        sinT = con[:, C_SIN:C_SIN + T]
        neg384 = con[:, C_NEG:C_NEG + 384]
        cT = small[:, S_CT:S_CT + KD * 32].rearrange("p (k c) -> p k c", k=KD)
        wsm = small[:, S_WSM:S_WSM + KD * WSM].rearrange("p (k c) -> p k c", k=KD)
        convw = small[:, S_CW:S_CW + CONVT * 4].rearrange("p (m j) -> p m j", j=4)

        qkvT = regA[:, :].rearrange("p (m t) -> p m t", t=T)
        oG = regB
        def cut(reg, at, *shape):
            n = 1
            for s in shape:
                n *= s
            v = reg[:, at:at + n]
            if len(shape) == 2:
                v = v.rearrange("p (a b) -> p a b", b=shape[1])
            if len(shape) == 3:
                v = v.rearrange("p (a b c) -> p a b c", b=shape[1], c=shape[2])
            return v
        upad = cut(regC, 0, 3, 3 + NPR)
        sigb = cut(regC, 800, 2, T)
        sqb = cut(regC, 1400, 2, T)
        rsb = cut(regC, 2900, 2, T)
        modA = cut(regC, 2300, KD, 9)
        convp = sb("convp", [P, CONVT, 3])
        smt = cut(regC, 2500, 2, CONVT, NSA)
        mrow = sb("mrow", [P, 2, P])
        bgm = sb("bgm", [NSA, H * NSA])
        egB = sb("egB", [P, H * NSA])
        beta_tok = sb("beta_tok", [P, 3, H])
        g_tok = sb("g_tok", [P, 3, H])
        G4 = 4 * P
        AT = cut(regC, 0, 2, G4)
        Xm = cut(regC, 1024, 2, G4)
        XTm = cut(regC, 2048, 2, G4)
        LTm = cut(regC, 3072, 2, G4)
        Aqk = cut(regC, 4096, 2, G4)
        qg = cut(regC, 5120, 2, G4)
        VB = cut(regC, 6144, 2, G4)
        KBG = cut(regC, 7168, 2, G4)
        K2 = cut(regC, 8192, 2, G4)
        Sst = cut(regC, 9216, 2, G4)
        gcol = sb("gcol", [P, 5, H])
        gsc = sb("gsc", [P, 3, 3, H])

        latT = cut(regC, 0, LORA, T)
        cqT = cut(regC, 1056, LORA, T)
        kpeT = cut(regC, 2112, T)
        vtok = cut(regC, 2376, 2, H * P)
        oM = cut(regC, 4424, H, T)
        mlat = 6536
        msc = [cut(regC, mlat + 384 * i, 384) for i in range(2)]
        mp = [cut(regC, mlat + 768 + 384 * i, 384) for i in range(2)]
        mpT = [cut(regC, mlat + 1536 + 384 * i, 384) for i in range(2)]
        msq = cut(regC, mlat, 2, T)
        mrs = cut(regC, mlat + 600, 2, T)
        mstat = cut(regC, mlat + 2304, 2, 8)
        rtmp = cut(regC, mlat, 2, T)
        qlatT = cut(regC, 2376, LORA * NSA * 32).rearrange("p (k b h) -> p k b h", k=LORA, b=NSA)
        olat = cut(regC, 3400, LORA * H * 32).rearrange("p (k h b) -> p k h b", k=LORA, h=H)
        qnS = cut(regC, mlat, H, 32)
        qpeS = cut(regC, mlat + 256, NSA, 32)
        qrow = cut(regC, mlat + 512, 2, 512)
        sstat = cut(regC, mlat + 1536, 2, 8)
        ps_ = [cut(regA, 2112 + 1032 * i, 1032) for i in range(2)]
        pT = cut(regA, 4176, PAGES, P)
        orow = cut(regC, 1056, 512)
        osr = cut(regC, 1568, 2 * P)
        pT9 = cut(regC, 1824, P)
        lat_tok = cut(regC, 8100, 512)
        qnT = cut(regA, 0, H, T)
        qpeT = cut(regA, 2112, 4, T)
        knT = cut(regA, 3168, H, NPR)
        peT = [cut((regA, regC)[i % 2], (5240, 9000)[i % 2], 1024)[ROPE * (i // 2):ROPE * (i // 2 + 1), :] for i in range(4)]
        yA = cut(regA, 0, KD, T)
        gB = regB
        gsig = cut(regC, mlat + 512, 2, T)
        h2tok = cut(regC, 0, 3, KD, P)
        acc = regB
        yout = cut(regC, 0, KD, T)
        a0 = 0
        lg = cut(regA, 0, 3, NE)
        ex = cut(regA, 96, 3, NE)
        sel = cut(regA, 192, 3, NE)
        eqm = cut(regA, 288, 3, NE)
        pre = [cut(regA, 384 + 144 * i, 3, 48) for i in range(2)]
        v8 = cut(regA, 672, 3, 8)
        rst = cut(regA, 700, 4, 3)
        gate = cut(regA, 712, 3, NE)
        maskT = cut(regA, 808, T)
        gateT = cut(regA, 1072, T)
        m1T = cut(regA, 1336, T)
        cntc = cut(regA, 1600, 8)
        e1h = cut(regA, 1608, NJ1)
        ge1 = cut(regA, 1657, NJ1)
        rr = cut(regA, 1706, 3, NJ1)
        gg = cut(regA, 1853, 3, NJ1)
        self_ = cut(regA, 2000, 3, SLOT)
        selg = cut(regA, 2192, 3, 2, SLOT)
        selT = cut(regA, 2576, T)
        gtok = cut(regA, 2840, 512)
        hg = cut(regA, 3352, 4, P)
        gmn = cut(regA, 3864, 512)
        upc = cut(regA, 4376, 512)
        sgm = cut(regA, 4888, 512)
        act_ = cut(regA, 5400, 512)
        actT = cut(regC, 7000, 4, P)
        ytok = cut(regC, 7512, 512)
        brow = cut(regC, 8100, 3 * 512)
        items = sb("items", [1, 64], I32)
        msq2 = cut(regC, 4000, KD, T)
        mrs2 = cut(regC, 6200, T)

        x32 = cut(regC, 0, CONVT, 32)
        krow = cut(regC, 4724, 4, 2, P)
        ksr = cut(regC, 1024, 2, P)
        vnr = cut(regC, 1280, 2, P)
        betac = cut(regC, 1536, 2)
        vnm = cut(regC, 1600, 2, NSA * P)
        stmp = cut(regC, 3700, NSA * P)
        zsig = cut(regC, 7300, 2, T)

        rot = cut(regC, 8000, T)
        cumc = sb("cumc", [P, 2, 16])
        modA2 = cut(regC, 6500, KD, 9)

        inputs_in = sem("inputs_in")
        slot_in = [sem(f"slot_in{i}") for i in range(RING)]
        dve_line = sem("dve_line")
        act_line = sem("act_line")
        root_ready = sem("root_ready")
        sq_ready = sem("sq_ready")
        ss_ready = sem("ss_ready")
        mod_ready = sem("mod_ready")
        mod_evac = sem("mod_evac")
        mod_row = sem("mod_row")
        mod_turned = sem("mod_turned")
        h_ready = sem("h_ready")
        proj_ready = sem("proj_ready")
        proj_evac = sem("proj_evac")
        ab_ready = sem("ab_ready")
        conv_done = sem("conv_done")
        sig_done = sem("sig_done")
        silu_done = sem("silu_done")
        l2sq = sem("l2sq")
        l2ss = sem("l2ss")
        l2done = sem("l2done")
        ab_act = sem("ab_act")
        bg_done = sem("bg_done")
        tr_ready = sem("tr_ready")
        tr_evac = sem("tr_evac")
        stored = sem("stored")

        names = {}

        def stage(name):
            if name not in names:
                names[name] = sem(name)
            return names[name]

        once_steps = {
            "pe_steps": ("cum_ready", "oss_turned", "kpe_ready", "kpe_turned", "qlat_ready", "ltok_ready", "os_ready", "os_turned", "logits"),
            "act_steps": ("x32_ready", "krow_copied", "kpe_copied", "qns_ready", "osr_copied", "os_copied"),
            "dve_steps": ("upad_zero", "cum_read", "kpe_rot", "v8_ready", "e1h_ready", "m1_ready", "items_ready", "x2_ready"),
            "pool_steps": ("x32_zero", "att_zero"),
        }

        def once(name):
            for line, steps in once_steps.items():
                if name in steps:
                    return stage(line), steps.index(name) + 1

        block = ctx.enter_context(nc.Block())

        used = {}
        for i in range(16):
            used[ada_chunk(i)] = (mod_ready, i + 1)
        for i in range(6):
            used[QKV + i] = (proj_ready, 4 * (i + 1))
        for i in range(2):
            used[SSM + i] = (stage(f"ssm_stored{i}"), 16)
        for i in range(2):
            used[ZZ + i] = (stage("z_ready"), 4 * (i + 1))
        used[CQ] = (stage("lat_ready"), 4)
        used[CKV] = (stage("lat_ready"), 8)
        used[UQN] = (stage("q_ready"), 8)
        used[UQR] = (stage("q_ready"), 12)
        used[UK] = (stage("kn_ready"), 8)
        used[UV] = (stage("vt_ready"), 4)
        used[UKT] = once("qlat_ready")
        for b in range(NSA):
            used[kv_chunk(b, 0)] = (stage("st_ready"), b // 4 + 1)
            used[kv_chunk(b, 1)] = (stage("ol_ready"), b // 4 + 1)
        used[UV2] = once("os_ready")
        for i in range(2):
            used[OG + i] = (stage("out_ready"), 4 * (i + 1))
            used[GA + i] = (stage("out_ready"), 8 + 4 * (i + 1))
            used[GB + i] = (stage("out_ready"), 16 + 4 * (i + 1))
            used[OM + i] = (stage("out_ready"), 24 + 4 * (i + 1))
            used[WO + i] = (stage("out_ready"), 32 + 4 * (i + 1))
        arrive = {}
        count = [0] * RING
        for n in range(NCH):
            count[n % RING] += 16 * (PAGES if n in KV_OF else 1)
            arrive[n] = count[n % RING]
        moe_base = list(count)

        def weights(pe, n):
            pe.wait_ge(slot_in[n % RING], arrive[n])
            return ring[n % RING][:, :].rearrange("p (k c) -> p k c", c=512)

        pe_mm = nc.tensor.matmul

        def chunk_k(n, m, k):
            return ring[n % RING][:, k * 512 + m * P:k * 512 + (m + 1) * P]

        moe_read = sem("moe_read")
        gu_ready = sem("gu_ready")
        sel_new = sem("sel_new")
        selg_new = sem("selg_new")
        gathered = sem("gathered")
        gtok_copied = sem("gtok_copied")
        g_turned = sem("g_turned")
        hg_ready = sem("hg_ready")
        selT_turned = sem("selT_turned")
        selT_copied = sem("selT_copied")
        gmin_ready = sem("gmin_ready")
        sig_ready = sem("sig_ready")
        act_ready = sem("act_ready")
        a_turned = sem("a_turned")
        actT_ready = sem("actT_ready")
        ytok_copied = sem("ytok_copied")
        scattered = sem("scattered")
        acc_added = sem("acc_added")
        moe_line = sem("moe_line")
        brow_in = sem("brow_in")
        wgu = t["w_gu"].rearrange("e (p k) n -> e p (k n)", p=P)
        wdn = t["w_dn"].rearrange("e (m p) n -> e p m n", p=P)
        tok_tiles = ((0, P), (1, P), (2, NSA))
        HALF = D // 2
        both = con[0:2, C_TWO:C_TWO + P]

        def number_of_items(eng):
            eng.wait_ge(*once("items_ready"))
            return eng.value_load(items[0:1, 0:1], min_val=1, max_val=NJ)

        def moe_loads(sp):
            K = number_of_items(sp)

            def load(c, e):
                if c < 4:
                    src = wgu[bass.ds(e, 1), :, CH * c:CH * (c + 1)].rearrange("a p n -> p (a n)")
                    sp.dma_start(ring[c][:, :], src).then_inc(slot_in[c], 16)
                else:
                    src = wdn[bass.ds(e, 1), :, 4 * (c - 4):4 * (c - 3), :].rearrange("a p m n -> p (a m) n")
                    sp.dma_start(ring[c][:, :].rearrange("p (m n) -> p m n", m=4), src).then_inc(slot_in[c], 16)

            def load_bias(e):
                sp.dma_start(brow[0:2, :], t["biases"][bass.ds(e, 1), :, :].rearrange("a h n -> h (a n)")).then_inc(brow_in, 16)

            e0 = sp.value_load(items[0:1, 1:2], min_val=0, max_val=NE - 1)
            for c in range(RING):
                sp.wait_ge(*used[NCH - RING + c])
                load(c, e0)
            load_bias(e0)
            with sp.Fori(1, NJ) as j:
                with sp.If(j < K):
                    e = sp.value_load(items[0:1, bass.ds(j + 1, 1)], min_val=0, max_val=NE - 1)
                    for c in range(RING):
                        sp.wait_ge(moe_read, j * 6 + (c - 5))
                        load(c, e)
                    load_bias(e)

        def moe_tensor(pe):
            K = number_of_items(pe)

            def gather(n):
                pe.wait_ge(sel_new, n)
                for i, r in tok_tiles:
                    for y in range(2):
                        mm = pe_mm(bank[2][SLOT * y:SLOT * (y + 1), :], lhsT=self_[0:r, i, :],
                                   rhs=h2tok[0:r, i, 4 * y:4 * y + 4, :].rearrange("p k c -> p (k c)"),
                                   start=(i == 0), stop=(i == 2), skip_group_check=True)
                mm.then_inc(gathered, 1)

            def turn_gathered(n):
                pe.wait_ge(gtok_copied, n)
                for q in range(4):
                    mm = pe_mm(bank[3][:, P * q:P * (q + 1)], lhsT=gtok[:, P * q:P * (q + 1)], rhs=ident, start=True, stop=True)
                mm.then_inc(g_turned, 1)

            def scatter(j):
                pe.wait_ge(ytok_copied, j + 1)
                pe.wait_ge(selT_copied, j + 1)
                for q in range(4):
                    b = (6, 2)[q % 2]
                    if q >= 2:
                        pe.wait_ge(acc_added, j * 4 + q)
                    for y in range(2):
                        r = slice(SLOT * y, SLOT * (y + 1))
                        mm = pe_mm(bank[b + y][:, 0:T], lhsT=ytok[r, P * q:P * (q + 1)], rhs=selT[r, :], start=True, stop=True)
                    mm.then_inc(scattered, 1)

            pe.wait_ge(stage("rg_copied"), 1)
            gather(1)
            turn_gathered(1)
            with pe.Fori(0, NJ) as j:
                with pe.If(j < K):
                    pe.wait_ge(hg_ready, j + 1)
                    for c in range(4):
                        pe.wait_ge(slot_in[c], j * 16 + (moe_base[c] + 16))
                        for kk in range(2):
                            k = 2 * c + kk
                            for x in range(4):
                                mm = pe_mm(bank[x // 2][SLOT * (x % 2):SLOT * (x % 2 + 1), :],
                                           lhsT=hg[:, k % 4, SLOT * (k // 4):SLOT * (k // 4 + 1)],
                                           rhs=ring[c][:, 2048 * kk + HALF * x:2048 * kk + HALF * (x + 1)],
                                           start=(k == 0), stop=False, skip_group_check=True)
                        mm.then_inc(moe_read, 1)
                        if c == 0:
                            scatter(j)
                            pe.wait_ge(selg_new, j + 1)
                            for i, r in tok_tiles:
                                mm = pe_mm(bank[4][:, P * i:P * i + r], lhsT=selg[0:r, i, :, :].rearrange("p a s -> p (a s)"),
                                           rhs=ident[0:r, 0:r], start=True, stop=True)
                            mm.then_inc(selT_turned, 1)
                    pe.wait_ge(brow_in, j * 16 + 16)
                    for x in range(2):
                        mm = pe_mm(bank[x][:, :], lhsT=both, rhs=brow[0:2, HALF * x:HALF * (x + 1)], start=False, stop=True, skip_group_check=True)
                    mm.then_inc(gu_ready, 1)
                    pe.wait_ge(acc_added, j * 4 + 5)
                    gather(j + 2)
                    turn_gathered(j + 2)
                    pe.wait_ge(selT_copied, j + 2)
                    pe.wait_ge(act_ready, j + 1)
                    for q in range(4):
                        if q == 2:
                            pe.wait_ge(hg_ready, j + 2)
                        mm = pe_mm(bank[4 - q // 2][:, P * q:P * (q + 1)], lhsT=act_[:, P * q:P * (q + 1)], rhs=ident, start=True, stop=True)
                        if q % 2 == 1:
                            mm.then_inc(a_turned, 1)
                    for m in range(8):
                        c = 4 + m // 4
                        if m % 4 == 0:
                            pe.wait_ge(slot_in[c], j * 16 + (moe_base[c] + 16))
                        if m == 0:
                            pe.wait_ge(actT_ready, j * 2 + 1)
                        if m == 2:
                            pe.wait_ge(actT_ready, j * 2 + 2)
                        for y in range(2):
                            mm = pe_mm(bank[5][SLOT * y:SLOT * (y + 1), :], lhsT=actT[:, m % 4, SLOT * (m // 4):SLOT * (m // 4 + 1)],
                                       rhs=ring[c][:, D * (m % 4) + HALF * y:D * (m % 4) + HALF * (y + 1)],
                                       start=(m == 0), stop=False, skip_group_check=True)
                        if m == 3:
                            mm.then_inc(moe_read, 1)
                    pe_mm(bank[5][:, :], lhsT=both, rhs=brow[0:2, 2 * HALF:3 * HALF], start=False, stop=True, skip_group_check=True).then_inc(moe_read, 1)
            scatter(K)

        def moe_scalar(act):
            A = nc.scalar.activation
            K = number_of_items(act)
            act.wait_ge(gathered, 1)
            A(gtok[:, :], bank[2][:, :], ACT.Copy).then_inc(gtok_copied, 1)
            act.wait_ge(g_turned, 1)
            A(hg[:, :, :], bank[3][:, :].rearrange("p (q s) -> p q s", q=4), ACT.Copy).then_inc(hg_ready, 1)
            with act.Fori(0, NJ) as j:
                with act.If(j < K):
                    act.wait_ge(selT_turned, j + 1)
                    A(selT[:, :], bank[4][:, 0:T], ACT.Copy).then_inc(selT_copied, 1)
                    act.wait_ge(gmin_ready, j + 1)
                    A(sgm[:, :], gmn[:, :], ACT.Sigmoid, scale=1.702).then_inc(sig_ready, 1)
                    act.wait_ge(gathered, j + 2)
                    A(gtok[:, :], bank[2][:, :], ACT.Copy).then_inc(gtok_copied, 1)
                    act.wait_ge(g_turned, j + 2)
                    A(hg[:, :, :], bank[3][:, :].rearrange("p (q s) -> p q s", q=4), ACT.Copy).then_inc(hg_ready, 1)
                    for y in range(2):
                        act.wait_ge(a_turned, j * 2 + (y + 1))
                        A(actT[:, 2 * y:2 * y + 2, :], bank[4 - y][:, 256 * y:256 * (y + 1)].rearrange("p (q s) -> p q s", q=2),
                          ACT.Copy).then_inc(actT_ready, 1)
                    act.wait_ge(moe_read, j * 6 + 6)
                    A(ytok[:, :], bank[5][:, :], ACT.Copy).then_inc(ytok_copied, 1)

        LINKS = 2

        def moe_vector(dve, link):
            V = nc.vector
            K = number_of_items(dve)
            iota = con[:, C_IOTA:C_IOTA + SLOT]
            dve.wait_ge(acc_added, 1)
            V.memset(selT[:, :], 0.0).then_inc(selT_copied, 1)
            V.memset(ytok[:, :], 0.0).then_inc(ytok_copied, 1)

            def choose(col):
                for i, r in tok_tiles:
                    ins = V.tensor_scalar(self_[0:r, i, :], iota[0:r, :], rr[0:r, i, col], None, ALU.is_equal)
                return ins

            def add(j):
                for q in range(4):
                    b = (6, 2)[q % 2]
                    dve.wait_ge(scattered, j * 4 + (q + 1))
                    pair = acc[:, q::4, :]
                    V.tensor_tensor(pair, pair, banks[:, b:b + 2, 0:T], ALU.add).then_inc(acc_added, 1)

            choose(slice(0, 1)).then_inc(sel_new, 1)
            with dve.Fori(0, NJ) as j:
                with dve.If(j < K):
                    n = [0]

                    def after(ins):
                        n[0] += 1
                        ins.then_inc(moe_line, 1)
                        dve.wait_ge(moe_line, j * LINKS + n[0])

                    dve.wait_ge(gathered, j + 1)
                    choose(bass.ds(j + 1, 1)).then_inc(sel_new, 1)
                    for i, r in tok_tiles:
                        ins = V.tensor_scalar(selg[0:r, i, :, :], iota[0:r, :].unsqueeze(1).to_broadcast([r, 2, SLOT]),
                                              rr[0:r, i, bass.ds(j, 1)], gg[0:r, i, bass.ds(j, 1)], ALU.is_equal, ALU.mult)
                    ins.then_inc(selg_new, 1)
                    add(j)
                    dve.wait_ge(gu_ready, j + 1)
                    V.tensor_scalar(gmn[:, :], bank[0][:, :], 7.0, None, ALU.min).then_inc(gmin_ready, 1)
                    after(V.tensor_scalar(upc[:, :], bank[1][:, :], 7.0, -7.0, ALU.min, ALU.max))
                    after(V.scalar_tensor_tensor(upc[:, :], upc[:, :], 1.0, gmn[:, :], ALU.add, ALU.mult))
                    dve.wait_ge(sig_ready, j + 1)
                    V.tensor_tensor(act_[:, :], upc[:, :], sgm[:, :], ALU.mult).then_inc(act_ready, 1)
                    assert n[0] == LINKS
            add(K)
            dve.wait_ge(acc_added, K * 4 + 5)

        ssm_view = [ring[(SSM + i) % RING][:, :].rearrange("p (h b v) -> p h b v", h=4, b=NSA) for i in range(2)]

        @block.sync
        def _(sp):
            sp.dma_start(small[:, :], t["small"]).then_inc(inputs_in, 16)
            sp.dma_start(xT[:, :, :], t["xT"]).then_inc(inputs_in, 16)
            sp.dma_start(con[:, :], t["con"]).then_inc(inputs_in, 16)
            sp.dma_start(samp[:, :, :, :], t["convT"]).then_inc(inputs_in, 16)
            sp.dma_start(pages_sb[:, :], t["pages"]).then_inc(stage("pages_in"), 16)
            for n in range(NCH):
                if n >= RING:
                    sp.wait_ge(*used[n - RING])
                dst = ring[n % RING]
                if n in KV_OF:
                    b, what = KV_OF[n]
                    if n == KV_AT[0]:
                        sp.wait_ge(stage("pages_in"), 16)
                    src = t["kvT"] if what == 0 else t["kv"]
                    if what == 0:
                        if b >= 4:
                            sp.wait_ge(stage("pe_used"), b - 3)
                        elif b == 0:
                            sp.wait_ge(stage("oss_ready"), 2)
                            sp.wait_ge(stage("ssmp_stored"), 16)
                    with sp.Fori(0, PAGES) as pg:
                        phys = sp.value_load(pages_sb[0:1, bass.ds(pg + b * PAGES, 1)], min_val=0, max_val=NPHYS - 1)
                        sp.dma_start(dst[:, bass.ds(pg * 512, 512)],
                                     src[bass.ds(phys, 1), :, :].rearrange("a p c -> p (a c)")
                                     ).then_inc(slot_in[n % RING], 16)
                        if what == 0:
                            sp.dma_start(peT[b % 4][:, bass.ds(pg * P, P)],
                                         t["peT"][bass.ds(phys, 1), :, :].rearrange("a p c -> p (a c)")
                                         ).then_inc(stage(f"pe_in{b % 4}"), 16)
                elif n == UQR:
                    sp.dma_start(dst[:, 0:2048], t["wpre"][wp_index(n), :, 0:2048]).then_inc(slot_in[n % RING], 16)
                elif SSM <= n < SSM + 2:
                    sp.dma_start(dst[:, :], t["ssm"][n - SSM, :, :]).then_inc(slot_in[n % RING], 16)
                else:
                    sp.dma_start(dst[:, :], t["wpre"][wp_index(n), :, :]).then_inc(slot_in[n % RING], 16)
            moe_loads(sp)

        @block.tensor
        def _(pe):
            def sum_squares(out, sq, k):
                for i in range(k):
                    mm = pe_mm(out, lhsT=ones, rhs=sq(i), start=(i == 0), stop=(i == k - 1))
                return mm

            pe.wait_ge(inputs_in, 64)
            pe.wait_ge(sq_ready, 1)
            sum_squares(bank[4][:, 0:T], lambda k: hT[:, k, :], KD).then_inc(ss_ready, 1)
            def modulate(i, b):
                n = ada_chunk(i)
                weights(pe, n)
                for k in range(KD):
                    for q in range(4):
                        mm = pe_mm(bank[b][32 * q:32 * q + 32, 0:P], lhsT=cT[:, k, :], rhs=chunk_k(n, q, k),
                                   start=(k == 0), stop=(k == KD - 1))
                mm.then_inc(mod_ready, 1)

            def turn_mod(i, b):
                pe.wait_ge(mod_row, i + 1)
                pe_mm(bank[b][:, 0:P], lhsT=mrow[:, i % 2, :], rhs=ident, start=True, stop=True).then_inc(mod_turned, 1)

            for i in range(5):
                if i < 4:
                    if i >= 2:
                        pe.wait_ge(mod_row, i - 1)
                    modulate(i, i % 2)
                if i >= 1:
                    if i >= 3:
                        pe.wait_ge(mod_evac, i - 2)
                    turn_mod(i - 1, 2 + (i - 1) % 2)
            pe.wait_ge(h_ready, 1)
            for i, (a, b) in enumerate(((0, P), (P, NPR), (NPR, T))):
                for k in range(KD):
                    mm = pe_mm(bank[6][0:b - a, 16 * i:16 * i + 16], lhsT=hT[:, k, a:b], rhs=wsm[:, k, 0:16],
                               start=(k == 0), stop=(k == KD - 1))
            mm.then_inc(ab_ready, 1)
            for m in range(CONVT):
                n = QKV + m // 4
                weights(pe, n)
                if m >= 4:
                    pe.wait_ge(proj_evac, m - 3)
                for k in range(KD):
                    mm = pe_mm(bank[m % 4][:, 0:T], lhsT=chunk_k(n, m % 4, k), rhs=hT[:, k, :],
                               start=(k == 0), stop=(k == KD - 1))
                mm.then_inc(proj_ready, 1)
            for i in range(2 * H):
                pe.wait_ge(l2sq, i + 1)
                if i >= 2:
                    pe.wait_ge(l2done, i - 1)
                pe_mm(bank[4 + i % 2][:, 0:T], lhsT=ones, rhs=sqb[:, i % 2, :], start=True, stop=True).then_inc(l2ss, 1)
            pe.wait_ge(bg_done, 1)
            for c in range(2):
                pe_mm(bank[6][:, 64 + 16 * c:72 + 16 * c], lhsT=upto, rhs=g_tok[:, c, :], start=True, stop=True)
                pe_mm(bank[6][:, 72 + 16 * c:80 + 16 * c], lhsT=ones, rhs=g_tok[:, c, :], start=True, stop=True)
            pe.wait_ge(stage("bgm_ready"), 1)
            mm = pe_mm(bank[6][:, 96:160], lhsT=ones[0:NSA, :], rhs=bgm[0:NSA, :], start=True, stop=True)
            mm.then_inc(once("cum_ready")[0], 1)
            pe.wait_ge(l2done, 2 * H)
            for c in range(2):
                tok = slice(c * P, (c + 1) * P)
                for g in range(2):
                    for w in range(2):
                        bk = bank[2 * w + g]
                        if g == 0 and w == 0 and c == 1:
                            pe.wait_ge(stage("gd_out"), 2)
                        for i in range(4):
                            mm = pe_mm(bk[:, i * P:(i + 1) * P],
                                       lhsT=qkvT[:, H * (1 + w) + 4 * g + i, tok], rhs=ident,
                                       start=True, stop=True)
                        mm.then_inc(tr_ready, 1)
                for g in range(2):
                    b0 = 4 - 4 * g
                    if g == 1:
                        pe.wait_ge(tr_evac, 4 * (c + 1))
                    for i in range(4):
                        h = 4 * g + i
                        pe_mm(bank[b0][:, i * P:(i + 1) * P], lhsT=g_tok[:, c, h:h + 1].to_broadcast([P, P]), rhs=upto, start=True, stop=True)
                    for i in range(4):
                        h = 4 * g + i
                        pe_mm(bank[b0 + 1][:, i * P:(i + 1) * P], lhsT=beta_tok[:, c, h:h + 1].to_broadcast([P, P]), rhs=ident, start=True, stop=True)
                    if g == 0 and c == 0:
                        pe.wait_ge(*once("cum_read"))
                        pe.wait_ge(stage("egB_ready"), 1)
                    for i in range(4):
                        h = 4 * g + i
                        pe_mm(bank[b0 + 2][:, i * P:(i + 1) * P], lhsT=qkvT[:, H + h, tok], rhs=qkvT[:, H + h, tok], start=True, stop=True)
                    for i in range(4):
                        h = 4 * g + i
                        mm = pe_mm(bank[b0 + 3][:, i * P:(i + 1) * P], lhsT=qkvT[:, H + h, tok], rhs=qkvT[:, h, tok], start=True, stop=True)
                    mm.then_inc(stage("gd_prod"), 1)
                for lv in range(LEVELS):
                    for g in range(2):
                        q = (c * LEVELS + lv) * 2 + g + 1
                        pe.wait_ge(stage("lt_done"), q)
                        if lv == 0:
                            pe.wait_ge(stage("prep_done"), 2 * c + 2)
                        for i in range(4):
                            s = slice(i * P, (i + 1) * P)
                            mm = pe_mm(bank[g][:, s], lhsT=LTm[:, g, s], rhs=Xm[:, g, s], start=True, stop=True)
                        mm.then_inc(stage("lx_done"), 1)
                    chunk = 4 + c * LEVELS + lv
                    if chunk < 16:
                        pe.wait_ge(mod_row, chunk)
                        modulate(chunk, 6)
                    for g in range(2):
                        q = (c * LEVELS + lv) * 2 + g + 1
                        pe.wait_ge(stage("lx_copied"), q)
                        for i in range(4):
                            s = slice(i * P, (i + 1) * P)
                            pe_mm(bank[2 + g][:, s], lhsT=XTm[:, g, s], rhs=LTm[:, g, s], start=True, stop=True)
                        for i in range(4):
                            s = slice(i * P, (i + 1) * P)
                            mm = pe_mm(bank[4 + g][:, s], lhsT=LTm[:, g, s], rhs=XTm[:, g, s], start=True, stop=True)
                        mm.then_inc(stage("xlx_done"), 1)
                    if chunk < 16:
                        pe.wait_ge(mod_evac, chunk)
                        turn_mod(chunk, 7)
                for g in range(2):
                    pe.wait_ge(stage("x_done"), (c + 1) * 2 * LEVELS if g == 1 else (c + 1) * 2 * LEVELS - 1)
                    for i in range(4):
                        s = slice(i * P, (i + 1) * P)
                        mm = pe_mm(bank[g][:, s], lhsT=XTm[:, g, s], rhs=VB[:, g, s], start=True, stop=True)
                    if c == 1:
                        for i in range(4):
                            s = slice(i * P, (i + 1) * P)
                            mm = pe_mm(bank[2 + g][:, s], lhsT=KBG[:, g, s], rhs=XTm[:, g, s], start=True, stop=True)
                    mm.then_inc(stage("uw_done"), 1)
                if c == 1:
                    for g in range(2):
                        pe.wait_ge(stage("wt_copied"), g + 1)
                        for i in range(4):
                            s = slice(i * P, (i + 1) * P)
                            mm = pe_mm(bank[4 + g][:, s], lhsT=Xm[:, g, s], rhs=Sst[:, g, s], start=True, stop=True)
                        mm.then_inc(stage("ws_done"), 1)
                pe.wait_ge(mod_evac, min(4 + (c + 1) * LEVELS, 16))
                for g in range(2):
                    pe.wait_ge(stage("vn_done"), 2 * c + g + 1)
                    for i in range(4):
                        s = slice(i * P, (i + 1) * P)
                        mm = pe_mm(bank[6 + g][:, s], lhsT=VB[:, g, s], rhs=Aqk[:, g, s], start=True, stop=(c == 0))
                        if c == 1:
                            mm = pe_mm(bank[6 + g][:, s], lhsT=Sst[:, g, s], rhs=qg[:, g, s], start=False, stop=True)
                    for i in range(4):
                        s = slice(i * P, (i + 1) * P)
                        mm = pe_mm(bank[2 + g][:, s], lhsT=K2[:, g, s], rhs=VB[:, g, s], start=True, stop=True)
                    mm.then_inc(stage("os_done"), 1)
            pe.wait_ge(stage("gd_out"), 4)
            pe.wait_ge(*once("x32_ready"))

            def state_product(w, g, base):
                for y in range(2):
                    for j in range(4):
                        mm = pe_mm(bank[base + y][32 * j:32 * j + 32, :], lhsT=x32[:, w * H + 4 * g + j, :],
                                   rhs=ssm_view[g][:, j, 4 * y:4 * y + 4, :].rearrange("p b v -> p (b v)"), start=True, stop=True)
                return mm

            for g in range(2):
                pe.wait_ge(stage("decayed"), g + 1)
                state_product(1, g, 2 * g).then_inc(stage("sample_products"), 1)
            for w in range(2):
                for g in range(2):
                    for j in range(4):
                        mm = pe_mm(bank[4 + w][32 * j:32 * j + 32, P * g:P * (g + 1)], lhsT=x32[:, (2 - w) * H + 4 * g + j, :],
                                   rhs=ident, start=True, stop=True)
            for j in range(4):
                mm = pe_mm(bank[6][32 * j:32 * j + 32, 0:2], lhsT=ident[0:NSA, 0:32], rhs=beta_tok[0:NSA, 2, j::4], start=True, stop=True)
            mm.then_inc(stage("sample_products"), 1)
            pe.wait_ge(*once("krow_copied"))
            for g in range(2):
                for y in range(2):
                    u = 2 * g + y
                    if u < 2:
                        pe.wait_ge(stage("vnm_ready"), u + 1)
                    else:
                        pe.wait_ge(stage("snew"), u - 1)
                    for j in range(4):
                        mm = pe_mm(bank[4 * y + j][:, :], lhsT=krow[:, j, g, :], rhs=vnm[:, g, 512 * y:512 * y + 512], start=True, stop=True)
                    mm.then_inc(stage("outer"), 1)
            pe.wait_ge(stage("snew"), 4)
            for g in range(2):
                mm = state_product(0, g, 2 * g)
                mm.then_inc(stage("oss_ready"), 1)
            for g in range(2):
                pe.wait_ge(stage("oss_row"), g + 1)
                mm = pe_mm(bank[4][:, P * g:P * (g + 1)], lhsT=ksr[:, g, :], rhs=ident, start=True, stop=True)
            mm.then_inc(once("oss_turned")[0], 1)
            for h in range(H):
                pe.wait_ge(stage("on_sq"), h + 1)
                if h >= 2:
                    pe.wait_ge(stage("on_rs"), h - 1)
                pe_mm(bank[h % 2][:, 0:T], lhsT=ones, rhs=msq[:, h % 2, :], start=True, stop=True).then_inc(stage("on_ss"), 1)
            pe.wait_ge(stage("on_rs"), H)
            for m in range(H):
                n = ZZ + m // 4
                weights(pe, n)
                if m >= 4:
                    pe.wait_ge(stage("z_evac"), m - 3)
                for k in range(KD):
                    mm = pe_mm(bank[m % 4][:, 0:T], lhsT=chunk_k(n, m % 4, k), rhs=hT[:, k, :], start=(k == 0), stop=(k == KD - 1))
                mm.then_inc(stage("z_ready"), 1)
            for m in range(8):
                n = CQ + m // 4
                weights(pe, n)
                if m >= 4:
                    pe.wait_ge(stage("lat_evac"), m - 3)
                for k in range(KD):
                    mm = pe_mm(bank[4 + m % 4][:, 0:T], lhsT=chunk_k(n, m % 4, k), rhs=hT[:, k, :], start=(k == 0), stop=(k == KD - 1))
                mm.then_inc(stage("lat_ready"), 1)
            pe.wait_ge(stage("z_evac"), H)
            for k in range(KD):
                for half in (slice(0, ROPE), slice(ROPE, P)):
                    mm = pe_mm(bank[0][half, 0:T], lhsT=wsm[:, k, 16:16 + ROPE], rhs=hT[:, k, :], start=(k == 0), stop=(k == KD - 1), skip_group_check=True)
            mm.then_inc(once("kpe_ready")[0], 1)
            pe.wait_ge(*once("kpe_copied"))
            pe_mm(bank[1][:, 0:T], lhsT=perm, rhs=kpeT[:, :], start=True, stop=True).then_inc(once("kpe_turned")[0], 1)
            for w in range(2):
                for i in range(LORA):
                    pe.wait_ge(stage("lsq"), LORA * w + i + 1)
                    mm = pe_mm(bank[2 + w][:, 0:T], lhsT=ones, rhs=msq[:, i % 2, :], start=(i == 0), stop=(i == LORA - 1))
                    mm.then_inc(stage("lss"), 1)
            pe.wait_ge(stage("lat_normed"), 1)
            pe.wait_ge(stage("lat_evac"), 8)
            for m in range(12):
                n = UQN if m < 8 else UQR
                pe.wait_ge(slot_in[n % RING], arrive[n])
                if m >= 4:
                    pe.wait_ge(stage("q_evac"), m - 3)
                W = 1024 if m < 8 else 512
                c0 = (m if m < 8 else m - 8) * P
                for k in range(LORA):
                    mm = pe_mm(bank[4 + m % 4][:, 0:T], lhsT=ring[n % RING][:, k * W + c0:k * W + c0 + P], rhs=cqT[:, k, :],
                               start=(k == 0), stop=(k == LORA - 1))
                mm.then_inc(stage("q_ready"), 1)
            for i in range(4):
                pe.wait_ge(stage("q_evac"), 9 + i)
                if i >= 2:
                    pe.wait_ge(stage("q_turned"), i - 1)
                pe_mm(bank[i % 2][:, 0:T], lhsT=perm, rhs=qpeT[:, i, :], start=True, stop=True).then_inc(stage("q_turn"), 1)
            pe.wait_ge(stage("lat_normed"), 2)
            pe.wait_ge(slot_in[UK % RING], arrive[UK])
            wk = ring[UK % RING][:, :].rearrange("p (c h n) -> p c h n", c=LORA, h=H)
            for h in range(H):
                pe.wait_ge(stage("kn_evac"), h - 3) if h >= 4 else pe.wait_ge(stage("q_evac"), 12)
                for k in range(LORA):
                    mm = pe_mm(bank[4 + h % 4][:, 0:NPR], lhsT=wk[:, k, h, :], rhs=latT[:, k, 0:NPR], start=(k == 0), stop=(k == LORA - 1))
                mm.then_inc(stage("kn_ready"), 1)
            pe.wait_ge(slot_in[UV % RING], arrive[UV])
            wv = ring[UV % RING][:, :].rearrange("p (c n) -> p c n", c=LORA)
            pe.wait_ge(stage("q_turned"), 4)
            for i in range(4):
                c, y = i // 2, i % 2
                for k in range(LORA):
                    mm = pe_mm(bank[i][:, :], lhsT=latT[:, k, c * P:(c + 1) * P], rhs=wv[:, k, 512 * y:512 * y + 512], start=(k == 0), stop=(k == LORA - 1))
                mm.then_inc(stage("vt_ready"), 1)
            pe.wait_ge(stage("kn_evac"), 8)
            pe.wait_ge(stage("vt_evac"), 4)
            for h in range(H + 1):
                if h < H:
                    s = bank[h % 2]
                    half = slice(64 * (h % 2), 64 * (h % 2) + 64)
                    if h >= 2:
                        pe.wait_ge(stage("pa_masked"), h - 1)
                    pe_mm(s[:, 0:P], lhsT=qnT[:, h, 0:P], rhs=knT[:, h, 0:P], start=True, stop=False)
                    pe_mm(s[:, 0:P], lhsT=qpeT[half, h // 2, 0:P], rhs=kpeT[half, 0:P], start=False, stop=True)
                    pe_mm(s[:, P:384], lhsT=qnT[:, h, P:NPR], rhs=knT[:, h, :], start=True, stop=False)
                    pe_mm(s[:, P:384], lhsT=qpeT[half, h // 2, P:NPR], rhs=kpeT[half, 0:NPR], start=False, stop=True).then_inc(stage("pa_scores"), 1)
                if h >= 1:
                    j = h - 1
                    pe.wait_ge(stage("pa_probs"), j + 1)
                    if j >= 2:
                        pe.wait_ge(stage("pa_pcopied"), j - 1)
                    w = bank[2 + j % 2]
                    pe.transpose(w[:, 0:P], mp[j % 2][:, 0:P], ident)
                    pe.transpose(w[:, P:256], mp[j % 2][:, P:256], ident)
                    pe.transpose(w[:, 256:384], mp[j % 2][:, 256:384], ident).then_inc(stage("pa_turned"), 1)
                    pe.wait_ge(stage("pa_pcopied"), j + 1)
                    if j >= 2:
                        pe.wait_ge(stage("pa_out"), j - 1)
                    o = bank[4 + j % 2]
                    pe_mm(o[:, 0:NPR], lhsT=vtok[:, 0, j * P:(j + 1) * P], rhs=mpT[j % 2][:, 0:NPR], start=True, stop=False)
                    pe_mm(o[:, P:NPR], lhsT=vtok[:, 1, j * P:(j + 1) * P], rhs=mpT[j % 2][:, NPR:384], start=False, stop=True).then_inc(stage("pa_ready"), 1)
            pe.wait_ge(slot_in[UKT % RING], arrive[UKT])
            wkt = ring[UKT % RING][:, :].rearrange("p (h c) -> p h c", h=H)
            pe.wait_ge(*once("qns_ready"))
            pe.wait_ge(stage("pa_out"), 8)
            for g in range(2):
                for j in range(4):
                    mm = pe_mm(bank[g][32 * j:32 * j + 32, :], lhsT=qnS[:, 4 * g + j, :], rhs=wkt[:, 4 * g + j, :], start=True, stop=True)
            mm.then_inc(once("qlat_ready")[0], 1)
            for half in (slice(0, ROPE), slice(ROPE, P)):
                pe_mm(bank[7][half, 0:32], lhsT=ident[:, 0:ROPE], rhs=qpeT[:, :, NPR:T], start=True, stop=True, skip_group_check=True)
                pe_mm(bank[7][half, 32:64], lhsT=ident[:, ROPE:P], rhs=qpeT[:, :, NPR:T], start=True, stop=True, skip_group_check=True)
            for k in range(LORA):
                mm = pe_mm(bank[5][0:NSA, k * P:(k + 1) * P], lhsT=latT[:, k, NPR:T], rhs=ident, start=True, stop=True)
            mm.then_inc(once("ltok_ready")[0], 1)
            for g in range(2):
                pe.wait_ge(stage("qrow_copied"), g + 1)
                for k in range(LORA):
                    mm = pe_mm(bank[2 + g][:, P * k:P * (k + 1)], lhsT=qrow[:, g, P * k:P * (k + 1)], rhs=ident, start=True, stop=True)
                mm.then_inc(stage("qlat_turned"), 1)
            pe.wait_ge(stage("qlat_copied"), 2)
            def project(first, last):
                for m in range(first, last):
                    n = (OG, GA, GB, OM, WO)[m // 8] + m % 8 // 4
                    rhs = (oG, hT, hT, oM, yA)[m // 8]
                    weights(pe, n)
                    if m == 0:
                        pe.wait_ge(stage("z_gated"), H)
                    if m == 24:
                        pe.wait_ge(*once("os_copied"))
                    if m == 32:
                        pe.wait_ge(stage("merged"), KD)
                    if m >= 2:
                        kind, r = (m - 2) // 8, (m - 2) % 8 + 1
                        pe.wait_ge(stage("gate_sig" if kind in (1, 2) else "out_evac"), (0, 0, 8, 8, 16)[kind] + r)
                    for k in range(KD):
                        mm = pe_mm(bank[4 + m % 2][:, 0:T], lhsT=chunk_k(n, m % 4, k), rhs=rhs[:, k, :], start=(k == 0), stop=(k == KD - 1))
                    mm.then_inc(stage("out_ready"), 1)

            for q in range(2):
                bs = range(4 * q, 4 * q + 4)
                if q == 1:
                    pe.wait_ge(stage("s_exp"), 1)
                for b in bs:
                    r = slice(32 * (b % 4), 32 * (b % 4) + 32)
                    half = slice(ROPE * (b % 4 // 2), ROPE * (b % 4 // 2 + 1))
                    pe.wait_ge(stage(f"pe_in{b % 4}"), 16 * PAGES * (b // 4 + 1))
                    for y in range(2):
                        mm = pe_mm(bank[y][r, :], lhsT=qpeS[half, b, :], rhs=peT[b % 4][:, 512 * y:512 * y + 512],
                                   start=True, stop=False, skip_group_check=True)
                    mm.then_inc(stage("pe_used"), 1)
                for b in bs:
                    r = slice(32 * (b % 4), 32 * (b % 4) + 32)
                    pe_mm(bank[6][r, 0:NSA], lhsT=qpeS[0:ROPE, b, :], rhs=kpeT[0:ROPE, NPR:T], start=True, stop=False, skip_group_check=True)
                for k in range(LORA):
                    for b in bs:
                        r = slice(32 * (b % 4), 32 * (b % 4) + 32)
                        mm = pe_mm(bank[6][r, 0:NSA], lhsT=qlatT[:, k, b, :], rhs=latT[:, k, NPR:T], start=False, stop=(k == LORA - 1), skip_group_check=True)
                mm.then_inc(stage("snew_scores"), 1)
                for b in bs:
                    pe.wait_ge(slot_in[kv_chunk(b, 0) % RING], arrive[kv_chunk(b, 0)])
                for y in range(2):
                    for k in range(LORA):
                        for b in bs:
                            r = slice(32 * (b % 4), 32 * (b % 4) + 32)
                            kt = ring[kv_chunk(b, 0) % RING][:, :].rearrange("p (g c s) -> p g c s", g=PAGES, c=LORA)
                            mm = pe_mm(bank[y][r, :], lhsT=qlatT[:, k, b, :], rhs=kt[:, 4 * y:4 * y + 4, k, :],
                                       start=False, stop=(k == LORA - 1), skip_group_check=True)
                mm.then_inc(stage("st_ready"), 1)
                project(16 * q, 16 * q + 4)
                pe.wait_ge(stage("p_ready"), q + 1)
                if q == 1:
                    pe.wait_ge(stage("ol_copied"), 1)
                for g in range(PAGES):
                    pe_mm(bank[2 + g // 4][:, P * (g % 4):P * (g % 4 + 1)], lhsT=ps_[q][:, P * g:P * (g + 1)], rhs=ident, start=True, stop=True)
                pe_mm(bank[7][0:NSA, 0:P], lhsT=ps_[q][:, 1024:1032], rhs=ident, start=True, stop=True).then_inc(stage("p_turned"), 1)
                project(16 * q + 4, 16 * q + 8)
                pe.wait_ge(stage("pT_copied"), q + 1)
                for b in bs:
                    pe.wait_ge(slot_in[kv_chunk(b, 1) % RING], arrive[kv_chunk(b, 1)])
                for g in range(PAGES):
                    for b in bs:
                        r = slice(32 * (b % 4), 32 * (b % 4) + 32)
                        pe_mm(bank[6][r, :], lhsT=pT[:, g, r], rhs=ring[kv_chunk(b, 1) % RING][:, 512 * g:512 * (g + 1)],
                              start=(g == 0), stop=False, skip_group_check=True)
                for b in bs:
                    r = slice(32 * (b % 4), 32 * (b % 4) + 32)
                    mm = pe_mm(bank[6][r, :], lhsT=pT9[0:NSA, r], rhs=lat_tok[0:NSA, :], start=False, stop=True, skip_group_check=True)
                mm.then_inc(stage("ol_ready"), 1)
                if q == 0:
                    project(8, 10)
                pe.wait_ge(stage("orow_copied"), q + 1)
                for k in range(LORA):
                    mm = pe_mm(bank[7][:, P * k:P * (k + 1)], lhsT=orow[:, P * k:P * (k + 1)], rhs=ident, start=True, stop=True)
                mm.then_inc(stage("ol_turned"), 1)
                if q == 0:
                    project(10, 16)
            pe.wait_ge(slot_in[UV2 % RING], arrive[UV2])
            pe.wait_ge(stage("ol_copied"), 2)
            wv2 = ring[UV2 % RING][:, :].rearrange("p (c n) -> p c n", c=LORA)
            for g in range(2):
                for k in range(LORA):
                    for j in range(4):
                        h = 4 * g + j
                        mm = pe_mm(bank[0][32 * j:32 * j + 32, P * g:P * (g + 1)], lhsT=olat[:, k, h, :], rhs=wv2[:, k, h * P:(h + 1) * P],
                                   start=(k == 0), stop=(k == LORA - 1), skip_group_check=True)
            mm.then_inc(once("os_ready")[0], 1)
            pe.wait_ge(*once("osr_copied"))
            for g in range(2):
                mm = pe_mm(bank[7][:, P * g:P * (g + 1)], lhsT=osr[:, P * g:P * (g + 1)], rhs=ident, start=True, stop=True)
            mm.then_inc(once("os_turned")[0], 1)
            project(24, 40)
            pe.wait_ge(sq_ready, 2)
            sum_squares(bank[4][:, 0:T], lambda k: msq2[:, k, :], KD).then_inc(ss_ready, 1)
            pe.wait_ge(h_ready, 2)
            tiles = ((0, P), (P, NPR), (NPR, T))
            for i, (a, b) in enumerate(tiles):
                for k in range(KD):
                    mm = pe_mm(bank[5][0:b - a, NE * i:NE * i + NE], lhsT=hT[:, k, a:b], rhs=wsm[:, k, 16 + ROPE:WSM], start=(k == 0), stop=(k == KD - 1))
            mm.then_inc(once("logits")[0], 1)
            for i, (a, b) in enumerate(tiles):
                for y in range(2):
                    q = 2 * i + y
                    if q >= 4:
                        pe.wait_ge(stage("h2_copied"), q - 3)
                    for k in range(4):
                        mm = pe.transpose(bank[q % 4][0:b - a, k * P:(k + 1) * P], hT[:, 4 * y + k, a:b], ident)
                    mm.then_inc(stage("h2_turned"), 1)
            pe.wait_ge(stage("sel_ready"), 1)
            pe_mm(bank[6][0:NE, 0:P], lhsT=sel[:, 0, :], rhs=before, start=True, stop=True)
            pe_mm(bank[6][0:NE, P:NPR], lhsT=sel[:, 0, :], rhs=ones, start=True, stop=False)
            pe_mm(bank[6][0:NE, P:NPR], lhsT=sel[:, 1, :], rhs=before, start=False, stop=True)
            pe_mm(bank[6][0:NE, NPR:T], lhsT=sel[:, 0, :], rhs=ones[:, 0:NSA], start=True, stop=False)
            pe_mm(bank[6][0:NE, NPR:T], lhsT=sel[:, 1, :], rhs=ones[:, 0:NSA], start=False, stop=False)
            pe_mm(bank[6][0:NE, NPR:T], lhsT=sel[0:NSA, 2, :], rhs=before[0:NSA, 0:NSA], start=False, stop=True)
            pe_mm(bank[7][0:NE, 0:1], lhsT=sel[:, 0, :], rhs=ones[:, 0:1], start=True, stop=False)
            pe_mm(bank[7][0:NE, 0:1], lhsT=sel[:, 1, :], rhs=ones[:, 0:1], start=False, stop=False)
            pe_mm(bank[7][0:NE, 0:1], lhsT=sel[0:NSA, 2, :], rhs=ones[0:NSA, 0:1], start=False, stop=True)
            pe.wait_ge(stage("sel_ready"), 2)
            for i, (a, b) in enumerate(tiles):
                pe.transpose(bank[4][0:NE, a:b], sel[0:b - a, i, :], ident[0:b - a, 0:b - a])
            pe.wait_ge(stage("h2_copied"), 6)
            for i, (a, b) in enumerate(tiles):
                mm = pe.transpose(bank[0][0:NE, a:b], gate[0:b - a, i, :], ident[0:b - a, 0:b - a])
            mm.then_inc(stage("route"), 1)
            pe.wait_ge(stage("blocks"), 1)
            pe_mm(bank[7][0:NE, 1:2], lhsT=before[0:NE, 0:NE], rhs=cntc[0:NE, 0:1], start=True, stop=True)
            pe_mm(bank[7][0:1, 2:3], lhsT=cntc[0:NE, 0:1], rhs=ones[0:NE, 0:1], start=True, stop=True).then_inc(stage("route"), 1)
            pe.wait_ge(*once("e1h_ready"))
            pe_mm(bank[7][0:1, 8:8 + NJ1], lhsT=con[0:NE, C_E:C_E + 1], rhs=e1h[0:NE, :], start=True, stop=True).then_inc(stage("route"), 1)
            pe.wait_ge(*once("m1_ready"))
            for i, (a, b) in enumerate(tiles):
                pe_mm(bank[1][0:b - a, NJ1 * i:NJ1 * (i + 1)], lhsT=m1T[0:NE, a:b], rhs=e1h[0:NE, :], start=True, stop=True)
            for i, (a, b) in enumerate(tiles):
                mm = pe_mm(bank[2][0:b - a, NJ1 * i:NJ1 * (i + 1)], lhsT=gateT[0:NE, a:b], rhs=e1h[0:NE, :], start=True, stop=True)
            mm.then_inc(stage("route"), 1)
            moe_tensor(pe)
            pe.wait_ge(sq_ready, 3)
            sum_squares(bank[0][:, 0:T], lambda k: msq2[:, k, :], KD).then_inc(ss_ready, 1)

        @block.scalar
        def _(act):
            line = [0]

            def link(ins):
                line[0] += 1
                ins.then_inc(act_line, 1)
                act.wait_ge(act_line, line[0])

            A = nc.scalar.activation
            act.wait_ge(inputs_in, 64)
            A(hT[:, :, :], xT[:, :, :], ACT.Square).then_inc(sq_ready, 1)

            def root(out, sums, scale):
                return A(out, sums, ACT.Sqrt, scale=scale, bias=con[:, C_EPS:C_EPS + 1])
            act.wait_ge(ss_ready, 1)
            act.wait_ge(*once("upad_zero"))
            root(rsb[:, 0, :], bank[4][:, 0:T], 1.0 / D).then_inc(root_ready, 1)
            def mod_rows(i, b):
                act.wait_ge(mod_ready, i + 1)
                if i >= 2:
                    act.wait_ge(mod_turned, i - 1)
                A(mrow[:, i % 2, :], bank[b][:, 0:P], ACT.Copy).then_inc(mod_row, 1)
            for i in range(4):
                mod_rows(i, i % 2)
            for m in range(CONVT + 1):
                if m < CONVT:
                    act.wait_ge(proj_ready, m + 1)
                    if m >= 3:
                        act.wait_ge(conv_done, m - 2)
                    elif m == 0:
                        act.wait_ge(*once("upad_zero"))
                    b = bank[m % 4]
                    A(samp[:, m, 3, :], b[:, NPR:T], ACT.Copy)
                    A(convp[:, m, :], b[:, NPR - 3:NPR], ACT.Copy)
                    A(upad[:, m % 3, 3:3 + NPR], b[:, 0:NPR], ACT.Copy).then_inc(proj_evac, 1)
                if m >= 1:
                    act.wait_ge(conv_done, m)
                    if m >= 3:
                        act.wait_ge(silu_done, m - 2)
                    A(sigb[:, (m - 1) % 2, 0:NPR], qkvT[:, m - 1, 0:NPR], ACT.Sigmoid).then_inc(sig_done, 1)
            act.wait_ge(stage("conv_s"), 1)
            A(smt[:, 1, :, :], smt[:, 0, :, :], ACT.Sigmoid).then_inc(sig_done, 1)
            act.wait_ge(ab_ready, 1)
            act.wait_ge(stage("ab_copied"), 1)
            A(beta_tok[:, :, :], gsc[:, 0, :, :], ACT.Sigmoid).then_inc(ab_act, 1)
            link(A(gsc[:, 2, :, :], gsc[:, 1, :, :], ACT.Abs))
            link(A(gsc[:, 2, :, :], gsc[:, 2, :, :], ACT.Exp, scale=-1.0))
            link(A(gcol[:, 0, :], small[:, S_ALOG:S_ALOG + 8], ACT.Exp))
            A(gsc[:, 2, :, :], gsc[:, 2, :, :], ACT.Ln, bias=1.0).then_inc(ab_act, 1)
            act.wait_ge(silu_done, CONVT + 1)
            for i in range(2 * H + 1):
                if i < 2 * H:
                    if i >= 2:
                        act.wait_ge(l2ss, i - 1)
                    A(sqb[:, i % 2, :], qkvT[:, i, :], ACT.Square).then_inc(l2sq, 1)
                if i >= 1:
                    act.wait_ge(l2ss, i)
                    if i >= 3:
                        act.wait_ge(l2done, i - 2)
                    root(rsb[:, (i - 1) % 2, :], bank[4 + (i - 1) % 2][:, 0:T], 1.0).then_inc(root_ready, 1)
            for c in range(2):
                if c == 0:
                    act.wait_ge(*once("cum_ready"))
                    A(egB[:, :], bank[6][:, 96:160], ACT.Exp).then_inc(stage("egB_ready"), 1)
                    act.wait_ge(l2done, 2 * H)
                    act.wait_ge(stage("cum_copied"), 1)
                else:
                    act.wait_ge(stage("gd_out"), 2)
                    act.wait_ge(stage("cum_copied"), 2)
                A(gcol[:, 1, :], gcol[:, 0, :], ACT.Exp).then_inc(stage("gexp"), 1)
                A(gcol[:, 4, :], gsc[:, 0, 0, :], ACT.Exp).then_inc(stage("gexp"), 1)
                A(gcol[:, 3, :], gsc[:, 0, 1, :], ACT.Exp).then_inc(stage("gexp"), 1)
                for q, (w, g) in enumerate(((0, 0), (1, 0), (0, 1), (1, 1))):
                    act.wait_ge(tr_ready, 4 * c + q + 1)
                    A((K2 if w == 0 else VB)[:, g, :], bank[2 * w + g][:, :], ACT.Copy).then_inc(tr_evac, 1)
                for g in range(2):
                    b0 = 4 - 4 * g
                    act.wait_ge(stage("gd_prod"), 2 * c + g + 1)
                    A(XTm[:, g, :], bank[b0][:, :], ACT.Exp).then_inc(stage("eg_done"), 1)
                    act.wait_ge(stage("dif_done"), 2 * c + g + 1)
                    A(LTm[:, g, :], LTm[:, g, :], ACT.Exp).then_inc(stage("dec_done"), 1)
                for lv in range(LEVELS):
                    for g in range(2):
                        act.wait_ge(stage("lx_done"), (c * LEVELS + lv) * 2 + g + 1)
                        A(LTm[:, g, :], bank[g][:, :], ACT.Copy).then_inc(stage("lx_copied"), 1)
                    if 4 + c * LEVELS + lv < 16:
                        mod_rows(4 + c * LEVELS + lv, 6)
                if c == 1:
                    for g in range(2):
                        act.wait_ge(stage("uw_done"), 2 + g + 1)
                        A(Xm[:, g, :], bank[2 + g][:, :], ACT.Copy).then_inc(stage("wt_copied"), 1)
                act.wait_ge(stored, 32)
                for g in range(2):
                    act.wait_ge(stage("os_done"), 2 * c + g + 1)
                    A(oG[:, 4 * g:4 * g + 4, c * P:(c + 1) * P], bank[6 + g][:, :].rearrange("p (h t) -> p h t", h=4),
                      ACT.Copy).then_inc(stage("o_copied"), 1)
            act.wait_ge(stage("gd_out"), 4)
            act.wait_ge(*once("x32_zero"))
            A(x32[:, :, 0:NSA], qkvT[:, :, NPR:T], ACT.Copy).then_inc(once("x32_ready")[0], 1)
            act.wait_ge(stage("sample_products"), 3)
            for j in range(4):
                r = slice(32 * j, 32 * j + 32)
                ins = A(krow[r, j, :, :], bank[5][r, 0:2 * P].rearrange("p (g v) -> p g v", g=2), ACT.Copy)
            ins.then_inc(once("krow_copied")[0], 1)
            act.wait_ge(*once("oss_turned"))
            A(oG[:, :, NPR:T], bank[4][:, 0:2 * P].rearrange("p (h b) -> p h b", h=H)[:, :, 0:NSA], ACT.Copy).then_inc(stage("o_copied"), 1)
            act.wait_ge(stage("o_copied"), 5)
            for h in range(H + 1):
                if h < H:
                    if h >= 2:
                        act.wait_ge(stage("on_ss"), h - 1)
                    A(msq[:, h % 2, :], oG[:, h, :], ACT.Square).then_inc(stage("on_sq"), 1)
                if h >= 1:
                    act.wait_ge(stage("on_ss"), h)
                    if h >= 3:
                        act.wait_ge(stage("on_rs"), h - 2)
                    root(mrs[:, (h - 1) % 2, :], bank[(h - 1) % 2][:, 0:T], 1.0 / P).then_inc(root_ready, 1)
            for m in range(H):
                act.wait_ge(stage("z_ready"), m + 1)
                if m == 0:
                    act.wait_ge(stage("on_rs"), H)
                if m >= 2:
                    act.wait_ge(stage("z_gated"), m - 1)
                A(zsig[:, m % 2, :], bank[m % 4][:, 0:T], ACT.Sigmoid).then_inc(stage("z_sig"), 1)
            for m in range(8):
                act.wait_ge(stage("lat_ready"), m + 1)
                A((cqT if m < 4 else latT)[:, m % 4, :], bank[4 + m % 4][:, 0:T], ACT.Copy).then_inc(stage("lat_evac"), 1)
            act.wait_ge(*once("kpe_ready"))
            A(kpeT[:, :], bank[0][:, 0:T], ACT.Copy).then_inc(once("kpe_copied")[0], 1)
            act.wait_ge(stage("lat_evac"), 8)
            act.wait_ge(stage("z_gated"), H)
            for i in range(2 * LORA):
                if i >= 2:
                    act.wait_ge(stage("lss"), i - 1)
                A(msq[:, i % 2, :], (cqT if i < 4 else latT)[:, i % 4, :], ACT.Square).then_inc(stage("lsq"), 1)
                if i % LORA == LORA - 1:
                    act.wait_ge(stage("lss"), i + 1)
                    root(mrs[:, i // LORA, :], bank[2 + i // LORA][:, 0:T], 1.0 / (LORA * P)).then_inc(root_ready, 1)
            for m in range(12):
                act.wait_ge(stage("q_ready"), m + 1)
                A(qnT[:, m, :] if m < 8 else qpeT[:, m - 8, :], bank[4 + m % 4][:, 0:T], ACT.Copy).then_inc(stage("q_evac"), 1)
            for h in range(H):
                act.wait_ge(stage("kn_ready"), h + 1)
                A(knT[:, h, :], bank[4 + h % 4][:, 0:NPR], ACT.Copy).then_inc(stage("kn_evac"), 1)
            for i in range(4):
                act.wait_ge(stage("vt_ready"), i + 1)
                A(vtok[:, i // 2, 512 * (i % 2):512 * (i % 2) + 512], bank[i][:, :], ACT.Copy).then_inc(stage("vt_evac"), 1)
            for h in range(H + 1):
                if h < H:
                    act.wait_ge(stage("pa_max"), h + 1)
                    if h >= 2:
                        act.wait_ge(stage("pa_turned"), h - 1)
                    st = mstat[:, h % 2, :]
                    A(mp[h % 2][:, 0:P], msc[h % 2][:, 0:P], ACT.Exp, bias=st[:, 2:3], scale=SCALE, accum_out=st[:, 4:5])
                    A(mp[h % 2][:, P:384], msc[h % 2][:, P:384], ACT.Exp, bias=st[:, 3:4], scale=SCALE, accum_out=st[:, 5:6]).then_inc(stage("pa_exp"), 1)
                if h >= 1:
                    j = h - 1
                    act.wait_ge(stage("pa_turned"), j + 1)
                    if j >= 2:
                        act.wait_ge(stage("pa_ready"), j - 1)
                    A(mpT[j % 2][:, :], bank[2 + j % 2][:, 0:384], ACT.Copy).then_inc(stage("pa_pcopied"), 1)
                    act.wait_ge(stage("pa_ready"), j + 1)
                    A(oM[:, j, 0:NPR], bank[4 + j % 2][:, 0:NPR], ACT.Copy).then_inc(stage("pa_out"), 1)
            act.wait_ge(*once("att_zero"))
            A(qnS[:, :, 0:NSA], qnT[:, :, NPR:T], ACT.Copy).then_inc(once("qns_ready")[0], 1)
            act.wait_ge(*once("qlat_ready"))
            for g in range(2):
                A(qrow[:, g, :], bank[g][:, :], ACT.Copy).then_inc(stage("qrow_copied"), 1)
            act.wait_ge(*once("ltok_ready"))
            for i in range(2):
                A(qpeS[:, :, i:NSA:2], bank[7][:, 32 * i:32 * i + 32].rearrange("p (a b) -> p b a", a=4), ACT.Copy)
            A(lat_tok[0:NSA, :], bank[5][0:NSA, :], ACT.Copy)
            for g in range(2):
                act.wait_ge(stage("qlat_turned"), g + 1)
                for k in range(LORA):
                    ins = A(qlatT[:, k, :, 4 * g:4 * g + 4], bank[2 + g][:, P * k:P * (k + 1)].rearrange("p (j b) -> p b j", j=4)[:, 0:NSA, :], ACT.Copy)
                ins.then_inc(stage("qlat_copied"), 1)
            def evacuate(first, last):
                for m in range(first, last):
                    act.wait_ge(stage("out_ready"), m + 1)
                    b = bank[4 + m % 2][:, 0:T]
                    if m < 8:
                        A(yA[:, m, :], b, ACT.Copy).then_inc(stage("out_evac"), 1)
                    elif m < 16:
                        if m >= 10:
                            act.wait_ge(stage("gated"), m - 9)
                        A(gsig[:, m % 2, :], b, ACT.Sigmoid).then_inc(stage("gate_sig"), 1)
                    else:
                        A(gB[:, m - 16, :], b, ACT.Sigmoid).then_inc(stage("gate_sig"), 1)

            for q in range(2):
                act.wait_ge(stage("s_max"), q + 1)
                st = sstat[:, q, :]
                A(ps_[q][:, 1024:1032], ps_[q][:, 1024:1032], ACT.Exp, bias=st[:, 2:3], scale=SCALE, accum_out=st[:, 4:5])
                A(ps_[q][:, 0:1024].rearrange("p (y s) -> p y s", y=2), banks[:, 0:2, :], ACT.Exp, bias=st[:, 2:3], scale=SCALE,
                  accum_out=st[:, 3:4]).then_inc(stage("s_exp"), 1)
                evacuate(16 * q, 16 * q + 4)
                act.wait_ge(stage("p_turned"), q + 1)
                for y in range(2):
                    A(pT[:, 4 * y:4 * y + 4, :], bank[2 + y][:, :].rearrange("p (g r) -> p g r", g=4), ACT.Copy)
                A(pT9[0:NSA, :], bank[7][0:NSA, 0:P], ACT.Copy).then_inc(stage("pT_copied"), 1)
                evacuate(16 * q + 4, 16 * q + 8)
                act.wait_ge(stage("ol_ready"), q + 1)
                A(orow[:, :], bank[6][:, :], ACT.Copy).then_inc(stage("orow_copied"), 1)
                if q == 0:
                    evacuate(8, 10)
                act.wait_ge(stage("ol_turned"), q + 1)
                for k in range(LORA):
                    ins = A(olat[:, k, :, 4 * q:4 * q + 4], bank[7][:, P * k:P * (k + 1)].rearrange("p (j h) -> p h j", j=4)[:, 0:H, :], ACT.Copy)
                ins.then_inc(stage("ol_copied"), 1)
                if q == 0:
                    evacuate(10, 16)
            act.wait_ge(*once("os_ready"))
            A(osr[:, :], bank[0][:, 0:2 * P], ACT.Copy).then_inc(once("osr_copied")[0], 1)
            act.wait_ge(*once("os_turned"))
            A(oM[:, :, NPR:T], bank[7][:, 0:2 * P].rearrange("p (h b) -> p h b", h=H)[:, :, 0:NSA], ACT.Copy).then_inc(once("os_copied")[0], 1)
            act.wait_ge(stage("out_evac"), 24)
            A(msq2[:, :, :], xT[:, :, :], ACT.Square).then_inc(sq_ready, 1)
            act.wait_ge(ss_ready, 2)
            root(mrs2[:, :], bank[4][:, 0:T], 1.0 / D).then_inc(root_ready, 1)
            act.wait_ge(stored, 64)
            for i in range(6):
                act.wait_ge(stage("h2_turned"), i + 1)
                n = P if i < 4 else NSA
                A(h2tok[0:n, i // 2, :, 64 * (i % 2):64 * (i % 2) + 64],
                  bank[i % 4][0:n, :].rearrange("p (x k) -> p k x", k=KD), ACT.Copy).then_inc(stage("h2_copied"), 1)
            act.wait_ge(*once("v8_ready"))
            for i in range(3):
                A(ex[:, i, :], lg[:, i, :], ACT.Exp, bias=rst[:, 0, i:i + 1]).then_inc(stage("route_exp"), 1)
            moe_scalar(act)
            act.wait_ge(*once("x2_ready"))
            A(msq2[:, :, :], xT[:, :, :], ACT.Square).then_inc(sq_ready, 1)
            act.wait_ge(ss_ready, 3)
            root(mrs2[:, :], bank[0][:, 0:T], 1.0 / D).then_inc(root_ready, 1)

        @block.vector
        def _(dve):
            line = [0]
            V = nc.vector

            def link(ins):
                line[0] += 1
                ins.then_inc(dve_line, 1)
                dve.wait_ge(dve_line, line[0])

            def norm_mod(r, x, out, sc, sh, nw, rs, A9):
                link(V.scalar_tensor_tensor(A9, mod[:, sc:sc + KD, :], 1.0,
                                            small[:, nw:nw + KD].unsqueeze(2).to_broadcast([P, KD, 9]), ALU.add, ALU.mult))
                dve.wait_ge(root_ready, (1, 28, 29)[r])
                link(V.reciprocal(rs, rs))
                link(V.tensor_tensor(out, x, rs.unsqueeze(1).to_broadcast([P, KD, T]), ALU.mult))
                for k in range(KD):
                    link(V.tensor_scalar(out[:, k, 0:NPR], out[:, k, 0:NPR], A9[:, k, 0:1], mod[:, sh + k, 0:1], ALU.mult, ALU.add))
                link(V.tensor_tensor(out[:, :, NPR:T], out[:, :, NPR:T], A9[:, :, 1:9], ALU.mult))
                V.tensor_tensor(out[:, :, NPR:T], out[:, :, NPR:T], mod[:, sh:sh + KD, 1:9], ALU.add).then_inc(h_ready, 1)
                dve.wait_ge(h_ready, r + 1)

            dve.wait_ge(inputs_in, 64)
            link(V.memset(upad[:, :, 0:3], 0.0))
            link(V.memset(gsc[:, :, :, :], 0.0))
            V.memset(rsb[:, :, :], 0.0).then_inc(once("upad_zero")[0], 1)

            def mod_bias(i, b):
                dve.wait_ge(mod_turned, i + 1)
                V.tensor_tensor(mod[:, 4 * i:4 * i + 4, :], bank[b][:, 0:P].rearrange("p (m c) -> p m c", c=32)[:, :, 0:9],
                                small[:, S_BADA + 4 * i:S_BADA + 4 * i + 4].unsqueeze(2).to_broadcast([P, 4, 9]),
                                ALU.add).then_inc(mod_evac, 1)
            for i in range(4):
                mod_bias(i, 2 + i % 2)
            dve.wait_ge(mod_evac, 4)
            dve.wait_ge(*once("upad_zero"))
            norm_mod(0, xT[:, :, :], hT[:, :, :], 8, 0, S_NMIX, rsb[:, 0, :], modA[:, :, :])
            for m in range(CONVT + 1):
                if m < CONVT:
                    dve.wait_ge(proj_evac, m + 1)
                    u = upad[:, m % 3, :]
                    y = qkvT[:, m, 0:NPR]
                    link(V.tensor_scalar(y, u[:, 0:NPR], convw[:, m, 0:1], None, ALU.mult))
                    for j in range(1, 3):
                        link(V.scalar_tensor_tensor(y, u[:, j:j + NPR], convw[:, m, j:j + 1], y, ALU.mult, ALU.add))
                    V.scalar_tensor_tensor(y, u[:, 3:3 + NPR], convw[:, m, 3:4], y, ALU.mult, ALU.add).then_inc(conv_done, 1)
                if m >= 1:
                    dve.wait_ge(sig_done, m)
                    V.tensor_tensor(qkvT[:, m - 1, 0:NPR], qkvT[:, m - 1, 0:NPR], sigb[:, (m - 1) % 2, 0:NPR], ALU.mult).then_inc(silu_done, 1)
            for j in range(4):
                dst = smt[:, 0, :, :] if j == 0 else smt[:, 1, :, :]
                link(V.tensor_tensor(dst, samp[:, :, j, :], convw[:, :, j:j + 1].to_broadcast([P, CONVT, NSA]), ALU.mult))
                if j:
                    ins = V.tensor_tensor(smt[:, 0, :, :], smt[:, 0, :, :], smt[:, 1, :, :], ALU.add)
                    if j < 3:
                        link(ins)
                    else:
                        ins.then_inc(stage("conv_s"), 1)
            dve.wait_ge(sig_done, CONVT + 1)
            V.tensor_tensor(qkvT[:, :, NPR:T], smt[:, 0, :, :], smt[:, 1, :, :], ALU.mult).then_inc(silu_done, 1)
            dve.wait_ge(ab_ready, 1)
            dve.wait_ge(dve_line, line[0])
            for i, n in ((0, P), (1, P), (2, NSA)):
                link(V.tensor_copy(gsc[0:n, 0, i, :], bank[6][0:n, 16 * i:16 * i + 8]))
                ins = V.tensor_tensor(gsc[0:n, 1, i, :], bank[6][0:n, 16 * i + 8:16 * i + 16], small[0:n, S_DT:S_DT + 8], ALU.add)
                if i < 2:
                    link(ins)
                else:
                    ins.then_inc(stage("ab_copied"), 1)
            dve.wait_ge(ab_act, 2)
            link(V.tensor_scalar(gsc[:, 1, :, :], gsc[:, 1, :, :], 0.0, None, ALU.max))
            link(V.tensor_tensor(gsc[:, 1, :, :], gsc[:, 1, :, :], gsc[:, 2, :, :], ALU.add))
            dve.wait_ge(act_line, 3)
            V.scalar_tensor_tensor(g_tok[:, :, :], gsc[:, 1, :, :], -1.0, gcol[:, 0, :].unsqueeze(1).to_broadcast([P, 3, H]),
                                   ALU.mult, ALU.mult).then_inc(bg_done, 1)
            dve.wait_ge(bg_done, 1)
            V.tensor_tensor(bgm[0:NSA, :].rearrange("p (h b) -> p h b", h=H), ident[0:NSA, 0:NSA].unsqueeze(1).to_broadcast([NSA, H, NSA]),
                            g_tok[0:NSA, 2, :].unsqueeze(2).to_broadcast([NSA, H, NSA]), ALU.mult).then_inc(stage("bgm_ready"), 1)
            for i in range(2 * H):
                dve.wait_ge(root_ready, i + 2)
                link(V.reciprocal(rsb[:, i % 2, :], rsb[:, i % 2, :]))
                V.scalar_tensor_tensor(qkvT[:, i, :], qkvT[:, i, :], P ** -0.5 if i < H else 1.0, rsb[:, i % 2, :], ALU.mult, ALU.mult).then_inc(l2done, 1)
                dve.wait_ge(l2done, i + 1)
            dve.wait_ge(*once("cum_ready"))
            dve.wait_ge(stage("egB_ready"), 1)
            V.tensor_copy(cumc[:, :, :], bank[6][:, 64:96].rearrange("p (c e) -> p c e", c=2)).then_inc(once("cum_read")[0], 1)
            dve.wait_ge(*once("cum_read"))
            for c in range(2):
                if c == 1:
                    dve.wait_ge(stage("gd_out"), 2)
                link(V.tensor_copy(gcol[:, 0, :], cumc[:, c, 0:8]))
                link(V.tensor_copy(gsc[:, 0, 0, :], cumc[:, c, 8:16]))
                V.tensor_tensor(gsc[:, 0, 1, :], cumc[:, c, 8:16], cumc[:, c, 0:8], ALU.subtract).then_inc(stage("cum_copied"), 1)
                dve.wait_ge(stage("gexp"), 3 * c + 3)
                link(V.tensor_tensor(gcol[:, 2, :], gcol[:, 1, :], beta_tok[:, c, :], ALU.mult))
                for g in range(2):
                    b0 = 4 - 4 * g
                    hs = slice(4 * g, 4 * g + 4)

                    def heads(v):
                        return v.rearrange("p (h t) -> p h t", h=4)

                    def col(v):
                        return v.unsqueeze(2).to_broadcast([P, 4, P])

                    def row(v):
                        return v.unsqueeze(1).to_broadcast([P, 4, P])
                    dve.wait_ge(stage("gd_prod"), 2 * c + g + 1)
                    dve.wait_ge(stage("eg_done"), 2 * c + g + 1)
                    link(V.tensor_tensor(heads(LTm[:, g, :]), heads(bank[b0][:, :]), col(gcol[:, 0, hs]), ALU.subtract))
                    V.tensor_scalar(LTm[:, g, :], LTm[:, g, :], 0.0, None, ALU.min).then_inc(stage("dif_done"), 1)
                    link(V.tensor_tensor(heads(qg[:, g, :]), heads(XTm[:, g, :]), qkvT[:, hs, c * P:(c + 1) * P], ALU.mult))
                    dve.wait_ge(tr_evac, 4 * c + 4)
                    link(V.tensor_tensor(heads(VB[:, g, :]), heads(VB[:, g, :]), col(beta_tok[:, c, hs]), ALU.mult))
                    link(V.tensor_tensor(heads(KBG[:, g, :]), heads(K2[:, g, :]), col(gcol[:, 2, hs]), ALU.mult))
                    link(V.tensor_tensor(heads(K2[:, g, :]), heads(K2[:, g, :]), col(gcol[:, 3, hs]), ALU.mult))
                    dve.wait_ge(stage("dec_done"), 2 * c + g + 1)
                    link(V.tensor_tensor(heads(LTm[:, g, :]), heads(LTm[:, g, :]), row(upto), ALU.mult))
                    link(V.tensor_tensor(Aqk[:, g, :], bank[b0 + 3][:, :], LTm[:, g, :], ALU.mult))
                    link(V.tensor_tensor(AT[:, g, :], bank[b0 + 2][:, :], LTm[:, g, :], ALU.mult))
                    link(V.tensor_tensor(AT[:, g, :], bank[b0 + 1][:, :], AT[:, g, :], ALU.mult))
                    link(V.tensor_copy(heads(Xm[:, g, :]), row(ident)))
                    V.tensor_copy(heads(XTm[:, g, :]), row(ident)).then_inc(stage("prep_done"), 1)
                    dve.wait_ge(stage("prep_done"), 2 * c + g + 1)
                for lv in range(LEVELS):
                    mask = con[:, C_LEV + lv * P:C_LEV + (lv + 1) * P]
                    for g in range(2):
                        q = (c * LEVELS + lv) * 2 + g + 1
                        if lv >= 1:
                            dve.wait_ge(stage("xlx_done"), q - 2)
                            link(V.tensor_tensor(Xm[:, g, :], Xm[:, g, :], bank[2 + g][:, :], ALU.subtract))
                            V.tensor_tensor(XTm[:, g, :], XTm[:, g, :], bank[4 + g][:, :], ALU.subtract).then_inc(stage("x_done"), 1)
                            dve.wait_ge(stage("x_done"), q - 2)
                        V.tensor_tensor(heads(LTm[:, g, :]), heads(AT[:, g, :]), row(mask), ALU.mult).then_inc(stage("lt_done"), 1)
                    if lv >= 1 and 3 + c * LEVELS + lv < 16:
                        mod_bias(3 + c * LEVELS + lv, 7)
                if 3 + (c + 1) * LEVELS < 16:
                    mod_bias(3 + (c + 1) * LEVELS, 7)
                for g in range(2):
                    q = (c * LEVELS + LEVELS) * 2 + g + 1 - 2
                    dve.wait_ge(stage("xlx_done"), q)
                    V.tensor_tensor(XTm[:, g, :], XTm[:, g, :], bank[4 + g][:, :], ALU.subtract).then_inc(stage("x_done"), 1)
                for g in range(2):
                    dve.wait_ge(stage("uw_done"), 2 * c + g + 1)
                    if c == 0:
                        V.tensor_copy(VB[:, g, :], bank[g][:, :]).then_inc(stage("vn_done"), 1)
                    else:
                        link(V.tensor_copy(VB[:, g, :], bank[g][:, :]))
                        dve.wait_ge(stage("ws_done"), g + 1)
                        V.tensor_tensor(VB[:, g, :], VB[:, g, :], bank[4 + g][:, :], ALU.subtract).then_inc(stage("vn_done"), 1)
                for g in range(2):
                    dve.wait_ge(stage("os_done"), 2 * c + g + 1)
                    dve.wait_ge(stage("o_copied"), 2 * c + g + 1)
                    if c == 1:
                        link(V.tensor_tensor(heads(Sst[:, g, :]), heads(Sst[:, g, :]), col(gcol[:, 4, 4 * g:4 * g + 4]), ALU.mult))
                        V.tensor_tensor(Sst[:, g, :], Sst[:, g, :], bank[2 + g][:, :], ALU.add).then_inc(stage("gd_out"), 1)
                    else:
                        V.tensor_copy(Sst[:, g, :], bank[2 + g][:, :]).then_inc(stage("gd_out"), 1)
                    dve.wait_ge(stage("gd_out"), 2 * c + g + 1)
            own = con[:, C_OWN:C_OWN + NSA].unsqueeze(2).to_broadcast([P, NSA, P])

            def own_rows(g, out):
                link(V.tensor_tensor(stmp[:, :].rearrange("p (b v) -> p b v", b=NSA),
                                     banks[:, 2 * g:2 * g + 2, :].rearrange("p y (b v) -> p (y b) v", b=4), own, ALU.mult))
                return V.tensor_reduce(out, stmp[:, :].rearrange("p (b v) -> p v b", b=NSA), AX, ALU.add)

            for g in range(2):
                dve.wait_ge(stage("sample_products"), g + 1)
                link(own_rows(g, ksr[:, g, :]))
            dve.wait_ge(stage("sample_products"), 3)
            link(V.tensor_copy(betac[:, :], bank[6][:, 0:2]))
            for g in range(2):
                link(V.tensor_tensor(vnr[:, g, :], bank[4][:, P * g:P * (g + 1)], ksr[:, g, :], ALU.subtract))
                link(V.tensor_scalar(vnr[:, g, :], vnr[:, g, :], betac[:, g:g + 1], None, ALU.mult))
                V.tensor_tensor(vnm[:, g, :].rearrange("p (b v) -> p b v", b=NSA), vnr[:, g, :].unsqueeze(1).to_broadcast([P, NSA, P]),
                                own, ALU.mult).then_inc(stage("vnm_ready"), 1)
            for u in range(4):
                g, y = u // 2, u % 2
                dve.wait_ge(stage("outer"), u + 1)
                S = ssm_view[g][:, :, 4 * y:4 * y + 4, :].rearrange("p h b v -> p h (b v)")
                V.tensor_tensor(S, S, banks[:, 4 * y:4 * y + 4, :], ALU.add).then_inc(stage("snew"), 1)
            for g in range(2):
                dve.wait_ge(stage("oss_ready"), g + 1)
                own_rows(g, ksr[:, g, :]).then_inc(stage("oss_row"), 1)
                dve.wait_ge(stage("oss_row"), g + 1)
            for h in range(H):
                dve.wait_ge(root_ready, 18 + h)
                link(V.reciprocal(mrs[:, h % 2, :], mrs[:, h % 2, :]))
                V.scalar_tensor_tensor(oG[:, h, :], oG[:, h, :], small[:, S_NGDN:S_NGDN + 1], mrs[:, h % 2, :], ALU.mult, ALU.mult).then_inc(stage("on_rs"), 1)
                dve.wait_ge(stage("on_rs"), h + 1)
            for m in range(H):
                dve.wait_ge(stage("z_sig"), m + 1)
                V.tensor_tensor(zsig[:, m % 2, :], zsig[:, m % 2, :], bank[m % 4][:, 0:T], ALU.mult).then_inc(stage("z_evac"), 1)
                dve.wait_ge(stage("z_evac"), m + 1)
                V.tensor_tensor(oG[:, m, :], oG[:, m, :], zsig[:, m % 2, :], ALU.mult).then_inc(stage("z_gated"), 1)

            def rotate(x, turned):
                link(V.tensor_tensor(rot[:, :], turned, sinT, ALU.mult))
                link(V.tensor_tensor(x, x, cosT, ALU.mult))
                return V.tensor_tensor(x, x, rot[:, :], ALU.add)
            dve.wait_ge(*once("kpe_turned"))
            rotate(kpeT[:, :], bank[1][:, 0:T]).then_inc(once("kpe_rot")[0], 1)
            for w in range(2):
                dve.wait_ge(root_ready, 26 + w)
                link(V.reciprocal(mrs[:, w, :], mrs[:, w, :]))
                for i in range(LORA):
                    v = (cqT, latT)[w][:, i, :]
                    nw = (S_NQ, S_NKV)[w] + i
                    ins = V.scalar_tensor_tensor(v, v, small[:, nw:nw + 1], mrs[:, w, :], ALU.mult, ALU.mult)
                    if i < LORA - 1:
                        link(ins)
                    else:
                        ins.then_inc(stage("lat_normed"), 1)
            dve.wait_ge(*once("kpe_rot"))
            for i in range(4):
                dve.wait_ge(stage("q_turn"), i + 1)
                rotate(qpeT[:, i, :], bank[i % 2][:, 0:T]).then_inc(stage("q_turned"), 1)
                dve.wait_ge(stage("q_turned"), i + 1)
            def normalise(j):
                dve.wait_ge(stage("pa_exp"), j + 1)
                st = mstat[:, j % 2, :]
                link(V.reciprocal(st[:, 6:8], st[:, 4:6]))
                link(V.tensor_scalar(mp[j % 2][:, 0:P], mp[j % 2][:, 0:P], st[:, 6:7], None, ALU.mult))
                V.tensor_scalar(mp[j % 2][:, P:384], mp[j % 2][:, P:384], st[:, 7:8], None, ALU.mult).then_inc(stage("pa_probs"), 1)

            for h in range(H + 1):
                if h < H:
                    dve.wait_ge(stage("pa_scores"), h + 1)
                    V.tensor_tensor(msc[h % 2][:, :], bank[h % 2][:, 0:384], neg384, ALU.add).then_inc(stage("pa_masked"), 1)
                    dve.wait_ge(stage("pa_masked"), h + 1)
                    st = mstat[:, h % 2, :]
                    link(V.tensor_reduce(st[:, 0:1], msc[h % 2][:, 0:P], AX, ALU.max))
                    link(V.tensor_reduce(st[:, 1:2], msc[h % 2][:, P:384], AX, ALU.max))
                    V.tensor_scalar(st[:, 2:4], st[:, 0:2], -SCALE, None, ALU.mult).then_inc(stage("pa_max"), 1)
                if h >= 1:
                    normalise(h - 1)
            for q in range(2):
                S, st = ps_[q], sstat[:, q, :]
                dve.wait_ge(stage("snew_scores"), q + 1)
                link(V.tensor_tensor(S[:, 1024:1032], bank[6][:, 0:NSA], con[:, C_B8 + 8 * q:C_B8 + 8 * q + 8], ALU.add))
                link(V.tensor_reduce(st[:, 1:2], S[:, 1024:1032], AX, ALU.max))
                dve.wait_ge(stage("st_ready"), q + 1)
                link(V.tensor_reduce(st[:, 0:1], banks[:, 0:2, :], AXY, ALU.max))
                link(V.tensor_tensor(st[:, 0:1], st[:, 0:1], st[:, 1:2], ALU.max))
                V.tensor_scalar(st[:, 2:3], st[:, 0:1], -SCALE, None, ALU.mult).then_inc(stage("s_max"), 1)
                dve.wait_ge(stage("s_exp"), q + 1)
                link(V.tensor_tensor(st[:, 5:6], st[:, 3:4], st[:, 4:5], ALU.add))
                link(V.reciprocal(st[:, 6:7], st[:, 5:6]))
                V.tensor_scalar(S[:, :], S[:, :], st[:, 6:7], None, ALU.mult).then_inc(stage("p_ready"), 1)
                if q == 0:
                    dve.wait_ge(stage("out_evac"), 8)
                    for m in range(8):
                        dve.wait_ge(stage("gate_sig"), m + 1)
                        V.tensor_tensor(yA[:, m, :], yA[:, m, :], gsig[:, m % 2, :], ALU.mult).then_inc(stage("gated"), 1)
                        dve.wait_ge(stage("gated"), m + 1)
            dve.wait_ge(stage("gate_sig"), 16)
            for m in range(8):
                dve.wait_ge(stage("out_ready"), 25 + m)
                V.tensor_tensor(gB[:, m, :], bank[4 + m % 2][:, 0:T], gB[:, m, :], ALU.mult).then_inc(stage("out_evac"), 1)
                dve.wait_ge(stage("out_evac"), 9 + m)
                V.tensor_tensor(yA[:, m, :], yA[:, m, :], gB[:, m, :], ALU.add).then_inc(stage("merged"), 1)
            for m in range(KD):
                dve.wait_ge(stage("out_ready"), 33 + m)
                b = bank[4 + m % 2]
                link(V.scalar_tensor_tensor(xT[:, m, 0:NPR], b[:, 0:NPR], mod[:, 16 + m, 0:1], xT[:, m, 0:NPR], ALU.mult, ALU.add))
                link(V.tensor_tensor(mrs2[:, 0:NSA], b[:, NPR:T], mod[:, 16 + m, 1:9], ALU.mult))
                V.tensor_tensor(xT[:, m, NPR:T], xT[:, m, NPR:T], mrs2[:, 0:NSA], ALU.add).then_inc(stage("out_evac"), 1)
                dve.wait_ge(stage("out_evac"), 17 + m)
            norm_mod(1, xT[:, :, :], hT[:, :, :], 32, 24, S_NFFN, mrs2[:, :], modA2[:, :, :])
            dve.wait_ge(*once("logits"))
            link(V.memset(lg[:, :, :], 0.0))
            for p_ in pre:
                link(V.memset(p_[:, :, :], 0.0))
            br = small[:, S_BR:S_BR + NE]
            link(V.tensor_tensor(lg[:, 0:2, :], bank[5][:, 0:64].rearrange("p (i e) -> p i e", i=2), br.unsqueeze(1).to_broadcast([P, 2, NE]), ALU.add))
            link(V.tensor_tensor(lg[0:NSA, 2, :], bank[5][0:NSA, 64:96], br[0:NSA, :], ALU.add))
            for i in range(3):
                link(V.max(v8[:, i, :], lg[:, i, :]))
            V.tensor_scalar(rst[:, 0, :], v8[:, :, 0], -1.0, None, ALU.mult).then_inc(once("v8_ready")[0], 1)
            fourth = v8[:, :, 3:4].to_broadcast([P, 3, NE])
            link(V.tensor_tensor(sel[:, :, :], lg[:, :, :], fourth, ALU.is_gt))
            link(V.tensor_tensor(eqm[:, :, :], lg[:, :, :], fourth, ALU.is_equal))
            link(V.tensor_reduce(rst[:, 1, :], sel[:, :, :], AX, ALU.add))
            link(V.tensor_scalar(rst[:, 1, :], rst[:, 1, :], -1.0, 4.0, ALU.mult, ALU.add))
            link(V.tensor_copy(pre[0][:, :, 16:48], eqm[:, :, :]))
            for i, s in enumerate((1, 2, 4, 8, 16)):
                a, b = pre[i % 2], pre[(i + 1) % 2]
                link(V.tensor_tensor(b[:, :, 16:48], a[:, :, 16:48], a[:, :, 16 - s:48 - s], ALU.add))
            link(V.tensor_tensor(pre[0][:, :, 16:48], pre[1][:, :, 16:48], rst[:, 1, :].unsqueeze(2).to_broadcast([P, 3, NE]), ALU.is_le))
            link(V.tensor_tensor(eqm[:, :, :], eqm[:, :, :], pre[0][:, :, 16:48], ALU.mult))
            V.tensor_tensor(sel[:, :, :], sel[:, :, :], eqm[:, :, :], ALU.add).then_inc(stage("sel_ready"), 1)
            dve.wait_ge(stage("sel_ready"), 1)
            dve.wait_ge(stage("route_exp"), 3)
            link(V.tensor_tensor(ex[:, :, :], ex[:, :, :], sel[:, :, :], ALU.mult))
            link(V.tensor_reduce(rst[:, 2, :], ex[:, :, :], AX, ALU.add))
            link(V.reciprocal(rst[:, 3, :], rst[:, 2, :]))
            V.tensor_tensor(gate[:, :, :], ex[:, :, :], rst[:, 3, :].unsqueeze(2).to_broadcast([P, 3, NE]), ALU.mult).then_inc(stage("sel_ready"), 1)
            dve.wait_ge(stage("route"), 1)
            link(V.tensor_copy(cntc[0:NE, 4:5], bank[7][0:NE, 0:1]))
            link(V.tensor_scalar(cntc[0:NE, 0:1], cntc[0:NE, 4:5], 0.0, None, ALU.is_gt))
            for i in range(1, 5):
                ins = V.scalar_tensor_tensor(cntc[0:NE, 0:1], cntc[0:NE, 4:5], float(SLOT * i), cntc[0:NE, 0:1], ALU.is_gt, ALU.add)
                if i < 4:
                    link(ins)
                else:
                    ins.then_inc(stage("blocks"), 1)
            dve.wait_ge(stage("blocks"), 1)
            dve.wait_ge(stage("route"), 2)
            link(V.tensor_copy(cntc[0:NE, 1:2], bank[7][0:NE, 1:2]))
            link(V.tensor_tensor(cntc[0:NE, 2:3], cntc[0:NE, 1:2], cntc[0:NE, 0:1], ALU.add))
            link(V.tensor_scalar(cntc[0:NE, 3:4], cntc[0:NE, 1:2], float(SLOT), 1.0, ALU.mult, ALU.add))
            jrow = con[0:NE, C_J:C_J + NJ1]
            link(V.tensor_scalar(ge1[0:NE, :], jrow, cntc[0:NE, 1:2], None, ALU.is_ge))
            V.scalar_tensor_tensor(e1h[0:NE, :], jrow, cntc[0:NE, 2:3], ge1[0:NE, :], ALU.is_lt, ALU.mult).then_inc(once("e1h_ready")[0], 1)
            link(V.tensor_copy(maskT[0:NE, :], bank[4][0:NE, 0:T]))
            link(V.tensor_copy(gateT[0:NE, :], bank[0][0:NE, 0:T]))
            V.scalar_tensor_tensor(m1T[0:NE, :], bank[6][0:NE, 0:T], cntc[0:NE, 3:4], maskT[0:NE, :], ALU.add, ALU.mult).then_inc(once("m1_ready")[0], 1)
            dve.wait_ge(stage("route"), 3)
            link(V.tensor_copy(items[0:1, 1:1 + NJ1], bank[7][0:1, 8:8 + NJ1]))
            V.tensor_copy(items[0:1, 0:1], bank[7][0:1, 2:3]).then_inc(once("items_ready")[0], 1)
            dve.wait_ge(stage("route"), 4)
            for i, n in ((0, P), (1, P), (2, NSA)):
                link(V.tensor_tensor(rr[0:n, i, :], bank[1][0:n, NJ1 * i:NJ1 * (i + 1)], con[0:n, C_J64:C_J64 + NJ1], ALU.subtract))
                ins = V.tensor_copy(gg[0:n, i, :], bank[2][0:n, NJ1 * i:NJ1 * (i + 1)])
                if i < 2:
                    link(ins)
                else:
                    ins.then_inc(stage("rg_copied"), 1)
            dve.wait_ge(stage("rg_copied"), 1)
            dve.wait_ge(*once("items_ready"))
            moe_vector(dve, link)
            for m in range(KD):
                link(V.scalar_tensor_tensor(xT[:, m, 0:NPR], acc[:, m, 0:NPR], mod[:, 40 + m, 0:1], xT[:, m, 0:NPR], ALU.mult, ALU.add))
            link(V.tensor_tensor(acc[:, :, NPR:T], acc[:, :, NPR:T], mod[:, 40:48, 1:9], ALU.mult))
            V.tensor_tensor(xT[:, :, NPR:T], xT[:, :, NPR:T], acc[:, :, NPR:T], ALU.add).then_inc(once("x2_ready")[0], 1)
            norm_mod(2, xT[:, :, :], yout[:, :, :], 56, 48, S_NFIN, mrs2[:, :], modA2[:, :, :])

        @block.gpsimd
        def _(pool):
            pool.wait_ge(h_ready, 1)
            pool.wait_ge(silu_done, CONVT + 1)
            pool.wait_ge(proj_evac, CONVT)
            pool.dma_start(t["o_convp"], convp[:, :, :]).then_inc(stored, 16)
            pool.dma_start(t["o_convs"], samp[:, :, :, :]).then_inc(stored, 16)
            pool.wait_ge(stage("egB_ready"), 1)
            for g in range(2):
                pool.wait_ge(slot_in[(SSM + g) % RING], arrive[SSM + g])
                S = ssm_view[g].rearrange("p h b v -> p (h b) v")
                nc.gpsimd.tensor_tensor(S, S, egB[:, 32 * g:32 * g + 32].unsqueeze(2).to_broadcast([P, 32, P]), ALU.mult).then_inc(stage("decayed"), 1)
            pool.wait_ge(stage("gd_out"), 4)
            nc.gpsimd.memset(krow[:, :, :, :], 0.0)
            nc.gpsimd.memset(x32[:, :, :], 0.0).then_inc(once("x32_zero")[0], 1)
            pool.dma_start(t["o_ssmp"], Sst[:, :, :]).then_inc(stage("ssmp_stored"), 16)
            for i in range(2):
                pool.wait_ge(stage("snew"), 2 * i + 2)
                pool.wait_ge(stage("oss_ready"), 2)
                pool.dma_start(t["o_ssms"][i, :, :], ring[(SSM + i) % RING][:, :]).then_inc(stage(f"ssm_stored{i}"), 16)
            pool.wait_ge(*once("kpe_rot"))
            pool.dma_start(t["o_kpe"], kpeT[0:ROPE, :]).then_inc(stored, 16)
            pool.wait_ge(stage("lat_normed"), 2)
            pool.dma_start(t["o_lat"], latT[:, :, :]).then_inc(stored, 16)
            pool.wait_ge(stage("pa_ready"), 8)
            nc.gpsimd.memset(regC[:, 2376:4424], 0.0)
            nc.gpsimd.memset(regC[:, mlat:mlat + 512], 0.0).then_inc(once("att_zero")[0], 1)
            pool.wait_ge(stage("merged"), KD)
            nc.gpsimd.memset(acc[:, :, :], 0.0).then_inc(acc_added, 1)
            pool.wait_ge(h_ready, 3)
            pool.dma_start(t["o_y"], yout[:, :, :]).then_inc(stored, 16)
            pool.wait_ge(stored, 80)
            pool.wait_ge(stage("ssm_stored0"), 16)
            pool.wait_ge(stage("ssm_stored1"), 16)
            pool.wait_ge(stage("ssmp_stored"), 16)


Q0, Z0, B0, CQ0, CKV0, KPE0, GA0, GB0 = 0, 3072, 4096, 4112, 4624, 5136, 5200, 6224


def wp_index(n):
    if n < SSM:
        return n
    return n - 2 - sum(c < n for c in KV_OF)


def lay_out(i):
    f = np.float32

    def cols(w, c0, n):
        w = w[:, c0:c0 + 512 * n].reshape(-1, P, n, 512)
        return w.transpose(2, 1, 0, 3).reshape(n, P, -1)

    def vec(v):
        return v.reshape(-1, P).T

    w_in = i["w_in"][0]
    w_uq = i["w_uq"][0].reshape(LORA, P, H, 192)
    half = np.zeros((P, 2048), f)
    uqr = w_uq[..., 128:].reshape(LORA, P, 512).transpose(1, 0, 2).reshape(P, 2048)
    uk = i["w_uk"][0].reshape(H, LORA, P, P)
    uv = i["w_uv"][0].reshape(H, LORA, P, P).transpose(2, 1, 0, 3).reshape(1, P, CH)
    wpre = np.concatenate([
        cols(i["w_ada"][0], 0, 4), cols(w_in, Q0, 6), cols(i["w_ada"][0], 2048, 8), cols(i["w_ada_final"], 0, 4),
        cols(w_in, Z0, 2),
        cols(w_in, CQ0, 1), cols(w_in, CKV0, 1),
        w_uq[..., :128].reshape(LORA, P, 1024).transpose(1, 0, 2).reshape(1, P, CH),
        np.concatenate([uqr, half], 1)[None],
        uk.transpose(2, 1, 0, 3).reshape(1, P, CH), uv,
        i["w_uk"][0].transpose(2, 0, 1).reshape(1, P, CH),
        cols(i["w_o_gdn"][0], 0, 2), cols(w_in, GA0, 2), cols(w_in, GB0, 2), uv, cols(i["w_o_mla"][0], 0, 2),
        cols(i["w_out"][0], 0, 2)], 0)
    n = np.arange(P)
    con = np.zeros((P, NCONST), f)
    con[:, C_ID:C_ID + P] = np.eye(P)
    con[:, C_ONE:C_ONE + P] = 1
    con[:, C_U:C_U + P] = n[:, None] <= n[None]
    con[:, C_STR:C_STR + P] = n[:, None] < n[None]
    con[:, C_PERM:C_PERM + P] = n[:, None] == (n[None] ^ 32)
    for lv in range(LEVELS):
        b = 1 << lv
        con[:, C_LEV + lv * P:C_LEV + (lv + 1) * P] = ((n[:, None] // (2 * b) == n[None] // (2 * b))
                                                     & (n[:, None] // b % 2 == 0) & (n[None] // b % 2 == 1))
    inv = f(10000.0) ** (-np.arange(32, dtype=f) / f(32))
    pos = np.concatenate([np.arange(NPR), np.full(NSA, PAGES * P)]).astype(f)
    ang = inv[n % 32][:, None] * pos[None]
    con[:, C_COS:C_COS + T] = np.cos(ang)
    con[:, C_SIN:C_SIN + T] = np.sin(ang) * np.where(n % 64 < 32, -1, 1)[:, None]
    low = np.where(n[None] <= n[:, None], 0, NEG)
    con[:, C_NEG:C_NEG + P] = low
    con[:, C_NEG + 256:C_NEG + 384] = low
    con[:, C_IOTA:C_IOTA + SLOT] = np.arange(SLOT)
    con[:, C_J:C_J + NJ1] = np.arange(NJ1)
    con[:, C_J64:C_J64 + NJ1] = SLOT * np.arange(NJ1) + 1
    con[:, C_E] = n
    con[:, C_EPS] = EPS
    con[:, C_OWN:C_OWN + NSA] = n[:, None] % 32 == np.arange(NSA)[None]
    con[0:2, C_TWO:C_TWO + P] = np.arange(2)[:, None] == n[None] // 64
    con[:, C_B8:C_B8 + 16] = np.where(np.arange(16)[None] // 8 * 4 + n[:, None] // 32 == np.arange(16)[None] % 8, 0, NEG)
    small = np.empty((P, NSMALL), f)
    small[:, S_NMIX:S_NMIX + 8] = vec(i["norm_mix_w"])
    small[:, S_NFFN:S_NFFN + 8] = vec(i["norm_ffn_w"])
    small[:, S_NFIN:S_NFIN + 8] = vec(i["norm_final_w"])
    small[:, S_NQ:S_NQ + 4] = vec(i["q_norm_w"])
    small[:, S_NKV:S_NKV + 4] = vec(i["kv_norm_w"])
    small[:, S_NGDN:S_NGDN + 1] = vec(i["gdn_norm_w"])
    small[:, S_BADA:S_BADA + 64] = np.concatenate([vec(i["b_ada"]), vec(i["b_ada_final"])], 1)
    small[:, S_ALOG:S_ALOG + 8] = i["A_log"]
    small[:, S_DT:S_DT + 8] = i["dt_bias"]
    small[:, S_BR:S_BR + NE] = i["b_router"]
    small[:, S_CW:S_CW + CONVT * 4] = i["conv_w"][0].reshape(CONVT, P, 4).transpose(1, 0, 2).reshape(P, -1)
    kpe = w_in[:, KPE0:KPE0 + ROPE]
    small[:, S_WSM:S_WSM + KD * WSM] = np.concatenate([w_in[:, B0:B0 + 16], kpe, i["w_router"][0]],
                                                      1).reshape(KD, P, WSM).transpose(1, 0, 2).reshape(P, -1)
    c = np.concatenate([i["c_prompt"], i["c_sample"], np.zeros((23, D), f)], 0)
    small[:, S_CT:] = c.T.reshape(KD, P, 32).transpose(1, 0, 2).reshape(P, -1)
    x = np.concatenate([i["x_prompt"][0], i["x_sample"][:, 0]], 0)
    conv = np.zeros((P, CONVT, 4, NSA), f)
    conv[:, :, 0:3] = i["state_conv"][0].reshape(NSA, 3, CONVT, P).transpose(3, 2, 1, 0)
    kv = i["cache_kv"][0]
    return {
        "small": small,
        "biases": np.concatenate([i["b_gu"][0].reshape(NE, 2, 2, 512), i["b_dn"][0].reshape(NE, 1, 2, 512)],
                                 1).transpose(0, 2, 1, 3).reshape(NE, 2, -1),
        "con": con,
        "xT": x.T.reshape(KD, P, T).transpose(1, 0, 2),
        "convT": conv,
        "pages": i["page_table"].reshape(1, -1),
        "wpre": wpre,
        "ssm": i["state_ssm"][0].reshape(NSA, 2, 4, P, P).transpose(1, 3, 2, 0, 4).reshape(2, P, CH),
        "kvT": kv.reshape(NPHYS, P, LORA, P).transpose(0, 3, 2, 1).reshape(NPHYS, P, 512),
        "kv": kv,
        "peT": i["cache_pe"][0].transpose(0, 2, 1),
        "w_gu": i["w_gu"][0],
        "w_dn": i["w_dn"][0],
    }


OUTS = {
    "o_y": (P, KD, T), "o_lat": (P, LORA, T), "o_kpe": (ROPE, T), "o_ssmp": (P, 2, 512),
    "o_convp": (P, CONVT, 3), "o_ssms": (2, P, CH), "o_convs": (P, CONVT, 4, NSA),
}


def kernel(**inputs):
    import concourse.bacc as bacc
    from concourse.bass_utils import run_bass_kernel_spmd

    nc = bacc.Bacc("TRN2", target_bir_lowering=False, num_devices=1)
    arrays = {k: np.ascontiguousarray(v) for k, v in lay_out({k: np.asarray(v) for k, v in inputs.items()}).items()}
    t = {k: nc.dram_tensor(k, v.shape, mybir.dt.from_np(v.dtype), kind="ExternalInput").ap() for k, v in arrays.items()}
    for k, shape in OUTS.items():
        t[k] = nc.dram_tensor(k, shape, F32, kind="ExternalOutput").ap()
    build_program(nc, t)
    r = run_bass_kernel_spmd(nc, [arrays], core_ids=[0]).results[0]

    def rows(v):
        return v.transpose(2, 1, 0).reshape(v.shape[2], -1)
    y, lat, kpe = rows(r["o_y"]), rows(r["o_lat"]), r["o_kpe"].T
    ssmp = r["o_ssmp"].reshape(P, H, P).transpose(1, 0, 2)
    convp = r["o_convp"].transpose(2, 1, 0).reshape(1, 1, 3, -1)
    ssms = r["o_ssms"].reshape(2, P, 4, NSA, P).transpose(3, 0, 2, 1, 4).reshape(1, NSA, H, P, P)
    convs = r["o_convs"][:, :, 1:4, :].transpose(3, 2, 1, 0).reshape(1, NSA, 3, -1)
    c = np.ascontiguousarray
    return (c(y[None, :NPR]), c(y[NPR:, None]), c(lat[None, None, :NPR]), c(kpe[None, None, :NPR]), c(ssmp[None, None]),
            c(convp), c(lat[None, NPR:, None]), c(kpe[None, NPR:, None]), c(ssms), c(convs))
```

```python
from contextlib import ExitStack

import numpy as np
import concourse.bass as bass
from concourse import mybir

F32 = mybir.dt.float32
I32 = mybir.dt.int32
ALU = mybir.AluOpType
ACT = mybir.ActivationFunctionType
AX = mybir.AxisListType.X
AXY = mybir.AxisListType.XY

P = 128
D = 1024
KD = D // P
NPR = 256
NSA = 8
T = NPR + NSA
H = 8
CONVT = 3 * H
RING = 6
CH = 4096
PAGES = 8
NPHYS = 80
LORA = 4
ROPE = 64
SCALE = (128 + 64) ** -0.5
EPS = 1e-6
NEG = -1e30
NE = 32
SLOT = 64
NJ = 48
NJ1 = NJ + 1
LEVELS = 7
MOD_PRE = 10
L2_BANKS = (4, 5, 0, 1)
VALUE_BANKS = (2, 3, 0, 1)
MOD_L2 = 7
MOD_GDN = 3

C_ID, C_ONE, C_EPS = 0, 128, 256
C_FIRST = C_EPS + 1
C_U = C_FIRST
C_STR, C_PERM = C_U + P, C_U + 2 * P
C_LEV = C_PERM + P
C_COS = C_LEV + LEVELS * P
C_SIN = C_COS + T
C_NEG = C_SIN + T
C_IOTA = C_NEG + 384
C_J = C_IOTA + SLOT
C_J64 = C_J + NJ1
C_E = C_J64 + NJ1
C_B8 = C_E + 1
C_TWO = C_B8 + 16
C_OWN = C_TWO + P
C_COL = C_OWN + NSA
NCONST = C_COL + 4 * H - 1

S_NMIX, S_NFFN, S_NFIN = 0, 8, 16
S_NQ, S_NKV, S_NGDN = 24, 28, 32
S_BADA = 33
S_ALOG = S_BADA + 64
S_DT = S_ALOG + 8
S_BR = S_DT + 8
S_CW = S_BR + NE
S_WSM = S_CW + CONVT * 4
WSM = 16 + ROPE + 32
S_CT = S_WSM + KD * WSM
NSMALL = S_CT + KD * 32

ADA, QKV, ADA2, SSM, ZZ, CQ, CKV, UQN, UQR, UV, UK, UKT = 0, 4, 10, 22, 24, 26, 27, 28, 29, 30, 31, 32
KV_AT = (UKT + 1, UKT + 7, UKT + 13, UKT + 19)
OG, GA, GB = KV_AT[0] + 4, KV_AT[1] + 4, KV_AT[2] + 4
UV2 = KV_AT[3] + 4
OM, WO = UV2 + 1, UV2 + 3
NCH = WO + 2
assert NCH % RING == 0


def ada_chunk(i):
    return ADA + i if i < 4 else ADA2 + i - 4


def kv_chunk(b, what):
    return KV_AT[2 * (b // 4) + what] + b % 4


KV_OF = {kv_chunk(b, what): (b, what) for b in range(NSA) for what in range(2)}


def build_program(nc, t):
    ctx = ExitStack()
    with ctx:
        def sb(name, shape, dt=F32):
            return ctx.enter_context(nc.sbuf_tensor(name, shape, dt))

        def sem(name):
            return ctx.enter_context(nc.semaphore(name))

        ring = [sb(f"ring{i}", [P, CH]) for i in range(RING)]
        con = sb("con_sb", [P, NCONST])
        small = sb("small_sb", [P, NSMALL])
        xT = sb("xT_sb", [P, KD, T])
        hT = sb("hT", [P, KD, T])
        mod = sb("mod", [P, 64, 9])
        regA = sb("regA", [P, CONVT * T])
        regB = sb("regB", [P, H, T])
        samp = regB[:, 0:3, :].rearrange("p a b -> p (a b)")[:, 0:CONVT * 32].rearrange("p (m j b) -> p m j b", m=CONVT, j=4)
        regC = sb("regC", [P, 10240])
        pages_sb = sb("pages_sb", [1, NSA * PAGES], I32)
        banks = ctx.enter_context(nc.psum_tensor("banks", [P, 8, 512], F32))
        bank = [banks[:, i, :] for i in range(8)]

        ident = con[:, C_ID:C_ID + P]
        ones = con[:, C_ONE:C_ONE + P]
        upto = con[:, C_U:C_U + P]
        before = con[:, C_STR:C_STR + P]
        perm = con[:, C_PERM:C_PERM + P]
        cosT = con[:, C_COS:C_COS + T]
        sinT = con[:, C_SIN:C_SIN + T]
        neg384 = con[:, C_NEG:C_NEG + 384]
        cT = small[:, S_CT:S_CT + KD * 32].rearrange("p (k c) -> p k c", k=KD)
        wsm = small[:, S_WSM:S_WSM + KD * WSM].rearrange("p (k c) -> p k c", k=KD)
        convw = small[:, S_CW:S_CW + CONVT * 4].rearrange("p (m j) -> p m j", j=4)

        qkvT = regA[:, :].rearrange("p (m t) -> p m t", t=T)
        oG = regB
        def cut(reg, at, *shape):
            n = 1
            for s in shape:
                n *= s
            v = reg[:, at:at + n]
            if len(shape) == 2:
                v = v.rearrange("p (a b) -> p a b", b=shape[1])
            if len(shape) == 3:
                v = v.rearrange("p (a b c) -> p a b c", b=shape[1], c=shape[2])
            return v
        upad = cut(regC, 0, 3, 3 + NPR)
        sigb = cut(regC, 800, 2, T)
        sqb = cut(regC, 1400, 2, T)
        sq_s = cut(regC, 1400, 2 * H, NSA)
        rsb = cut(regC, 2900, 2, T)
        modA = cut(regC, 2300, KD, 9)
        convp = sb("convp", [P, CONVT, 3])
        smt = cut(regC, 2500, 2, CONVT, NSA)
        mrow = sb("mrow", [P, 2, P])
        bgm = sb("bgm", [NSA, H * NSA])
        egB = sb("egB", [P, H * NSA])
        beta_tok = sb("beta_tok", [P, 3, H])
        g_tok = sb("g_tok", [P, 3, H])
        G4 = 4 * P
        AT = cut(regC, 0, 2, G4)
        Xm = cut(regC, 1024, 2, G4)
        XTm = cut(regC, 2048, 2, G4)
        LTm = cut(regC, 3072, 2, G4)
        Aqk = cut(regC, 4096, 2, G4)
        qg = cut(regC, 5120, 2, G4)
        VB = cut(regC, 6144, 2, G4)
        KBG = cut(regC, 7168, 2, G4)
        K2 = cut(regC, 8192, 2, G4)
        Sst = cut(regC, 9216, 2, G4)
        gcol = sb("gcol", [P, 5, H])
        gsc = sb("gsc", [P, 3, 3, H])

        latT = cut(regC, 0, LORA, T)
        cqT = cut(regC, 1056, LORA, T)
        kpeT = cut(regC, 2112, T)
        vtok = cut(regC, 2376, 2, H * P)
        oM = cut(regC, 4424, H, T)
        mlat = 6536
        msc = [cut(regC, mlat + 384 * i, 384) for i in range(2)]
        mp = [cut(regC, mlat + 768 + 384 * i, 384) for i in range(2)]
        mpT = [cut(regC, mlat + 1536 + 384 * i, 384) for i in range(2)]
        msq = cut(regC, mlat, 2, T)
        ors = cut(regC, 2400, T)
        mrs = cut(regC, mlat + 600, 2, T)
        mstat = cut(regC, mlat + 2304, 2, 8)
        qlatT = cut(regC, 2376, LORA * NSA * 32).rearrange("p (k b h) -> p k b h", k=LORA, b=NSA)
        olat = cut(regC, 3400, LORA * H * 32).rearrange("p (k h b) -> p k h b", k=LORA, h=H)
        qnS = cut(regC, mlat, H, 32)
        qpeS = cut(regC, mlat + 256, NSA, 32)
        qrow = cut(regC, mlat + 512, 2, 512)
        sstat = cut(regC, mlat + 1536, 2, 8)
        ps_ = [cut(regA, 2112 + 1032 * i, 1032) for i in range(2)]
        pT = cut(regA, 4176, PAGES, P)
        orow = cut(regC, 1056, 512)
        osr = cut(regC, 1568, 2 * P)
        pT9 = cut(regC, 1824, P)
        lat_tok = cut(regC, 8100, 512)
        qnT = cut(regA, 0, H, T)
        qpeT = cut(regA, 2112, 4, T)
        knT = cut(regA, 3168, H, NPR)
        peT = [cut((regA, regC)[i % 2], (5240, 9000)[i % 2], 1024)[ROPE * (i // 2):ROPE * (i // 2 + 1), :] for i in range(4)]
        yA = cut(regA, 0, KD, T)
        gB = regB
        gsig = cut(regC, mlat + 512, 2, T)
        h2tok = cut(regC, 0, 3, KD, P)
        acc = regB
        yout = cut(regC, 0, KD, T)
        lg = cut(regA, 0, 3, NE)
        ex = cut(regA, 96, 3, NE)
        sel = cut(regA, 192, 3, NE)
        eqm = cut(regA, 288, 3, NE)
        pre = [cut(regA, 384 + 144 * i, 3, 48) for i in range(2)]
        v8 = cut(regA, 672, 3, 8)
        rst = cut(regA, 700, 4, 3)
        gate = cut(regA, 712, 3, NE)
        maskT = cut(regA, 808, T)
        gateT = cut(regA, 1072, T)
        m1T = cut(regA, 1336, T)
        cntc = cut(regA, 1600, 8)
        e1h = cut(regA, 1608, NJ1)
        ge1 = cut(regA, 1657, NJ1)
        rr = cut(regA, 1706, 3, NJ1)
        gg = cut(regA, 1853, 3, NJ1)
        self_ = cut(regA, 2000, 3, SLOT)
        selg = cut(regA, 2192, 3, 2, SLOT)
        selT = cut(regA, 2576, T)
        gtok = cut(regA, 2840, 512)
        hg = cut(regA, 3352, 4, P)
        gmn = cut(regA, 3864, 512)
        upc = cut(regA, 4376, 512)
        sgm = cut(regA, 4888, 512)
        act_ = cut(regA, 5400, 512)
        actT = cut(regC, 7000, 4, P)
        ytok = cut(regC, 7512, 512)
        brow = cut(regC, 8100, 3 * 512)
        items = sb("items", [1, 64], I32)
        msq2 = cut(regC, 4000, KD, T)
        mrs2 = cut(regC, 6200, T)

        x32 = cut(regC, 0, CONVT, 32)
        krow = cut(regC, 4724, 4, 2, P)
        ksr = cut(regC, 1024, 2, P)
        vnr = cut(regC, 1280, 2, P)
        betac = cut(regC, 1536, 2)
        vnm = cut(regC, 1600, 2, NSA * P)
        stmp = cut(regC, 3700, NSA * P)
        zsig = cut(regC, 7300, 2, T)

        rot = cut(regC, 8000, T)
        cumc = sb("cumc", [P, 2, 16])
        modA2 = cut(regC, 6500, KD, 9)

        inputs_in = sem("inputs_in")
        slot_in = [sem(f"slot_in{i}") for i in range(RING)]
        dve_line = sem("dve_line")
        act_line = sem("act_line")
        root_ready = sem("root_ready")
        sq_ready = sem("sq_ready")
        ss_ready = sem("ss_ready")
        mod_ready = sem("mod_ready")
        mod_evac = sem("mod_evac")
        mod_row = sem("mod_row")
        mod_turned = sem("mod_turned")
        h_ready = sem("h_ready")
        proj_ready = sem("proj_ready")
        proj_evac = sem("proj_evac")
        ab_ready = sem("ab_ready")
        conv_done = sem("conv_done")
        sig_done = sem("sig_done")
        silu_done = sem("silu_done")
        l2sq = sem("l2sq")
        l2ss = sem("l2ss")
        l2done = sem("l2done")
        ab_act = sem("ab_act")
        bg_done = sem("bg_done")
        tr_ready = sem("tr_ready")
        tr_evac = sem("tr_evac")
        stored = sem("stored")

        names = {}

        def stage(name):
            if name not in names:
                names[name] = sem(name)
            return names[name]

        once_steps = {
            "pe_steps": ("ab_made", "cum_ready", "oss_turned", "kpe_ready", "kpe_turned", "ltok_ready", "qlat_ready", "os_ready", "os_turned", "logits_T", "logits"),
            "act_steps": ("x32_ready", "krow_copied", "kpe_copied", "qns_ready", "osr_copied", "os_copied"),
            "dve_steps": ("upad_zero", "cum_read", "kpe_rot", "logits_copied", "v8_ready", "e1h_ready", "m1_ready", "items_ready"),
            "pool_steps": ("x32_zero", "krow_zero", "att_zero"),
        }

        def once(name):
            for line, steps in once_steps.items():
                if name in steps:
                    return stage(line), steps.index(name) + 1

        block = ctx.enter_context(nc.Block())

        used = {}
        for i in range(16):
            used[ada_chunk(i)] = (mod_ready, i + 1)
        for i in range(6):
            used[QKV + i] = (proj_ready, 4 * (i + 1))
        for i in range(2):
            used[SSM + i] = (stage(f"ssm_stored{i}"), 16)
        for i in range(2):
            used[ZZ + i] = (stage("z_ready"), 4 * (i + 1))
        used[CQ] = (stage("lat_ready"), 4)
        used[CKV] = (stage("lat_ready"), 8)
        used[UQN] = (stage("q_ready"), 8)
        used[UQR] = (stage("q_ready"), 12)
        used[UK] = (stage("kn_ready"), 8)
        used[UV] = (stage("vt_ready"), 4)
        used[UKT] = once("qlat_ready")
        for b in range(NSA):
            used[kv_chunk(b, 0)] = (stage("st_ready"), b // 4 + 1)
            used[kv_chunk(b, 1)] = (stage("ol_ready"), b // 4 + 1)
        used[UV2] = once("os_ready")
        for i in range(2):
            used[OG + i] = (stage("out_ready"), 4 * (i + 1))
            used[GA + i] = (stage("out_ready"), 8 + 4 * (i + 1))
            used[GB + i] = (stage("out_ready"), 16 + 4 * (i + 1))
            used[OM + i] = (stage("out_ready"), 24 + 4 * (i + 1))
            used[WO + i] = (stage("out_ready"), 32 + 4 * (i + 1))
        arrive = {}
        count = [0] * RING
        for n in range(NCH):
            count[n % RING] += 16 * (PAGES if n in KV_OF else 1)
            arrive[n] = count[n % RING]
        moe_base = list(count)

        def weights(pe, n):
            pe.wait_ge(slot_in[n % RING], arrive[n])
            return ring[n % RING][:, :].rearrange("p (k c) -> p k c", c=512)

        pe_mm = nc.tensor.matmul

        def doubling(c, lv, g):
            return (c * (LEVELS - 1) + lv - 1) * 2 + g + 1

        def chunk_k(n, m, k):
            return ring[n % RING][:, k * 512 + m * P:k * 512 + (m + 1) * P]

        moe_read = sem("moe_read")
        gu_ready = sem("gu_ready")
        sel_new = sem("sel_new")
        selg_new = sem("selg_new")
        gathered = sem("gathered")
        gtok_copied = sem("gtok_copied")
        g_turned = sem("g_turned")
        hg_ready = sem("hg_ready")
        selT_turned = sem("selT_turned")
        selT_copied = sem("selT_copied")
        gmin_ready = sem("gmin_ready")
        sig_ready = sem("sig_ready")
        act_ready = sem("act_ready")
        a_turned = sem("a_turned")
        actT_ready = sem("actT_ready")
        ytok_copied = sem("ytok_copied")
        scattered = sem("scattered")
        acc_added = sem("acc_added")
        moe_line = sem("moe_line")
        brow_in = sem("brow_in")
        wgu = t["w_gu"].rearrange("e (p k) n -> e p (k n)", p=P)
        wdn = t["w_dn"].rearrange("e (m p) n -> e p m n", p=P)
        tok_tiles = ((0, P), (1, P), (2, NSA))
        HALF = D // 2
        both = con[0:2, C_TWO:C_TWO + P]

        def number_of_items(eng):
            eng.wait_ge(*once("items_ready"))
            return eng.value_load(items[0:1, 0:1], min_val=1, max_val=NJ)

        def for_items(eng, K, first, item):
            with eng.Fori(first, NE) as j:
                with eng.If(j < K):
                    item(j)
            with eng.If(K > NE):
                with eng.Fori(NE, NJ) as j:
                    with eng.If(j < K):
                        item(j)

        def moe_loads(sp):
            def load(c, e):
                if c < 4:
                    src = wgu[bass.ds(e, 1), :, CH * c:CH * (c + 1)].rearrange("a p n -> p (a n)")
                    sp.dma_start(ring[c][:, :], src).then_inc(slot_in[c], 16)
                else:
                    src = wdn[bass.ds(e, 1), :, 4 * (c - 4):4 * (c - 3), :].rearrange("a p m n -> p (a m) n")
                    sp.dma_start(ring[c][:, :].rearrange("p (m n) -> p m n", m=4), src).then_inc(slot_in[c], 16)

            def load_bias(e):
                sp.dma_start(brow[0:2, :], t["biases"][bass.ds(e, 1), :, :].rearrange("a h n -> h (a n)")).then_inc(brow_in, 16)

            for c in range(RING):
                sp.wait_ge(*used[NCH - RING + c])
                load(c, 0)
            K = number_of_items(sp)
            load_bias(0)
            def item(j):
                e = sp.value_load(items[0:1, bass.ds(j + 1, 1)], min_val=0, max_val=NE - 1)
                for c in range(RING):
                    sp.wait_ge(moe_read, j * 6 + (c - 5))
                    load(c, e)
                load_bias(e)

            for_items(sp, K, 1, item)

        def moe_tensor(pe):
            K = number_of_items(pe)

            def gather(n):
                pe.wait_ge(sel_new, n)
                for i, r in tok_tiles:
                    for y in range(2):
                        mm = pe_mm(bank[2][SLOT * y:SLOT * (y + 1), :], lhsT=self_[0:r, i, :],
                                   rhs=h2tok[0:r, i, 4 * y:4 * y + 4, :].rearrange("p k c -> p (k c)"),
                                   start=(i == 0), stop=(i == 2), skip_group_check=True)
                mm.then_inc(gathered, 1)

            def turn_gathered(n):
                pe.wait_ge(gtok_copied, n)
                for q in range(4):
                    mm = pe_mm(bank[3][:, P * q:P * (q + 1)], lhsT=gtok[:, P * q:P * (q + 1)], rhs=ident, start=True, stop=True)
                mm.then_inc(g_turned, 1)

            def scatter(j):
                pe.wait_ge(ytok_copied, j + 1)
                pe.wait_ge(selT_copied, j + 1)
                for q in range(4):
                    b = (6, 2)[q % 2]
                    if q >= 2:
                        pe.wait_ge(acc_added, j * 4 + q)
                    for y in range(2):
                        r = slice(SLOT * y, SLOT * (y + 1))
                        mm = pe_mm(bank[b + y][:, 0:T], lhsT=ytok[r, P * q:P * (q + 1)], rhs=selT[r, :], start=True, stop=True)
                    mm.then_inc(scattered, 1)

            pe.wait_ge(stage("rg_copied"), 1)
            gather(1)
            turn_gathered(1)
            def item(j):
                pe.wait_ge(hg_ready, j + 1)
                for c in range(4):
                    pe.wait_ge(slot_in[c], j * 16 + (moe_base[c] + 16))
                    for kk in range(2):
                        k = 2 * c + kk
                        for x in range(4):
                            mm = pe_mm(bank[x // 2][SLOT * (x % 2):SLOT * (x % 2 + 1), :],
                                       lhsT=hg[:, k % 4, SLOT * (k // 4):SLOT * (k // 4 + 1)],
                                       rhs=ring[c][:, 2048 * kk + HALF * x:2048 * kk + HALF * (x + 1)],
                                       start=(k == 0), stop=False, skip_group_check=True)
                    mm.then_inc(moe_read, 1)
                    if c == 0:
                        scatter(j)
                        pe.wait_ge(selg_new, j + 1)
                        for i, r in tok_tiles:
                            mm = pe_mm(bank[4][:, P * i:P * i + r], lhsT=selg[0:r, i, :, :].rearrange("p a s -> p (a s)"),
                                       rhs=ident[0:r, 0:r], start=True, stop=True)
                        mm.then_inc(selT_turned, 1)
                pe.wait_ge(brow_in, j * 16 + 16)
                for x in range(2):
                    pe_mm(bank[x][:, :], lhsT=both, rhs=brow[0:2, HALF * x:HALF * (x + 1)], start=False, stop=True,
                          skip_group_check=True).then_inc(gu_ready, 1)
                pe.wait_ge(acc_added, j * 4 + 5)
                gather(j + 2)
                pe.wait_ge(selT_copied, j + 2)
                pe.wait_ge(act_ready, j + 1)
                for y in range(2):
                    for q in (2 * y, 2 * y + 1):
                        mm = pe_mm(bank[4 - 2 * y][:, P * q:P * (q + 1)], lhsT=act_[:, P * q:P * (q + 1)], rhs=ident, start=True, stop=True)
                    mm.then_inc(a_turned, 1)
                    if y == 0:
                        turn_gathered(j + 2)
                for m in range(8):
                    c = 4 + m // 4
                    if m % 4 == 0:
                        pe.wait_ge(slot_in[c], j * 16 + (moe_base[c] + 16))
                    if m == 0:
                        pe.wait_ge(actT_ready, j * 2 + 1)
                    if m == 2:
                        pe.wait_ge(actT_ready, j * 2 + 2)
                    for y in range(2):
                        mm = pe_mm(bank[5][SLOT * y:SLOT * (y + 1), :], lhsT=actT[:, m % 4, SLOT * (m // 4):SLOT * (m // 4 + 1)],
                                   rhs=ring[c][:, D * (m % 4) + HALF * y:D * (m % 4) + HALF * (y + 1)],
                                   start=(m == 0), stop=False, skip_group_check=True)
                    if m == 3:
                        mm.then_inc(moe_read, 1)
                pe_mm(bank[5][:, :], lhsT=both, rhs=brow[0:2, 2 * HALF:3 * HALF], start=False, stop=True, skip_group_check=True).then_inc(moe_read, 1)

            for_items(pe, K, 0, item)
            scatter(K)

        def moe_scalar(act):
            A = nc.scalar.activation
            K = number_of_items(act)
            act.wait_ge(gathered, 1)
            A(gtok[:, :], bank[2][:, :], ACT.Copy).then_inc(gtok_copied, 1)
            act.wait_ge(g_turned, 1)
            A(hg[:, :, :], bank[3][:, :].rearrange("p (q s) -> p q s", q=4), ACT.Copy).then_inc(hg_ready, 1)
            def item(j):
                act.wait_ge(selT_turned, j + 1)
                A(selT[:, :], bank[4][:, 0:T], ACT.Copy).then_inc(selT_copied, 1)
                act.wait_ge(gmin_ready, j + 1)
                A(sgm[:, :], gmn[:, :], ACT.Sigmoid, scale=1.702).then_inc(sig_ready, 1)
                act.wait_ge(gathered, j + 2)
                A(gtok[:, :], bank[2][:, :], ACT.Copy).then_inc(gtok_copied, 1)
                for y in range(2):
                    act.wait_ge(a_turned, j * 2 + (y + 1))
                    A(actT[:, 2 * y:2 * y + 2, :], bank[4 - 2 * y][:, 256 * y:256 * (y + 1)].rearrange("p (q s) -> p q s", q=2),
                      ACT.Copy).then_inc(actT_ready, 1)
                    if y == 0:
                        act.wait_ge(g_turned, j + 2)
                        A(hg[:, :, :], bank[3][:, :].rearrange("p (q s) -> p q s", q=4), ACT.Copy).then_inc(hg_ready, 1)
                act.wait_ge(moe_read, j * 6 + 6)
                A(ytok[:, :], bank[5][:, :], ACT.Copy).then_inc(ytok_copied, 1)

            for_items(act, K, 0, item)

        LINKS = 2

        def moe_vector(dve, link):
            V = nc.vector
            K = number_of_items(dve)
            iota = con[:, C_IOTA:C_IOTA + SLOT]
            dve.wait_ge(acc_added, 1)
            V.memset(selT[:, :], 0.0).then_inc(selT_copied, 1)
            V.memset(ytok[:, :], 0.0).then_inc(ytok_copied, 1)

            def choose(col):
                for i, r in tok_tiles:
                    ins = V.tensor_scalar(self_[0:r, i, :], iota[0:r, :], rr[0:r, i, col], None, ALU.is_equal)
                return ins

            def add(j):
                for q in range(4):
                    b = (6, 2)[q % 2]
                    dve.wait_ge(scattered, j * 4 + (q + 1))
                    pair = acc[:, q::4, :]
                    V.tensor_tensor(pair, pair, banks[:, b:b + 2, 0:T], ALU.add).then_inc(acc_added, 1)

            choose(slice(0, 1)).then_inc(sel_new, 1)
            def item(j):
                n = [0]

                def after(ins):
                    n[0] += 1
                    ins.then_inc(moe_line, 1)
                    dve.wait_ge(moe_line, j * LINKS + n[0])

                dve.wait_ge(gathered, j + 1)
                choose(bass.ds(j + 1, 1)).then_inc(sel_new, 1)
                for i, r in tok_tiles:
                    ins = V.tensor_scalar(selg[0:r, i, :, :], iota[0:r, :].unsqueeze(1).to_broadcast([r, 2, SLOT]),
                                          rr[0:r, i, bass.ds(j, 1)], gg[0:r, i, bass.ds(j, 1)], ALU.is_equal, ALU.mult)
                ins.then_inc(selg_new, 1)
                add(j)
                dve.wait_ge(gu_ready, j * 2 + 1)
                V.tensor_scalar(gmn[:, :], bank[0][:, :], 7.0, None, ALU.min).then_inc(gmin_ready, 1)
                dve.wait_ge(gu_ready, j * 2 + 2)
                after(V.tensor_scalar(upc[:, :], bank[1][:, :], 7.0, -7.0, ALU.min, ALU.max))
                after(V.scalar_tensor_tensor(upc[:, :], upc[:, :], 1.0, gmn[:, :], ALU.add, ALU.mult))
                dve.wait_ge(sig_ready, j + 1)
                V.tensor_tensor(act_[:, :], upc[:, :], sgm[:, :], ALU.mult).then_inc(act_ready, 1)
                assert n[0] == LINKS

            for_items(dve, K, 0, item)
            add(K)
            dve.wait_ge(acc_added, K * 4 + 5)

        ssm_view = [ring[(SSM + i) % RING][:, :].rearrange("p (h b v) -> p h b v", h=4, b=NSA) for i in range(2)]

        @block.sync
        def _(sp):
            sp.dma_start(small[:, :], t["small"]).then_inc(inputs_in, 16)
            sp.dma_start(xT[:, :, :], t["xT"]).then_inc(inputs_in, 16)
            sp.dma_start(con[:, 0:C_FIRST], t["con"][:, 0:C_FIRST]).then_inc(inputs_in, 16)
            phys = {}

            def read_pages(samples):
                for b in samples:
                    phys[b] = [sp.value_load(pages_sb[0:1, b * PAGES + i:b * PAGES + i + 1], min_val=0, max_val=NPHYS - 1) for i in range(PAGES)]

            def load_rotary(b):
                if b >= 4:
                    sp.wait_ge(stage("pe_used"), b - 3)
                for i in range(PAGES):
                    sp.dma_start(peT[b % 4][:, P * i:P * i + P], t["peT"][bass.ds(phys[b][i], 1), :, :].rearrange("a p c -> p (a c)")
                                 ).then_inc(stage(f"pe_in{b % 4}"), 16)

            for n in range(NCH):
                if n == QKV:
                    sp.dma_start(con[:, C_FIRST:NCONST], t["con"][:, C_FIRST:NCONST]).then_inc(stage("rest_in"), 16)
                    sp.dma_start(samp[:, :, :, :], t["convT"]).then_inc(stage("rest_in"), 16)
                    sp.dma_start(pages_sb[:, :], t["pages"]).then_inc(stage("rest_in"), 16)
                if n == KV_AT[0]:
                    sp.wait_ge(stage("rest_in"), 48)
                    read_pages(range(4))
                elif n == OG + 1:
                    read_pages((4, 5))
                elif n == KV_AT[1]:
                    load_rotary(4)
                    load_rotary(5)
                elif n == GA:
                    read_pages((6, 7))
                elif n == KV_AT[2]:
                    load_rotary(6)
                    load_rotary(7)
                if n >= RING:
                    sp.wait_ge(*used[n - RING])
                    if SSM <= n - RING < SSM + 2:
                        sp.wait_ge(stage("oss_ready"), n - RING - SSM + 1)
                dst = ring[n % RING]
                if n in KV_OF:
                    b, what = KV_OF[n]
                    src = t["kvT"] if what == 0 else t["kv"]
                    if n == KV_AT[0]:
                        sp.wait_ge(stage("oss_ready"), 2)
                        sp.wait_ge(stage("ssmp_stored"), 16)
                    for i in range(PAGES):
                        sp.dma_start(dst[:, 512 * i:512 * i + 512], src[bass.ds(phys[b][i], 1), :, :].rearrange("a p c -> p (a c)")
                                     ).then_inc(slot_in[n % RING], 16)
                    if what == 0 and b < 4:
                        load_rotary(b)
                elif n == UQR:
                    sp.dma_start(dst[:, 0:2048], t["wpre"][wp_index(n), :, 0:2048]).then_inc(slot_in[n % RING], 16)
                elif SSM <= n < SSM + 2:
                    sp.dma_start(dst[:, :], t["ssm"][n - SSM, :, :]).then_inc(slot_in[n % RING], 16)
                else:
                    sp.dma_start(dst[:, :], t["wpre"][wp_index(n), :, :]).then_inc(slot_in[n % RING], 16)
            moe_loads(sp)
            sp.wait_ge(h_ready, 3)
            sp.dma_start(t["o_y"], yout[:, :, :]).then_inc(stage("y_stored"), 16)
            sp.wait_ge(stage("y_stored"), 16)

        @block.tensor
        def _(pe):
            pe.wait_ge(inputs_in, 48)
            pe.wait_ge(sq_ready, 1)
            for k in range(KD):
                mm = pe_mm(bank[4][:, 0:T], lhsT=ones, rhs=hT[:, k, :], start=(k == 0), stop=(k == KD - 1))
            mm.then_inc(ss_ready, 1)

            def square_sum(b, k, before):
                pe.wait_ge(sq_ready, before + k + 1)
                return pe_mm(bank[b][:, 0:T], lhsT=ones, rhs=msq2[:, k, :], start=(k == 0), stop=(k == KD - 1))

            def modulate(i, b):
                n = ada_chunk(i)
                weights(pe, n)
                for k in range(KD):
                    for q in range(4):
                        mm = pe_mm(bank[b][32 * q:32 * q + 32, 0:P], lhsT=cT[:, k, :], rhs=chunk_k(n, q, k),
                                   start=(k == 0), stop=(k == KD - 1))
                mm.then_inc(mod_ready, 1)

            def turn_mod(i, b, at=0):
                pe.wait_ge(mod_row, i + 1)
                pe_mm(bank[b][:, at:at + P], lhsT=mrow[:, i % 2, :], rhs=ident, start=True, stop=True).then_inc(mod_turned, 1)

            for i in range(5):
                if i < 4:
                    if i >= 2:
                        pe.wait_ge(mod_row, i - 1)
                    modulate(i, i % 2)
                if i >= 1:
                    if i >= 3:
                        pe.wait_ge(mod_evac, i - 2)
                    turn_mod(i - 1, 2 + (i - 1) % 2)
            def row_sum(i, rows=2 * H):
                return con[:, C_COL + 2 * H - 1 - i:C_COL + 2 * H - 1 - i + rows]

            def small_projection(out, weights_of, r):
                for k in range(KD):
                    pe.wait_ge(stage("modulated"), r * KD + k + 1)
                    pe_mm(out[:, 0:NPR], lhsT=weights_of(k), rhs=hT[:, k, 0:NPR], start=(k == 0), stop=(k == KD - 1), skip_group_check=True)
                pe.wait_ge(h_ready, r + 1)
                for k in range(KD):
                    mm = pe_mm(out[:, NPR:T], lhsT=weights_of(k), rhs=hT[:, k, NPR:T], start=(k == 0), stop=(k == KD - 1), skip_group_check=True)
                return mm

            small_projection(bank[7][0:2 * H, 0:T], lambda k: wsm[:, k, 0:2 * H], 0).then_inc(once("ab_made")[0], 1)
            pe.wait_ge(stage("rest_in"), 48)
            for m in range(CONVT):
                if m == 1:
                    pe.wait_ge(stage("abT_copied"), 1)
                    for i, (a, b) in enumerate(((0, P), (P, NPR), (NPR, T))):
                        mm = pe.transpose(bank[6][0:b - a, 16 * i:16 * i + 16], rsb[0:2 * H, 1, a:b], ident[0:2 * H, 0:2 * H])
                    mm.then_inc(ab_ready, 1)
                n = QKV + m // 4
                weights(pe, n)
                if m >= 4:
                    pe.wait_ge(proj_evac, m - 3)
                for k in range(KD):
                    mm = pe_mm(bank[m % 4][:, 0:T], lhsT=chunk_k(n, m % 4, k), rhs=hT[:, k, :],
                               start=(k == 0), stop=(k == KD - 1))
                mm.then_inc(proj_ready, 1)
                i = m - 3
                if 0 <= i < 2 * H:
                    pe.wait_ge(l2sq, i + 1)
                    pe_mm(bank[5][0:2 * H, 0:NPR], lhsT=row_sum(i), rhs=sqb[:, i % 2, 0:NPR], start=(i == 0), stop=(i == 2 * H - 1),
                          skip_group_check=True).then_inc(l2ss, 1)
            pe.wait_ge(proj_evac, CONVT)
            for i in range(4, MOD_PRE + 1):
                if i < MOD_PRE:
                    pe.wait_ge(mod_row, i - 1)
                    modulate(i, i % 2)
                if i > 4:
                    pe.wait_ge(mod_evac, i - 2)
                    turn_mod(i - 1, 2 + (i - 1) % 2)
                if i == MOD_L2:
                    pe.wait_ge(l2sq, 2 * H + 1)
                    for j in range(2 * H):
                        mm = pe_mm(bank[5][0:2 * H, NPR:T], lhsT=row_sum(j), rhs=sq_s[:, j, :], start=(j == 0), stop=(j == 2 * H - 1),
                                   skip_group_check=True)
                    mm.then_inc(l2ss, 1)
            for i in range(2 * H):
                if i == 0:
                    pe.wait_ge(stage("l2_rs"), 1)
                if i == 2:
                    pe.wait_ge(mod_row, MOD_PRE)
                if i >= 4:
                    pe.wait_ge(l2done, i - 3)
                pe_mm(bank[L2_BANKS[i % 4]][:, 0:T], lhsT=ident[0:2 * H, i:i + 1].to_broadcast([2 * H, P]), rhs=rsb[0:2 * H, 0, :],
                      start=True, stop=True).then_inc(l2ss, 1)
            pe.wait_ge(bg_done, 1)
            for c in range(2):
                pe_mm(bank[6][:, 64 + 16 * c:72 + 16 * c], lhsT=upto, rhs=g_tok[:, c, :], start=True, stop=True)
                pe_mm(bank[6][:, 72 + 16 * c:80 + 16 * c], lhsT=ones, rhs=g_tok[:, c, :], start=True, stop=True)
            pe.wait_ge(stage("bgm_ready"), 1)
            mm = pe_mm(bank[6][:, 96:160], lhsT=ones[0:NSA, :], rhs=bgm[0:NSA, :], start=True, stop=True)
            mm.then_inc(once("cum_ready")[0], 1)
            pe.wait_ge(l2done, 2 * H)
            for c in range(2):
                tok = slice(c * P, (c + 1) * P)

                def products(g):
                    b0 = 4 - 4 * g
                    for i in range(4):
                        h = 4 * g + i
                        pe_mm(bank[b0][:, i * P:(i + 1) * P], lhsT=g_tok[:, c, h:h + 1].to_broadcast([P, P]), rhs=upto, start=True, stop=True)
                    for i in range(4):
                        h = 4 * g + i
                        pe_mm(bank[b0 + 1][:, i * P:(i + 1) * P], lhsT=beta_tok[:, c, h:h + 1].to_broadcast([P, P]), rhs=ident, start=True, stop=True)
                    if g == 0 and c == 0:
                        pe.wait_ge(*once("cum_read"))
                        pe.wait_ge(stage("egB_ready"), 1)
                    for i in range(4):
                        h = 4 * g + i
                        pe_mm(bank[b0 + 2][:, i * P:(i + 1) * P], lhsT=qkvT[:, H + h, tok], rhs=qkvT[:, H + h, tok], start=True, stop=True)
                    for i in range(4):
                        h = 4 * g + i
                        mm = pe_mm(bank[b0 + 3][:, i * P:(i + 1) * P], lhsT=qkvT[:, H + h, tok], rhs=qkvT[:, h, tok], start=True, stop=True)
                    mm.then_inc(stage("gd_prod"), 1)

                if c == 1:
                    pe.wait_ge(stage("gd_out"), 2)
                products(0)
                for g in range(2):
                    for w in range(2):
                        for i in range(4):
                            mm = pe_mm(bank[2 * w + g][:, i * P:(i + 1) * P],
                                       lhsT=qkvT[:, H * (1 + w) + 4 * g + i, tok], rhs=ident,
                                       start=True, stop=True)
                        mm.then_inc(tr_ready, 1)
                pe.wait_ge(tr_evac, 4 * (c + 1))
                products(1)
                pe.wait_ge(stage("prep_done"), 2 * c + 1)
                first = MOD_PRE + MOD_GDN * c
                for i in range(MOD_GDN + 1):
                    if i < MOD_GDN:
                        if i >= 2:
                            pe.wait_ge(mod_row, first + i - 1)
                        modulate(first + i, 4 + i % 2)
                    if i >= 1:
                        turn_mod(first + i - 1, 6 + (i - 1) % 2, P * ((i - 1) // 2))
                for lv in range(LEVELS):
                    for g in range(2):
                        q = (c * LEVELS + lv) * 2 + g + 1
                        pe.wait_ge(stage("lt_done"), q)
                        if lv == 0:
                            pe.wait_ge(stage("prep_done"), 2 * c + 2)
                        for i in range(4):
                            s = slice(i * P, (i + 1) * P)
                            mm = pe_mm(bank[g][:, s], lhsT=LTm[:, g, s], rhs=Xm[:, g, s], start=True, stop=True)
                        mm.then_inc(stage("lx_done"), 1)
                    for g in range(2 if lv else 0):
                        pe.wait_ge(stage("lx_copied"), doubling(c, lv, g))
                        for i in range(4 if lv < LEVELS - 1 else 0):
                            s = slice(i * P, (i + 1) * P)
                            pe_mm(bank[2 + g][:, s], lhsT=XTm[:, g, s], rhs=LTm[:, g, s], start=True, stop=True)
                        for i in range(4):
                            s = slice(i * P, (i + 1) * P)
                            mm = pe_mm(bank[4 + g][:, s], lhsT=LTm[:, g, s], rhs=XTm[:, g, s], start=True, stop=True)
                        mm.then_inc(stage("xlx_done"), 1)
                for g in range(2):
                    pe.wait_ge(stage("x_done"), (c + 1) * 2 * LEVELS if g == 1 else (c + 1) * 2 * LEVELS - 1)
                    for i in range(4):
                        s = slice(i * P, (i + 1) * P)
                        mm = pe_mm(bank[g][:, s], lhsT=XTm[:, g, s], rhs=VB[:, g, s], start=True, stop=True)
                    if c == 1:
                        for i in range(4):
                            s = slice(i * P, (i + 1) * P)
                            mm = pe_mm(bank[2 + g][:, s], lhsT=KBG[:, g, s], rhs=XTm[:, g, s], start=True, stop=True)
                    mm.then_inc(stage("uw_done"), 1)
                if c == 1:
                    for g in range(2):
                        pe.wait_ge(stage("wt_copied"), g + 1)
                        for i in range(4):
                            s = slice(i * P, (i + 1) * P)
                            mm = pe_mm(bank[4 + g][:, s], lhsT=Xm[:, g, s], rhs=Sst[:, g, s], start=True, stop=True)
                        mm.then_inc(stage("ws_done"), 1)
                pe.wait_ge(mod_evac, MOD_PRE + MOD_GDN * (c + 1))
                for g in range(2):
                    pe.wait_ge(stage("vn_done"), 2 * c + g + 1)
                    for i in range(4):
                        s = slice(i * P, (i + 1) * P)
                        mm = pe_mm(bank[6 + g][:, s], lhsT=VB[:, g, s], rhs=Aqk[:, g, s], start=True, stop=(c == 0))
                        if c == 1:
                            mm = pe_mm(bank[6 + g][:, s], lhsT=Sst[:, g, s], rhs=qg[:, g, s], start=False, stop=True)
                    for i in range(4):
                        s = slice(i * P, (i + 1) * P)
                        mm = pe_mm(bank[2 + g][:, s], lhsT=K2[:, g, s], rhs=VB[:, g, s], start=True, stop=True)
                    mm.then_inc(stage("os_done"), 1)
            pe.wait_ge(*once("x32_ready"))

            def state_product(w, g, base):
                for y in range(2):
                    for j in range(4):
                        mm = pe_mm(bank[base + y][32 * j:32 * j + 32, :], lhsT=x32[:, w * H + 4 * g + j, :],
                                   rhs=ssm_view[g][:, j, 4 * y:4 * y + 4, :].rearrange("p b v -> p (b v)"), start=True, stop=True)
                return mm

            for g in range(2):
                pe.wait_ge(stage("decayed"), g + 1)
                if g == 1:
                    pe.wait_ge(stage("gd_out"), 4)
                state_product(1, g, 2 * g).then_inc(stage("sample_products"), 1)
            for w in range(2):
                for g in range(2):
                    for j in range(4):
                        mm = pe_mm(bank[4 + w][32 * j:32 * j + 32, P * g:P * (g + 1)], lhsT=x32[:, (2 - w) * H + 4 * g + j, :],
                                   rhs=ident, start=True, stop=True)
            for j in range(4):
                mm = pe_mm(bank[6][32 * j:32 * j + 32, 0:2], lhsT=ident[0:NSA, 0:32], rhs=beta_tok[0:NSA, 2, j::4], start=True, stop=True)
            mm.then_inc(stage("sample_products"), 1)
            pe.wait_ge(*once("krow_copied"))
            for g in range(2):
                for y in range(2):
                    u = 2 * g + y
                    if u < 2:
                        pe.wait_ge(stage("vnm_ready"), u + 1)
                    else:
                        pe.wait_ge(stage("snew"), u - 1)
                    for j in range(4):
                        mm = pe_mm(bank[4 * y + j][:, :], lhsT=krow[:, j, g, :], rhs=vnm[:, g, 512 * y:512 * y + 512], start=True, stop=True)
                    mm.then_inc(stage("outer"), 1)
            for g in range(2):
                pe.wait_ge(stage("snew"), 3 + g)
                mm = state_product(0, g, 2 * g)
                mm.then_inc(stage("oss_ready"), 1)
            for g in range(2):
                pe.wait_ge(stage("oss_row"), g + 1)
                mm = pe_mm(bank[4][:, P * g:P * (g + 1)], lhsT=ksr[:, g, :], rhs=ident, start=True, stop=True)
            mm.then_inc(once("oss_turned")[0], 1)
            def project_z(m):
                weights(pe, ZZ + m // 4)
                if m >= 4:
                    pe.wait_ge(stage("z_evac"), m - 3)
                for k in range(KD):
                    mm = pe_mm(bank[m % 4][:, 0:T], lhsT=chunk_k(ZZ + m // 4, m % 4, k), rhs=hT[:, k, :], start=(k == 0), stop=(k == KD - 1))
                mm.then_inc(stage("z_ready"), 1)

            project_z(0)
            pe.wait_ge(stage("on_sq"), 1)
            for h in range(H):
                mm = pe_mm(bank[6][0:H, 0:T], lhsT=row_sum(h, H), rhs=oM[:, h, :], start=(h == 0), stop=(h == H - 1))
            mm.then_inc(stage("on_ss"), 1)
            project_z(1)
            pe.wait_ge(stage("on_root"), 1)
            for h in range(H):
                if h >= 2:
                    pe.wait_ge(stage("on_rs"), h - 1)
                pe_mm(bank[4 + h % 2][:, 0:T], lhsT=ident[0:H, h:h + 1].to_broadcast([H, P]), rhs=ors[0:H, :],
                      start=True, stop=True).then_inc(stage("on_spread"), 1)
                if h + 2 < H:
                    project_z(h + 2)
            pe.wait_ge(stage("on_rs"), H)
            for m in range(8):
                n = CQ + m // 4
                weights(pe, n)
                if m >= 4:
                    pe.wait_ge(stage("lat_evac"), m - 3)
                for k in range(KD):
                    mm = pe_mm(bank[4 + m % 4][:, 0:T], lhsT=chunk_k(n, m % 4, k), rhs=hT[:, k, :], start=(k == 0), stop=(k == KD - 1))
                mm.then_inc(stage("lat_ready"), 1)
            pe.wait_ge(stage("z_evac"), H)
            for k in range(KD):
                for half in (slice(0, ROPE), slice(ROPE, P)):
                    mm = pe_mm(bank[0][half, 0:T], lhsT=wsm[:, k, 16:16 + ROPE], rhs=hT[:, k, :], start=(k == 0), stop=(k == KD - 1), skip_group_check=True)
            mm.then_inc(once("kpe_ready")[0], 1)
            pe.wait_ge(*once("kpe_copied"))
            pe_mm(bank[1][:, 0:T], lhsT=perm, rhs=kpeT[:, :], start=True, stop=True).then_inc(once("kpe_turned")[0], 1)
            for w in range(2):
                for i in range(LORA):
                    pe.wait_ge(stage("lsq"), LORA * w + i + 1)
                    mm = pe_mm(bank[2 + w][:, 0:T], lhsT=ones, rhs=msq[:, i % 2, :], start=(i == 0), stop=(i == LORA - 1))
                    mm.then_inc(stage("lss"), 1)
            pe.wait_ge(stage("lat_normed"), 1)
            pe.wait_ge(stage("lat_evac"), 8)
            for m in range(12):
                n = UQN if m < 8 else UQR
                pe.wait_ge(slot_in[n % RING], arrive[n])
                if m >= 4:
                    pe.wait_ge(stage("q_evac"), m - 3)
                W = 1024 if m < 8 else 512
                c0 = (m if m < 8 else m - 8) * P
                for k in range(LORA):
                    mm = pe_mm(bank[4 + m % 4][:, 0:T], lhsT=ring[n % RING][:, k * W + c0:k * W + c0 + P], rhs=cqT[:, k, :],
                               start=(k == 0), stop=(k == LORA - 1))
                mm.then_inc(stage("q_ready"), 1)
            for i in range(4):
                pe.wait_ge(stage("q_evac"), 9 + i)
                if i >= 2:
                    pe.wait_ge(stage("q_turned"), i - 1)
                pe_mm(bank[i % 2][:, 0:T], lhsT=perm, rhs=qpeT[:, i, :], start=True, stop=True).then_inc(stage("q_turn"), 1)
            pe.wait_ge(stage("lat_normed"), 2)
            pe.wait_ge(slot_in[UV % RING], arrive[UV])
            wv = ring[UV % RING][:, :].rearrange("p (c n) -> p c n", c=LORA)
            for i in VALUE_BANKS:
                c, y = i // 2, i % 2
                if i < 2:
                    pe.wait_ge(stage("q_turned"), 3 + i)
                for k in range(LORA):
                    mm = pe_mm(bank[i][:, :], lhsT=latT[:, k, c * P:(c + 1) * P], rhs=wv[:, k, 512 * y:512 * y + 512], start=(k == 0), stop=(k == LORA - 1))
                mm.then_inc(stage("vt_ready"), 1)
            pe.wait_ge(slot_in[UK % RING], arrive[UK])
            wk = ring[UK % RING][:, :].rearrange("p (c h n) -> p c h n", c=LORA, h=H)

            def keys(h):
                pe.wait_ge(stage("kn_evac"), h - 1) if h >= 2 else pe.wait_ge(stage("q_evac"), 12)
                for k in range(LORA):
                    mm = pe_mm(bank[6 + h % 2][:, 0:NPR], lhsT=wk[:, k, h, :], rhs=latT[:, k, 0:NPR], start=(k == 0), stop=(k == LORA - 1))
                mm.then_inc(stage("kn_ready"), 1)
            keys(0)
            keys(1)
            pe.wait_ge(stage("vt_evac"), 4)
            for h in range(H + 1):
                if h < H:
                    s = bank[h % 2]
                    pe.wait_ge(stage("kn_evac"), h + 1)
                    half = slice(64 * (h % 2), 64 * (h % 2) + 64)
                    if h >= 2:
                        pe.wait_ge(stage("pa_masked"), h - 1)
                    pe_mm(s[:, 0:P], lhsT=qnT[:, h, 0:P], rhs=knT[:, h, 0:P], start=True, stop=False)
                    pe_mm(s[:, 0:P], lhsT=qpeT[half, h // 2, 0:P], rhs=kpeT[half, 0:P], start=False, stop=True)
                    pe_mm(s[:, P:384], lhsT=qnT[:, h, P:NPR], rhs=knT[:, h, :], start=True, stop=False)
                    pe_mm(s[:, P:384], lhsT=qpeT[half, h // 2, P:NPR], rhs=kpeT[half, 0:NPR], start=False, stop=True).then_inc(stage("pa_scores"), 1)
                    if h + 2 < H:
                        keys(h + 2)
                if h == H - 1:
                    for half in (slice(0, ROPE), slice(ROPE, P)):
                        pe_mm(bank[7][half, 0:32], lhsT=ident[:, 0:ROPE], rhs=qpeT[:, :, NPR:T], start=True, stop=True, skip_group_check=True)
                        pe_mm(bank[7][half, 32:64], lhsT=ident[:, ROPE:P], rhs=qpeT[:, :, NPR:T], start=True, stop=True, skip_group_check=True)
                    for k in range(LORA):
                        mm = pe_mm(bank[6][0:NSA, k * P:(k + 1) * P], lhsT=latT[:, k, NPR:T], rhs=ident, start=True, stop=True)
                    mm.then_inc(once("ltok_ready")[0], 1)
                if h >= 1:
                    j = h - 1
                    pe.wait_ge(stage("pa_probs"), j + 1)
                    if j >= 2:
                        pe.wait_ge(stage("pa_pcopied"), j - 1)
                    w = bank[2 + j % 2]
                    pe.transpose(w[:, 0:P], mp[j % 2][:, 0:P], ident)
                    pe.transpose(w[:, P:256], mp[j % 2][:, P:256], ident)
                    pe.transpose(w[:, 256:384], mp[j % 2][:, 256:384], ident).then_inc(stage("pa_turned"), 1)
                    pe.wait_ge(stage("pa_pcopied"), j + 1)
                    if j >= 2:
                        pe.wait_ge(stage("pa_out"), j - 1)
                    o = bank[4 + j % 2]
                    pe_mm(o[:, 0:NPR], lhsT=vtok[:, 0, j * P:(j + 1) * P], rhs=mpT[j % 2][:, 0:NPR], start=True, stop=False)
                    pe_mm(o[:, P:NPR], lhsT=vtok[:, 1, j * P:(j + 1) * P], rhs=mpT[j % 2][:, NPR:384], start=False, stop=True).then_inc(stage("pa_ready"), 1)
            pe.wait_ge(slot_in[UKT % RING], arrive[UKT])
            wkt = ring[UKT % RING][:, :].rearrange("p (h c) -> p h c", h=H)
            pe.wait_ge(*once("qns_ready"))
            pe.wait_ge(stage("pa_out"), 8)
            for g in range(2):
                for j in range(4):
                    mm = pe_mm(bank[g][32 * j:32 * j + 32, :], lhsT=qnS[:, 4 * g + j, :], rhs=wkt[:, 4 * g + j, :], start=True, stop=True)
            mm.then_inc(once("qlat_ready")[0], 1)
            for g in range(2):
                pe.wait_ge(stage("qrow_copied"), g + 1)
                for k in range(LORA):
                    mm = pe_mm(bank[2 + g][:, P * k:P * (k + 1)], lhsT=qrow[:, g, P * k:P * (k + 1)], rhs=ident, start=True, stop=True)
                mm.then_inc(stage("qlat_turned"), 1)
            pe.wait_ge(stage("qlat_copied"), 2)
            def project(first, last):
                for m in range(first, last):
                    n = (OG, GA, GB, OM, WO)[m // 8] + m % 8 // 4
                    rhs = (oG, hT, hT, oM, yA)[m // 8]
                    weights(pe, n)
                    if m == 0:
                        pe.wait_ge(stage("z_gated"), H)
                    if m == 24:
                        pe.wait_ge(*once("os_copied"))
                    if m == 32:
                        pe.wait_ge(stage("merged"), KD)
                    if m >= 2:
                        kind, r = (m - 2) // 8, (m - 2) % 8 + 1
                        pe.wait_ge(stage("gate_sig" if kind in (1, 2) else "out_evac"), (0, 0, 8, 8, 16)[kind] + r)
                    for k in range(KD):
                        mm = pe_mm(bank[4 + m % 2][:, 0:T], lhsT=chunk_k(n, m % 4, k), rhs=rhs[:, k, :], start=(k == 0), stop=(k == KD - 1))
                    mm.then_inc(stage("out_ready"), 1)
                    if m >= 33:
                        square_sum(6, m - 33, 1)

            for q in range(2):
                bs = range(4 * q, 4 * q + 4)
                if q == 1:
                    pe.wait_ge(stage("s_exp"), 1)
                for b in bs:
                    r = slice(32 * (b % 4), 32 * (b % 4) + 32)
                    half = slice(ROPE * (b % 4 // 2), ROPE * (b % 4 // 2 + 1))
                    pe.wait_ge(stage(f"pe_in{b % 4}"), 16 * PAGES * (b // 4 + 1))
                    for y in range(2):
                        mm = pe_mm(bank[y][r, :], lhsT=qpeS[half, b, :], rhs=peT[b % 4][:, 512 * y:512 * y + 512],
                                   start=True, stop=False, skip_group_check=True)
                    mm.then_inc(stage("pe_used"), 1)
                for b in bs:
                    r = slice(32 * (b % 4), 32 * (b % 4) + 32)
                    pe_mm(bank[6][r, 0:NSA], lhsT=qpeS[0:ROPE, b, :], rhs=kpeT[0:ROPE, NPR:T], start=True, stop=False, skip_group_check=True)
                for k in range(LORA):
                    for b in bs:
                        r = slice(32 * (b % 4), 32 * (b % 4) + 32)
                        mm = pe_mm(bank[6][r, 0:NSA], lhsT=qlatT[:, k, b, :], rhs=latT[:, k, NPR:T], start=False, stop=(k == LORA - 1), skip_group_check=True)
                mm.then_inc(stage("snew_scores"), 1)
                for b in bs:
                    pe.wait_ge(slot_in[kv_chunk(b, 0) % RING], arrive[kv_chunk(b, 0)])
                for y in range(2):
                    for k in range(LORA):
                        for b in bs:
                            r = slice(32 * (b % 4), 32 * (b % 4) + 32)
                            kt = ring[kv_chunk(b, 0) % RING][:, :].rearrange("p (g c s) -> p g c s", g=PAGES, c=LORA)
                            mm = pe_mm(bank[y][r, :], lhsT=qlatT[:, k, b, :], rhs=kt[:, 4 * y:4 * y + 4, k, :],
                                       start=False, stop=(k == LORA - 1), skip_group_check=True)
                mm.then_inc(stage("st_ready"), 1)
                project(16 * q, 16 * q + 4)
                pe.wait_ge(stage("p_ready"), q + 1)
                if q == 1:
                    pe.wait_ge(stage("ol_copied"), 1)
                for g in range(PAGES):
                    pe_mm(bank[2 + g // 4][:, P * (g % 4):P * (g % 4 + 1)], lhsT=ps_[q][:, P * g:P * (g + 1)], rhs=ident, start=True, stop=True)
                pe_mm(bank[7][0:NSA, 0:P], lhsT=ps_[q][:, 1024:1032], rhs=ident, start=True, stop=True).then_inc(stage("p_turned"), 1)
                project(16 * q + 4, 16 * q + 8)
                pe.wait_ge(stage("pT_copied"), q + 1)
                for b in bs:
                    pe.wait_ge(slot_in[kv_chunk(b, 1) % RING], arrive[kv_chunk(b, 1)])
                for g in range(PAGES):
                    for b in bs:
                        r = slice(32 * (b % 4), 32 * (b % 4) + 32)
                        pe_mm(bank[6][r, :], lhsT=pT[:, g, r], rhs=ring[kv_chunk(b, 1) % RING][:, 512 * g:512 * (g + 1)],
                              start=(g == 0), stop=False, skip_group_check=True)
                for b in bs:
                    r = slice(32 * (b % 4), 32 * (b % 4) + 32)
                    mm = pe_mm(bank[6][r, :], lhsT=pT9[0:NSA, r], rhs=lat_tok[0:NSA, :], start=False, stop=True, skip_group_check=True)
                mm.then_inc(stage("ol_ready"), 1)
                if q == 0:
                    project(8, 10)
                pe.wait_ge(stage("orow_copied"), q + 1)
                for k in range(LORA):
                    mm = pe_mm(bank[7][:, P * k:P * (k + 1)], lhsT=orow[:, P * k:P * (k + 1)], rhs=ident, start=True, stop=True)
                mm.then_inc(stage("ol_turned"), 1)
                if q == 0:
                    project(10, 16)
            pe.wait_ge(slot_in[UV2 % RING], arrive[UV2])
            pe.wait_ge(stage("ol_copied"), 2)
            wv2 = ring[UV2 % RING][:, :].rearrange("p (c n) -> p c n", c=LORA)
            for g in range(2):
                for k in range(LORA):
                    for j in range(4):
                        h = 4 * g + j
                        mm = pe_mm(bank[0][32 * j:32 * j + 32, P * g:P * (g + 1)], lhsT=olat[:, k, h, :], rhs=wv2[:, k, h * P:(h + 1) * P],
                                   start=(k == 0), stop=(k == LORA - 1), skip_group_check=True)
            mm.then_inc(once("os_ready")[0], 1)
            pe.wait_ge(*once("osr_copied"))
            for g in range(2):
                mm = pe_mm(bank[7][:, P * g:P * (g + 1)], lhsT=osr[:, P * g:P * (g + 1)], rhs=ident, start=True, stop=True)
            mm.then_inc(once("os_turned")[0], 1)
            project(24, 40)
            square_sum(6, KD - 1, 1).then_inc(ss_ready, 1)
            small_projection(bank[7][0:NE, 0:T], lambda k: wsm[:, k, 16 + ROPE:WSM], 1).then_inc(once("logits_T")[0], 1)
            tiles = ((0, P), (P, NPR), (NPR, T))
            pe.wait_ge(*once("logits_copied"))
            for i, (a, b) in enumerate(tiles):
                mm = pe.transpose(bank[5][0:b - a, NE * i:NE * i + NE], gateT[0:NE, a:b], ident[0:NE, 0:NE])
            mm.then_inc(once("logits")[0], 1)
            for i, (a, b) in enumerate(tiles):
                for y in range(2):
                    q = 2 * i + y
                    if q >= 4:
                        pe.wait_ge(stage("h2_copied"), q - 3)
                    for k in range(4):
                        mm = pe.transpose(bank[q % 4][0:b - a, k * P:(k + 1) * P], hT[:, 4 * y + k, a:b], ident)
                    mm.then_inc(stage("h2_turned"), 1)
            pe.wait_ge(stage("sel_ready"), 1)
            pe_mm(bank[6][0:NE, 0:P], lhsT=sel[:, 0, :], rhs=before, start=True, stop=True)
            pe_mm(bank[6][0:NE, P:NPR], lhsT=sel[:, 0, :], rhs=ones, start=True, stop=False)
            pe_mm(bank[6][0:NE, P:NPR], lhsT=sel[:, 1, :], rhs=before, start=False, stop=True)
            pe_mm(bank[6][0:NE, NPR:T], lhsT=sel[:, 0, :], rhs=ones[:, 0:NSA], start=True, stop=False)
            pe_mm(bank[6][0:NE, NPR:T], lhsT=sel[:, 1, :], rhs=ones[:, 0:NSA], start=False, stop=False)
            pe_mm(bank[6][0:NE, NPR:T], lhsT=sel[0:NSA, 2, :], rhs=before[0:NSA, 0:NSA], start=False, stop=True)
            pe_mm(bank[7][0:NE, 0:1], lhsT=sel[:, 0, :], rhs=ones[:, 0:1], start=True, stop=False)
            pe_mm(bank[7][0:NE, 0:1], lhsT=sel[:, 1, :], rhs=ones[:, 0:1], start=False, stop=False)
            pe_mm(bank[7][0:NE, 0:1], lhsT=sel[0:NSA, 2, :], rhs=ones[0:NSA, 0:1], start=False, stop=True)
            pe.wait_ge(stage("sel_ready"), 2)
            for i, (a, b) in enumerate(tiles):
                pe.transpose(bank[4][0:NE, a:b], sel[0:b - a, i, :], ident[0:b - a, 0:b - a])
            pe.wait_ge(stage("h2_copied"), 6)
            for i, (a, b) in enumerate(tiles):
                mm = pe.transpose(bank[0][0:NE, a:b], gate[0:b - a, i, :], ident[0:b - a, 0:b - a])
            mm.then_inc(stage("route"), 1)
            pe.wait_ge(stage("blocks"), 1)
            pe_mm(bank[7][0:NE, 1:2], lhsT=before[0:NE, 0:NE], rhs=cntc[0:NE, 0:1], start=True, stop=True)
            pe_mm(bank[7][0:1, 2:3], lhsT=cntc[0:NE, 0:1], rhs=ones[0:NE, 0:1], start=True, stop=True).then_inc(stage("route"), 1)
            pe.wait_ge(*once("e1h_ready"))
            pe_mm(bank[7][0:1, 8:8 + NJ1], lhsT=con[0:NE, C_E:C_E + 1], rhs=e1h[0:NE, :], start=True, stop=True).then_inc(stage("route"), 1)
            pe.wait_ge(*once("m1_ready"))
            for i, (a, b) in enumerate(tiles):
                pe_mm(bank[1][0:b - a, NJ1 * i:NJ1 * (i + 1)], lhsT=m1T[0:NE, a:b], rhs=e1h[0:NE, :], start=True, stop=True)
            for i, (a, b) in enumerate(tiles):
                mm = pe_mm(bank[2][0:b - a, NJ1 * i:NJ1 * (i + 1)], lhsT=gateT[0:NE, a:b], rhs=e1h[0:NE, :], start=True, stop=True)
            mm.then_inc(stage("route"), 1)
            moe_tensor(pe)
            for k in range(KD):
                mm = square_sum(0, k, 1 + KD)
            mm.then_inc(ss_ready, 1)

        @block.scalar
        def _(act):
            line = [0]

            def link(ins):
                line[0] += 1
                ins.then_inc(act_line, 1)
                act.wait_ge(act_line, line[0])

            A = nc.scalar.activation
            act.wait_ge(inputs_in, 48)
            A(hT[:, :, :], xT[:, :, :], ACT.Square).then_inc(sq_ready, 1)

            def modulate_prompt(r, out, sh, A9):
                for k in range(KD):
                    act.wait_ge(stage("normed"), r * KD + k + 1)
                    A(out[:, k, 0:NPR], out[:, k, 0:NPR], ACT.Identity, scale=A9[:, k, 0:1], bias=mod[:, sh + k, 0:1]).then_inc(stage("modulated"), 1)

            def root(out, sums, scale):
                return A(out, sums, ACT.Sqrt, scale=scale, bias=con[:, C_EPS:C_EPS + 1])
            act.wait_ge(ss_ready, 1)
            act.wait_ge(*once("upad_zero"))
            root(rsb[:, 0, :], bank[4][:, 0:T], 1.0 / D).then_inc(root_ready, 1)
            def mod_rows(i, b):
                act.wait_ge(mod_ready, i + 1)
                if i >= 2:
                    act.wait_ge(mod_turned, i - 1)
                A(mrow[:, i % 2, :], bank[b][:, 0:P], ACT.Copy).then_inc(mod_row, 1)
            for i in range(4):
                mod_rows(i, i % 2)
            modulate_prompt(0, hT, 0, modA)
            act.wait_ge(*once("ab_made"))
            A(rsb[0:2 * H, 1, :], bank[7][0:2 * H, 0:T], ACT.Copy).then_inc(stage("abT_copied"), 1)
            act.wait_ge(stage("rest_in"), 48)
            for m in range(CONVT + 1):
                if m < CONVT:
                    act.wait_ge(proj_ready, m + 1)
                    if m >= 3:
                        act.wait_ge(conv_done, m - 2)
                    elif m == 0:
                        act.wait_ge(*once("upad_zero"))
                    b = bank[m % 4]
                    A(samp[:, m, 3, :], b[:, NPR:T], ACT.Copy)
                    A(convp[:, m, :], b[:, NPR - 3:NPR], ACT.Copy)
                    A(upad[:, m % 3, 3:3 + NPR], b[:, 0:NPR], ACT.Copy).then_inc(proj_evac, 1)
                if m >= 1:
                    act.wait_ge(conv_done, m)
                    if m >= 3:
                        act.wait_ge(silu_done, m - 2)
                    A(sigb[:, (m - 1) % 2, 0:NPR], qkvT[:, m - 1, 0:NPR], ACT.Sigmoid).then_inc(sig_done, 1)
                i = m - 2
                if 0 <= i < 2 * H:
                    act.wait_ge(silu_done, i + 1)
                    if i >= 2:
                        act.wait_ge(l2ss, i - 1)
                    A(sqb[:, i % 2, 0:NPR], qkvT[:, i, 0:NPR], ACT.Square).then_inc(l2sq, 1)
            for i in range(4, 6):
                mod_rows(i, i % 2)
            act.wait_ge(stage("conv_s"), 1)
            A(smt[:, 1, :, :], smt[:, 0, :, :], ACT.Sigmoid).then_inc(sig_done, 1)
            act.wait_ge(ab_ready, 1)
            act.wait_ge(stage("ab_copied"), 1)
            A(beta_tok[:, :, :], gsc[:, 0, :, :], ACT.Sigmoid).then_inc(ab_act, 1)
            act.wait_ge(silu_done, CONVT + 1)
            act.wait_ge(l2ss, 2 * H)
            A(sq_s[:, :, :], qkvT[:, 0:2 * H, NPR:T], ACT.Square).then_inc(l2sq, 1)
            for i in range(6, MOD_PRE):
                mod_rows(i, i % 2)
                if i == MOD_L2:
                    act.wait_ge(l2ss, 2 * H + 1)
                    A(rsb[0:2 * H, 0, :], bank[5][0:2 * H, 0:T], ACT.Sqrt, scale=1.0, bias=con[0:2 * H, C_EPS:C_EPS + 1]).then_inc(root_ready, 1)
            link(A(gsc[:, 2, :, :], gsc[:, 1, :, :], ACT.Abs))
            link(A(gsc[:, 2, :, :], gsc[:, 2, :, :], ACT.Exp, scale=-1.0))
            link(A(gcol[:, 0, :], small[:, S_ALOG:S_ALOG + 8], ACT.Exp))
            A(gsc[:, 2, :, :], gsc[:, 2, :, :], ACT.Ln, bias=1.0).then_inc(ab_act, 1)
            for c in range(2):
                if c == 0:
                    act.wait_ge(*once("cum_ready"))
                    A(egB[:, :], bank[6][:, 96:160], ACT.Exp).then_inc(stage("egB_ready"), 1)
                    act.wait_ge(l2done, 2 * H)
                    act.wait_ge(stage("cum_copied"), 1)
                else:
                    act.wait_ge(stage("gd_out"), 2)
                    act.wait_ge(stage("cum_copied"), 2)
                A(gcol[:, 1, :], gcol[:, 0, :], ACT.Exp).then_inc(stage("gexp"), 1)
                A(gcol[:, 4, :], gsc[:, 0, 0, :], ACT.Exp).then_inc(stage("gexp"), 1)
                A(gcol[:, 3, :], gsc[:, 0, 1, :], ACT.Exp).then_inc(stage("gexp"), 1)
                for g in range(2):
                    act.wait_ge(stage("gd_prod"), 2 * c + g + 1)
                    A(XTm[:, g, :], bank[4 - 4 * g][:, :], ACT.Exp).then_inc(stage("eg_done"), 1)
                    act.wait_ge(stage("dif_done"), 2 * c + g + 1)
                    A(LTm[:, g, :], LTm[:, g, :], ACT.Exp).then_inc(stage("dec_done"), 1)
                    if g == 0:
                        for q, (w, x) in enumerate(((0, 0), (1, 0), (0, 1), (1, 1))):
                            act.wait_ge(tr_ready, 4 * c + q + 1)
                            A((K2 if w == 0 else VB)[:, x, :], bank[2 * w + x][:, :], ACT.Copy).then_inc(tr_evac, 1)
                for i in range(MOD_GDN):
                    mod_rows(MOD_PRE + MOD_GDN * c + i, 4 + i % 2)
                for lv in range(1, LEVELS):
                    for g in range(2):
                        act.wait_ge(stage("lx_done"), (c * LEVELS + lv) * 2 + g + 1)
                        A(LTm[:, g, :], bank[g][:, :], ACT.Copy).then_inc(stage("lx_copied"), 1)
                if c == 1:
                    for g in range(2):
                        act.wait_ge(stage("uw_done"), 2 + g + 1)
                        A(Xm[:, g, :], bank[2 + g][:, :], ACT.Copy).then_inc(stage("wt_copied"), 1)
                    act.wait_ge(*once("x32_zero"))
                    A(x32[:, :, 0:NSA], qkvT[:, :, NPR:T], ACT.Copy).then_inc(once("x32_ready")[0], 1)
                act.wait_ge(stored, 32)
                for g in range(2):
                    act.wait_ge(stage("os_done"), 2 * c + g + 1)
                    A(oG[:, 4 * g:4 * g + 4, c * P:(c + 1) * P], bank[6 + g][:, :].rearrange("p (h t) -> p h t", h=4),
                      ACT.Copy).then_inc(stage("o_copied"), 1)
            act.wait_ge(stage("sample_products"), 3)
            act.wait_ge(*once("krow_zero"))
            for j in range(4):
                r = slice(32 * j, 32 * j + 32)
                ins = A(krow[r, j, :, :], bank[5][r, 0:2 * P].rearrange("p (g v) -> p g v", g=2), ACT.Copy)
            ins.then_inc(once("krow_copied")[0], 1)
            act.wait_ge(*once("oss_turned"))
            A(oG[:, :, NPR:T], bank[4][:, 0:2 * P].rearrange("p (h b) -> p h b", h=H)[:, :, 0:NSA], ACT.Copy).then_inc(stage("o_copied"), 1)
            act.wait_ge(stage("o_copied"), 5)
            A(oM[:, :, :], oG[:, :, :], ACT.Square).then_inc(stage("on_sq"), 1)
            act.wait_ge(stage("on_ss"), 1)
            A(ors[0:H, :], bank[6][0:H, 0:T], ACT.Sqrt, scale=1.0 / P, bias=con[0:H, C_EPS:C_EPS + 1]).then_inc(root_ready, 1)
            for m in range(H):
                act.wait_ge(stage("z_ready"), m + 1)
                if m >= 2:
                    act.wait_ge(stage("z_gated"), m - 1)
                A(zsig[:, m % 2, :], bank[m % 4][:, 0:T], ACT.Sigmoid).then_inc(stage("z_sig"), 1)
            for m in range(8):
                act.wait_ge(stage("lat_ready"), m + 1)
                A((cqT if m < 4 else latT)[:, m % 4, :], bank[4 + m % 4][:, 0:T], ACT.Copy).then_inc(stage("lat_evac"), 1)
            act.wait_ge(*once("kpe_ready"))
            A(kpeT[:, :], bank[0][:, 0:T], ACT.Copy).then_inc(once("kpe_copied")[0], 1)
            act.wait_ge(stage("lat_evac"), 8)
            act.wait_ge(stage("z_gated"), H)
            for i in range(2 * LORA):
                if i >= 2:
                    act.wait_ge(stage("lss"), i - 1)
                A(msq[:, i % 2, :], (cqT if i < 4 else latT)[:, i % 4, :], ACT.Square).then_inc(stage("lsq"), 1)
                if i % LORA == LORA - 1:
                    act.wait_ge(stage("lss"), i + 1)
                    root(mrs[:, i // LORA, :], bank[2 + i // LORA][:, 0:T], 1.0 / (LORA * P)).then_inc(root_ready, 1)
            for m in range(12):
                act.wait_ge(stage("q_ready"), m + 1)
                A(qnT[:, m, :] if m < 8 else qpeT[:, m - 8, :], bank[4 + m % 4][:, 0:T], ACT.Copy).then_inc(stage("q_evac"), 1)
            def copy_keys(h):
                act.wait_ge(stage("kn_ready"), h + 1)
                A(knT[:, h, :], bank[6 + h % 2][:, 0:NPR], ACT.Copy).then_inc(stage("kn_evac"), 1)
            for j, i in enumerate(VALUE_BANKS):
                act.wait_ge(stage("vt_ready"), j + 1)
                A(vtok[:, i // 2, 512 * (i % 2):512 * (i % 2) + 512], bank[i][:, :], ACT.Copy).then_inc(stage("vt_evac"), 1)
            copy_keys(0)
            copy_keys(1)
            for h in range(H + 1):
                if h < H:
                    if h + 2 < H:
                        copy_keys(h + 2)
                    act.wait_ge(stage("pa_max"), h + 1)
                    if h >= 2:
                        act.wait_ge(stage("pa_turned"), h - 1)
                    st = mstat[:, h % 2, :]
                    A(mp[h % 2][:, 0:P], msc[h % 2][:, 0:P], ACT.Exp, bias=st[:, 2:3], scale=SCALE, accum_out=st[:, 4:5])
                    A(mp[h % 2][:, P:384], msc[h % 2][:, P:384], ACT.Exp, bias=st[:, 3:4], scale=SCALE, accum_out=st[:, 5:6]).then_inc(stage("pa_exp"), 1)
                if h >= 1:
                    j = h - 1
                    act.wait_ge(stage("pa_turned"), j + 1)
                    if j >= 2:
                        act.wait_ge(stage("pa_ready"), j - 1)
                    A(mpT[j % 2][:, :], bank[2 + j % 2][:, 0:384], ACT.Copy).then_inc(stage("pa_pcopied"), 1)
                    act.wait_ge(stage("pa_ready"), j + 1)
                    A(oM[:, j, 0:NPR], bank[4 + j % 2][:, 0:NPR], ACT.Copy).then_inc(stage("pa_out"), 1)
            act.wait_ge(*once("att_zero"))
            A(qnS[:, :, 0:NSA], qnT[:, :, NPR:T], ACT.Copy).then_inc(once("qns_ready")[0], 1)
            act.wait_ge(*once("qlat_ready"))
            for g in range(2):
                A(qrow[:, g, :], bank[g][:, :], ACT.Copy).then_inc(stage("qrow_copied"), 1)
            act.wait_ge(*once("ltok_ready"))
            for i in range(2):
                A(qpeS[:, :, i:NSA:2], bank[7][:, 32 * i:32 * i + 32].rearrange("p (a b) -> p b a", a=4), ACT.Copy)
            A(lat_tok[0:NSA, :], bank[6][0:NSA, :], ACT.Copy)
            for g in range(2):
                act.wait_ge(stage("qlat_turned"), g + 1)
                for k in range(LORA):
                    ins = A(qlatT[:, k, :, 4 * g:4 * g + 4], bank[2 + g][:, P * k:P * (k + 1)].rearrange("p (j b) -> p b j", j=4)[:, 0:NSA, :], ACT.Copy)
                ins.then_inc(stage("qlat_copied"), 1)
            def evacuate(first, last):
                for m in range(first, last):
                    act.wait_ge(stage("out_ready"), m + 1)
                    b = bank[4 + m % 2][:, 0:T]
                    if m < 8:
                        A(yA[:, m, :], b, ACT.Copy).then_inc(stage("out_evac"), 1)
                    elif m < 16:
                        if m >= 10:
                            act.wait_ge(stage("gated"), m - 9)
                        A(gsig[:, m % 2, :], b, ACT.Sigmoid).then_inc(stage("gate_sig"), 1)
                    else:
                        A(gB[:, m - 16, :], b, ACT.Sigmoid).then_inc(stage("gate_sig"), 1)

            for q in range(2):
                act.wait_ge(stage("s_max"), q + 1)
                st = sstat[:, q, :]
                A(ps_[q][:, 1024:1032], ps_[q][:, 1024:1032], ACT.Exp, bias=st[:, 2:3], scale=SCALE, accum_out=st[:, 4:5])
                A(ps_[q][:, 0:1024].rearrange("p (y s) -> p y s", y=2), banks[:, 0:2, :], ACT.Exp, bias=st[:, 2:3], scale=SCALE,
                  accum_out=st[:, 3:4]).then_inc(stage("s_exp"), 1)
                evacuate(16 * q, 16 * q + 4)
                act.wait_ge(stage("p_turned"), q + 1)
                for y in range(2):
                    A(pT[:, 4 * y:4 * y + 4, :], bank[2 + y][:, :].rearrange("p (g r) -> p g r", g=4), ACT.Copy)
                A(pT9[0:NSA, :], bank[7][0:NSA, 0:P], ACT.Copy).then_inc(stage("pT_copied"), 1)
                evacuate(16 * q + 4, 16 * q + 8)
                act.wait_ge(stage("ol_ready"), q + 1)
                A(orow[:, :], bank[6][:, :], ACT.Copy).then_inc(stage("orow_copied"), 1)
                if q == 0:
                    evacuate(8, 10)
                act.wait_ge(stage("ol_turned"), q + 1)
                for k in range(LORA):
                    ins = A(olat[:, k, :, 4 * q:4 * q + 4], bank[7][:, P * k:P * (k + 1)].rearrange("p (j h) -> p h j", j=4)[:, 0:H, :], ACT.Copy)
                ins.then_inc(stage("ol_copied"), 1)
                if q == 0:
                    evacuate(10, 16)
            act.wait_ge(*once("os_ready"))
            A(osr[:, :], bank[0][:, 0:2 * P], ACT.Copy).then_inc(once("osr_copied")[0], 1)
            act.wait_ge(*once("os_turned"))
            A(oM[:, :, NPR:T], bank[7][:, 0:2 * P].rearrange("p (h b) -> p h b", h=H)[:, :, 0:NSA], ACT.Copy).then_inc(once("os_copied")[0], 1)
            for k in range(KD):
                act.wait_ge(stage("out_evac"), 17 + k)
                A(msq2[:, k, :], xT[:, k, :], ACT.Square).then_inc(sq_ready, 1)
            act.wait_ge(ss_ready, 2)
            root(mrs2[:, :], bank[6][:, 0:T], 1.0 / D).then_inc(root_ready, 1)
            modulate_prompt(1, hT, 24, modA2)
            act.wait_ge(stored, 64)
            for i in range(6):
                act.wait_ge(stage("h2_turned"), i + 1)
                n = P if i < 4 else NSA
                A(h2tok[0:n, i // 2, :, 64 * (i % 2):64 * (i % 2) + 64],
                  bank[i % 4][0:n, :].rearrange("p (x k) -> p k x", k=KD), ACT.Copy).then_inc(stage("h2_copied"), 1)
            act.wait_ge(*once("v8_ready"))
            for i in range(3):
                A(ex[:, i, :], lg[:, i, :], ACT.Exp, bias=rst[:, 0, i:i + 1]).then_inc(stage("route_exp"), 1)
            moe_scalar(act)
            for k in range(KD):
                act.wait_ge(stage("x2_ready"), k + 1)
                A(msq2[:, k, :], xT[:, k, :], ACT.Square).then_inc(sq_ready, 1)
            act.wait_ge(ss_ready, 3)
            root(mrs2[:, :], bank[0][:, 0:T], 1.0 / D).then_inc(root_ready, 1)
            modulate_prompt(2, yout, 48, modA2)

        @block.vector
        def _(dve):
            line = [0]
            V = nc.vector

            def link(ins):
                line[0] += 1
                ins.then_inc(dve_line, 1)
                dve.wait_ge(dve_line, line[0])

            def norm_mod(r, x, out, sc, sh, nw, rs, A9):
                link(V.scalar_tensor_tensor(A9, mod[:, sc:sc + KD, :], 1.0,
                                            small[:, nw:nw + KD].unsqueeze(2).to_broadcast([P, KD, 9]), ALU.add, ALU.mult))
                dve.wait_ge(root_ready, (1, 6, 7)[r])
                link(V.reciprocal(rs, rs))
                for k in range(KD):
                    V.tensor_tensor(out[:, k, :], x[:, k, :], rs, ALU.mult).then_inc(stage("normed"), 1)
                dve.wait_ge(stage("normed"), (r + 1) * KD)
                link(V.tensor_tensor(out[:, :, NPR:T], out[:, :, NPR:T], A9[:, :, 1:9], ALU.mult))
                dve.wait_ge(stage("modulated"), (r + 1) * KD)
                V.tensor_tensor(out[:, :, NPR:T], out[:, :, NPR:T], mod[:, sh:sh + KD, 1:9], ALU.add).then_inc(h_ready, 1)
                dve.wait_ge(h_ready, r + 1)

            dve.wait_ge(inputs_in, 48)
            link(V.memset(upad[:, :, 0:3], 0.0))
            link(V.memset(gsc[:, :, :, :], 0.0))
            V.memset(rsb[:, :, :], 0.0).then_inc(once("upad_zero")[0], 1)

            def mod_bias(i, b, at=0):
                dve.wait_ge(mod_turned, i + 1)
                V.tensor_tensor(mod[:, 4 * i:4 * i + 4, :], bank[b][:, at:at + P].rearrange("p (m c) -> p m c", c=32)[:, :, 0:9],
                                small[:, S_BADA + 4 * i:S_BADA + 4 * i + 4].unsqueeze(2).to_broadcast([P, 4, 9]),
                                ALU.add).then_inc(mod_evac, 1)
            for i in range(4):
                mod_bias(i, 2 + i % 2)
            dve.wait_ge(mod_evac, 4)
            dve.wait_ge(*once("upad_zero"))
            norm_mod(0, xT[:, :, :], hT[:, :, :], 8, 0, S_NMIX, rsb[:, 0, :], modA[:, :, :])
            dve.wait_ge(stage("rest_in"), 48)
            for m in range(CONVT + 1):
                if m < CONVT:
                    dve.wait_ge(proj_evac, m + 1)
                    u = upad[:, m % 3, :]
                    y = qkvT[:, m, 0:NPR]
                    link(V.tensor_scalar(y, u[:, 0:NPR], convw[:, m, 0:1], None, ALU.mult))
                    for j in range(1, 3):
                        link(V.scalar_tensor_tensor(y, u[:, j:j + NPR], convw[:, m, j:j + 1], y, ALU.mult, ALU.add))
                    V.scalar_tensor_tensor(y, u[:, 3:3 + NPR], convw[:, m, 3:4], y, ALU.mult, ALU.add).then_inc(conv_done, 1)
                if m >= 1:
                    dve.wait_ge(sig_done, m)
                    V.tensor_tensor(qkvT[:, m - 1, 0:NPR], qkvT[:, m - 1, 0:NPR], sigb[:, (m - 1) % 2, 0:NPR], ALU.mult).then_inc(silu_done, 1)
            for j in range(4):
                dst = smt[:, 0, :, :] if j == 0 else smt[:, 1, :, :]
                link(V.tensor_tensor(dst, samp[:, :, j, :], convw[:, :, j:j + 1].to_broadcast([P, CONVT, NSA]), ALU.mult))
                if j:
                    ins = V.tensor_tensor(smt[:, 0, :, :], smt[:, 0, :, :], smt[:, 1, :, :], ALU.add)
                    if j < 3:
                        link(ins)
                    else:
                        ins.then_inc(stage("conv_s"), 1)
            dve.wait_ge(sig_done, CONVT + 1)
            V.tensor_tensor(qkvT[:, :, NPR:T], smt[:, 0, :, :], smt[:, 1, :, :], ALU.mult).then_inc(silu_done, 1)
            dve.wait_ge(ab_ready, 1)
            dve.wait_ge(dve_line, line[0])
            for i, n in ((0, P), (1, P), (2, NSA)):
                link(V.tensor_copy(gsc[0:n, 0, i, :], bank[6][0:n, 16 * i:16 * i + 8]))
                ins = V.tensor_tensor(gsc[0:n, 1, i, :], bank[6][0:n, 16 * i + 8:16 * i + 16], small[0:n, S_DT:S_DT + 8], ALU.add)
                if i < 2:
                    link(ins)
                else:
                    ins.then_inc(stage("ab_copied"), 1)
            for i in range(4, MOD_PRE):
                mod_bias(i, 2 + i % 2)
                if i == MOD_L2:
                    dve.wait_ge(root_ready, 2)
                    V.reciprocal(rsb[0:2 * H, 0, :], rsb[0:2 * H, 0, :]).then_inc(stage("l2_rs"), 1)
            for i in range(2 * H):
                dve.wait_ge(l2ss, 2 * H + 2 + i)
                V.scalar_tensor_tensor(qkvT[:, i, :], qkvT[:, i, :], P ** -0.5 if i < H else 1.0, bank[L2_BANKS[i % 4]][:, 0:T], ALU.mult, ALU.mult).then_inc(l2done, 1)
                dve.wait_ge(l2done, i + 1)
                if i == H - 1:
                    dve.wait_ge(ab_act, 2)
                    link(V.tensor_scalar(gsc[:, 1, :, :], gsc[:, 1, :, :], 0.0, None, ALU.max))
                    link(V.tensor_tensor(gsc[:, 1, :, :], gsc[:, 1, :, :], gsc[:, 2, :, :], ALU.add))
                    dve.wait_ge(act_line, 3)
                    V.scalar_tensor_tensor(g_tok[:, :, :], gsc[:, 1, :, :], -1.0, gcol[:, 0, :].unsqueeze(1).to_broadcast([P, 3, H]),
                                           ALU.mult, ALU.mult).then_inc(bg_done, 1)
                    dve.wait_ge(bg_done, 1)
                    V.tensor_tensor(bgm[0:NSA, :].rearrange("p (h b) -> p h b", h=H), ident[0:NSA, 0:NSA].unsqueeze(1).to_broadcast([NSA, H, NSA]),
                                    g_tok[0:NSA, 2, :].unsqueeze(2).to_broadcast([NSA, H, NSA]), ALU.mult).then_inc(stage("bgm_ready"), 1)
            dve.wait_ge(*once("cum_ready"))
            dve.wait_ge(stage("egB_ready"), 1)
            V.tensor_copy(cumc[:, :, :], bank[6][:, 64:96].rearrange("p (c e) -> p c e", c=2)).then_inc(once("cum_read")[0], 1)
            dve.wait_ge(*once("cum_read"))
            for c in range(2):
                if c == 1:
                    dve.wait_ge(stage("gd_out"), 2)
                link(V.tensor_copy(gcol[:, 0, :], cumc[:, c, 0:8]))
                link(V.tensor_copy(gsc[:, 0, 0, :], cumc[:, c, 8:16]))
                V.tensor_tensor(gsc[:, 0, 1, :], cumc[:, c, 8:16], cumc[:, c, 0:8], ALU.subtract).then_inc(stage("cum_copied"), 1)
                dve.wait_ge(stage("gexp"), 3 * c + 3)
                link(V.tensor_tensor(gcol[:, 2, :], gcol[:, 1, :], beta_tok[:, c, :], ALU.mult))
                for g in range(2):
                    b0 = 4 - 4 * g
                    hs = slice(4 * g, 4 * g + 4)

                    def heads(v):
                        return v.rearrange("p (h t) -> p h t", h=4)

                    def col(v):
                        return v.unsqueeze(2).to_broadcast([P, 4, P])

                    def row(v):
                        return v.unsqueeze(1).to_broadcast([P, 4, P])
                    dve.wait_ge(stage("gd_prod"), 2 * c + g + 1)
                    dve.wait_ge(stage("eg_done"), 2 * c + g + 1)
                    link(V.tensor_tensor(heads(LTm[:, g, :]), heads(bank[b0][:, :]), col(gcol[:, 0, hs]), ALU.subtract))
                    V.tensor_scalar(LTm[:, g, :], LTm[:, g, :], 0.0, None, ALU.min).then_inc(stage("dif_done"), 1)
                    link(V.tensor_tensor(heads(qg[:, g, :]), heads(XTm[:, g, :]), qkvT[:, hs, c * P:(c + 1) * P], ALU.mult))
                    dve.wait_ge(stage("dec_done"), 2 * c + g + 1)
                    link(V.tensor_tensor(heads(LTm[:, g, :]), heads(LTm[:, g, :]), row(upto), ALU.mult))
                    link(V.tensor_tensor(Aqk[:, g, :], bank[b0 + 3][:, :], LTm[:, g, :], ALU.mult))
                    link(V.tensor_tensor(AT[:, g, :], bank[b0 + 2][:, :], LTm[:, g, :], ALU.mult))
                    link(V.tensor_tensor(AT[:, g, :], bank[b0 + 1][:, :], AT[:, g, :], ALU.mult))
                    link(V.tensor_copy(heads(Xm[:, g, :]), row(ident)))
                    V.tensor_copy(heads(XTm[:, g, :]), row(ident)).then_inc(stage("prep_done"), 1)
                    dve.wait_ge(stage("prep_done"), 2 * c + g + 1)
                    for x in range(2 if g == 0 else 0):
                        xs = slice(4 * x, 4 * x + 4)
                        dve.wait_ge(tr_evac, 4 * c + 2 * x + 2)
                        link(V.tensor_tensor(heads(VB[:, x, :]), heads(VB[:, x, :]), col(beta_tok[:, c, xs]), ALU.mult))
                        if c == 1:
                            link(V.tensor_tensor(heads(KBG[:, x, :]), heads(K2[:, x, :]), col(gcol[:, 2, xs]), ALU.mult))
                        link(V.tensor_tensor(heads(K2[:, x, :]), heads(K2[:, x, :]), col(gcol[:, 3, xs]), ALU.mult))
                dve.wait_ge(mod_turned, MOD_PRE + MOD_GDN * (c + 1))
                for i in range(MOD_GDN):
                    mod_bias(MOD_PRE + MOD_GDN * c + i, 6 + i % 2, P * (i // 2))
                for lv in range(LEVELS):
                    mask = con[:, C_LEV + lv * P:C_LEV + (lv + 1) * P]
                    for g in range(2):
                        q = (c * LEVELS + lv) * 2 + g + 1
                        if lv == 1:
                            dve.wait_ge(stage("lx_done"), q - 2)
                            link(V.tensor_tensor(Xm[:, g, :], Xm[:, g, :], bank[g][:, :], ALU.subtract))
                            V.tensor_tensor(XTm[:, g, :], XTm[:, g, :], LTm[:, g, :], ALU.subtract).then_inc(stage("x_done"), 1)
                            dve.wait_ge(stage("x_done"), q - 2)
                        elif lv >= 2:
                            dve.wait_ge(stage("xlx_done"), doubling(c, lv - 1, g))
                            link(V.tensor_tensor(Xm[:, g, :], Xm[:, g, :], bank[2 + g][:, :], ALU.subtract))
                            V.tensor_tensor(XTm[:, g, :], XTm[:, g, :], bank[4 + g][:, :], ALU.subtract).then_inc(stage("x_done"), 1)
                            dve.wait_ge(stage("x_done"), q - 2)
                        V.tensor_tensor(heads(LTm[:, g, :]), heads(AT[:, g, :]), row(mask), ALU.mult).then_inc(stage("lt_done"), 1)
                for g in range(2):
                    dve.wait_ge(stage("xlx_done"), doubling(c, LEVELS - 1, g))
                    V.tensor_tensor(XTm[:, g, :], XTm[:, g, :], bank[4 + g][:, :], ALU.subtract).then_inc(stage("x_done"), 1)
                for g in range(2):
                    dve.wait_ge(stage("uw_done"), 2 * c + g + 1)
                    if c == 0:
                        V.tensor_copy(VB[:, g, :], bank[g][:, :]).then_inc(stage("vn_done"), 1)
                    else:
                        link(V.tensor_copy(VB[:, g, :], bank[g][:, :]))
                        dve.wait_ge(stage("ws_done"), g + 1)
                        V.tensor_tensor(VB[:, g, :], VB[:, g, :], bank[4 + g][:, :], ALU.subtract).then_inc(stage("vn_done"), 1)
                for g in range(2):
                    dve.wait_ge(stage("os_done"), 2 * c + g + 1)
                    dve.wait_ge(stage("o_copied"), 2 * c + g + 1)
                    if c == 1:
                        link(V.tensor_tensor(heads(Sst[:, g, :]), heads(Sst[:, g, :]), col(gcol[:, 4, 4 * g:4 * g + 4]), ALU.mult))
                        V.tensor_tensor(Sst[:, g, :], Sst[:, g, :], bank[2 + g][:, :], ALU.add).then_inc(stage("gd_out"), 1)
                    else:
                        V.tensor_copy(Sst[:, g, :], bank[2 + g][:, :]).then_inc(stage("gd_out"), 1)
                    dve.wait_ge(stage("gd_out"), 2 * c + g + 1)
            own = con[:, C_OWN:C_OWN + NSA].unsqueeze(2).to_broadcast([P, NSA, P])

            def own_rows(g, out):
                link(V.tensor_tensor(stmp[:, :].rearrange("p (b v) -> p b v", b=NSA),
                                     banks[:, 2 * g:2 * g + 2, :].rearrange("p y (b v) -> p (y b) v", b=4), own, ALU.mult))
                return V.tensor_reduce(out, stmp[:, :].rearrange("p (b v) -> p v b", b=NSA), AX, ALU.add)

            for g in range(2):
                dve.wait_ge(stage("sample_products"), g + 1)
                link(own_rows(g, ksr[:, g, :]))
            dve.wait_ge(stage("sample_products"), 3)
            link(V.tensor_copy(betac[:, :], bank[6][:, 0:2]))
            for g in range(2):
                link(V.tensor_tensor(vnr[:, g, :], bank[4][:, P * g:P * (g + 1)], ksr[:, g, :], ALU.subtract))
                link(V.tensor_scalar(vnr[:, g, :], vnr[:, g, :], betac[:, g:g + 1], None, ALU.mult))
                V.tensor_tensor(vnm[:, g, :].rearrange("p (b v) -> p b v", b=NSA), vnr[:, g, :].unsqueeze(1).to_broadcast([P, NSA, P]),
                                own, ALU.mult).then_inc(stage("vnm_ready"), 1)
            for u in range(4):
                g, y = u // 2, u % 2
                dve.wait_ge(stage("outer"), u + 1)
                S = ssm_view[g][:, :, 4 * y:4 * y + 4, :].rearrange("p h b v -> p h (b v)")
                V.tensor_tensor(S, S, banks[:, 4 * y:4 * y + 4, :], ALU.add).then_inc(stage("snew"), 1)
            for g in range(2):
                dve.wait_ge(stage("oss_ready"), g + 1)
                own_rows(g, ksr[:, g, :]).then_inc(stage("oss_row"), 1)
                dve.wait_ge(stage("oss_row"), g + 1)
            dve.wait_ge(root_ready, 3)
            V.reciprocal(ors[0:H, :], ors[0:H, :]).then_inc(stage("on_root"), 1)
            for h in range(H):
                dve.wait_ge(stage("on_spread"), h + 1)
                V.scalar_tensor_tensor(oG[:, h, :], oG[:, h, :], small[:, S_NGDN:S_NGDN + 1], bank[4 + h % 2][:, 0:T], ALU.mult, ALU.mult).then_inc(stage("on_rs"), 1)
                dve.wait_ge(stage("z_sig"), h + 1)
                V.tensor_tensor(zsig[:, h % 2, :], zsig[:, h % 2, :], bank[h % 4][:, 0:T], ALU.mult).then_inc(stage("z_evac"), 1)
                dve.wait_ge(stage("on_rs"), h + 1)
                dve.wait_ge(stage("z_evac"), h + 1)
                V.tensor_tensor(oG[:, h, :], oG[:, h, :], zsig[:, h % 2, :], ALU.mult).then_inc(stage("z_gated"), 1)

            def rotate(x, turned):
                link(V.tensor_tensor(rot[:, :], turned, sinT, ALU.mult))
                link(V.tensor_tensor(x, x, cosT, ALU.mult))
                return V.tensor_tensor(x, x, rot[:, :], ALU.add)
            dve.wait_ge(*once("kpe_turned"))
            rotate(kpeT[:, :], bank[1][:, 0:T]).then_inc(once("kpe_rot")[0], 1)
            for w in range(2):
                dve.wait_ge(root_ready, 4 + w)
                link(V.reciprocal(mrs[:, w, :], mrs[:, w, :]))
                for i in range(LORA):
                    v = (cqT, latT)[w][:, i, :]
                    nw = (S_NQ, S_NKV)[w] + i
                    ins = V.scalar_tensor_tensor(v, v, small[:, nw:nw + 1], mrs[:, w, :], ALU.mult, ALU.mult)
                    if i < LORA - 1:
                        link(ins)
                    else:
                        ins.then_inc(stage("lat_normed"), 1)
            dve.wait_ge(*once("kpe_rot"))
            for i in range(4):
                dve.wait_ge(stage("q_turn"), i + 1)
                rotate(qpeT[:, i, :], bank[i % 2][:, 0:T]).then_inc(stage("q_turned"), 1)
                dve.wait_ge(stage("q_turned"), i + 1)
            def normalise(j):
                dve.wait_ge(stage("pa_exp"), j + 1)
                st = mstat[:, j % 2, :]
                link(V.reciprocal(st[:, 6:8], st[:, 4:6]))
                link(V.tensor_scalar(mp[j % 2][:, 0:P], mp[j % 2][:, 0:P], st[:, 6:7], None, ALU.mult))
                V.tensor_scalar(mp[j % 2][:, P:384], mp[j % 2][:, P:384], st[:, 7:8], None, ALU.mult).then_inc(stage("pa_probs"), 1)

            for h in range(H + 1):
                if h < H:
                    dve.wait_ge(stage("pa_scores"), h + 1)
                    V.tensor_tensor(msc[h % 2][:, :], bank[h % 2][:, 0:384], neg384, ALU.add).then_inc(stage("pa_masked"), 1)
                    dve.wait_ge(stage("pa_masked"), h + 1)
                    st = mstat[:, h % 2, :]
                    link(V.tensor_reduce(st[:, 0:1], msc[h % 2][:, 0:P], AX, ALU.max))
                    link(V.tensor_reduce(st[:, 1:2], msc[h % 2][:, P:384], AX, ALU.max))
                    V.tensor_scalar(st[:, 2:4], st[:, 0:2], -SCALE, None, ALU.mult).then_inc(stage("pa_max"), 1)
                if h >= 1:
                    normalise(h - 1)
            for q in range(2):
                S, st = ps_[q], sstat[:, q, :]
                dve.wait_ge(stage("snew_scores"), q + 1)
                link(V.tensor_tensor(S[:, 1024:1032], bank[6][:, 0:NSA], con[:, C_B8 + 8 * q:C_B8 + 8 * q + 8], ALU.add))
                link(V.tensor_reduce(st[:, 1:2], S[:, 1024:1032], AX, ALU.max))
                dve.wait_ge(stage("st_ready"), q + 1)
                link(V.tensor_reduce(st[:, 0:1], banks[:, 0:2, :], AXY, ALU.max))
                link(V.tensor_tensor(st[:, 0:1], st[:, 0:1], st[:, 1:2], ALU.max))
                V.tensor_scalar(st[:, 2:3], st[:, 0:1], -SCALE, None, ALU.mult).then_inc(stage("s_max"), 1)
                dve.wait_ge(stage("s_exp"), q + 1)
                link(V.tensor_tensor(st[:, 5:6], st[:, 3:4], st[:, 4:5], ALU.add))
                link(V.reciprocal(st[:, 6:7], st[:, 5:6]))
                V.tensor_scalar(S[:, :], S[:, :], st[:, 6:7], None, ALU.mult).then_inc(stage("p_ready"), 1)
                if q == 0:
                    dve.wait_ge(stage("out_evac"), 8)
                    for m in range(8):
                        dve.wait_ge(stage("gate_sig"), m + 1)
                        V.tensor_tensor(yA[:, m, :], yA[:, m, :], gsig[:, m % 2, :], ALU.mult).then_inc(stage("gated"), 1)
                        dve.wait_ge(stage("gated"), m + 1)
            dve.wait_ge(stage("gate_sig"), 16)
            for m in range(8):
                dve.wait_ge(stage("out_ready"), 25 + m)
                V.tensor_tensor(gB[:, m, :], bank[4 + m % 2][:, 0:T], gB[:, m, :], ALU.mult).then_inc(stage("out_evac"), 1)
                dve.wait_ge(stage("out_evac"), 9 + m)
                V.tensor_tensor(yA[:, m, :], yA[:, m, :], gB[:, m, :], ALU.add).then_inc(stage("merged"), 1)
            for m in range(KD):
                dve.wait_ge(stage("out_ready"), 33 + m)
                b = bank[4 + m % 2]
                link(V.scalar_tensor_tensor(xT[:, m, 0:NPR], b[:, 0:NPR], mod[:, 16 + m, 0:1], xT[:, m, 0:NPR], ALU.mult, ALU.add))
                link(V.tensor_tensor(mrs2[:, 0:NSA], b[:, NPR:T], mod[:, 16 + m, 1:9], ALU.mult))
                V.tensor_tensor(xT[:, m, NPR:T], xT[:, m, NPR:T], mrs2[:, 0:NSA], ALU.add).then_inc(stage("out_evac"), 1)
                dve.wait_ge(stage("out_evac"), 17 + m)
            norm_mod(1, xT[:, :, :], hT[:, :, :], 32, 24, S_NFFN, mrs2[:, :], modA2[:, :, :])
            link(V.memset(lg[:, :, :], 0.0))
            for p_ in pre:
                link(V.memset(p_[:, :, :], 0.0))
            dve.wait_ge(*once("logits_T"))
            V.tensor_copy(gateT[0:NE, :], bank[7][0:NE, 0:T]).then_inc(once("logits_copied")[0], 1)
            dve.wait_ge(*once("logits"))
            br = small[:, S_BR:S_BR + NE]
            link(V.tensor_tensor(lg[:, 0:2, :], bank[5][:, 0:64].rearrange("p (i e) -> p i e", i=2), br.unsqueeze(1).to_broadcast([P, 2, NE]), ALU.add))
            link(V.tensor_tensor(lg[0:NSA, 2, :], bank[5][0:NSA, 64:96], br[0:NSA, :], ALU.add))
            for i in range(3):
                link(V.max(v8[:, i, :], lg[:, i, :]))
            V.tensor_scalar(rst[:, 0, :], v8[:, :, 0], -1.0, None, ALU.mult).then_inc(once("v8_ready")[0], 1)
            fourth = v8[:, :, 3:4].to_broadcast([P, 3, NE])
            link(V.tensor_tensor(sel[:, :, :], lg[:, :, :], fourth, ALU.is_gt))
            link(V.tensor_tensor(eqm[:, :, :], lg[:, :, :], fourth, ALU.is_equal))
            link(V.tensor_reduce(rst[:, 1, :], sel[:, :, :], AX, ALU.add))
            link(V.tensor_scalar(rst[:, 1, :], rst[:, 1, :], -1.0, 4.0, ALU.mult, ALU.add))
            link(V.tensor_copy(pre[0][:, :, 16:48], eqm[:, :, :]))
            for i, s in enumerate((1, 2, 4, 8, 16)):
                a, b = pre[i % 2], pre[(i + 1) % 2]
                link(V.tensor_tensor(b[:, :, 16:48], a[:, :, 16:48], a[:, :, 16 - s:48 - s], ALU.add))
            link(V.tensor_tensor(pre[0][:, :, 16:48], pre[1][:, :, 16:48], rst[:, 1, :].unsqueeze(2).to_broadcast([P, 3, NE]), ALU.is_le))
            link(V.tensor_tensor(eqm[:, :, :], eqm[:, :, :], pre[0][:, :, 16:48], ALU.mult))
            V.tensor_tensor(sel[:, :, :], sel[:, :, :], eqm[:, :, :], ALU.add).then_inc(stage("sel_ready"), 1)
            dve.wait_ge(stage("sel_ready"), 1)
            dve.wait_ge(stage("route_exp"), 3)
            link(V.tensor_tensor(ex[:, :, :], ex[:, :, :], sel[:, :, :], ALU.mult))
            link(V.tensor_reduce(rst[:, 2, :], ex[:, :, :], AX, ALU.add))
            link(V.reciprocal(rst[:, 3, :], rst[:, 2, :]))
            V.tensor_tensor(gate[:, :, :], ex[:, :, :], rst[:, 3, :].unsqueeze(2).to_broadcast([P, 3, NE]), ALU.mult).then_inc(stage("sel_ready"), 1)
            dve.wait_ge(stage("route"), 1)
            link(V.tensor_copy(cntc[0:NE, 4:5], bank[7][0:NE, 0:1]))
            link(V.scalar_tensor_tensor(cntc[0:NE, 0:1], cntc[0:NE, 4:5], 0.0, ident[0:NE, 0:1], ALU.is_gt, ALU.max))
            for i in range(1, 5):
                ins = V.scalar_tensor_tensor(cntc[0:NE, 0:1], cntc[0:NE, 4:5], float(SLOT * i), cntc[0:NE, 0:1], ALU.is_gt, ALU.add)
                if i < 4:
                    link(ins)
                else:
                    ins.then_inc(stage("blocks"), 1)
            dve.wait_ge(stage("blocks"), 1)
            dve.wait_ge(stage("route"), 2)
            link(V.tensor_copy(cntc[0:NE, 1:2], bank[7][0:NE, 1:2]))
            link(V.tensor_tensor(cntc[0:NE, 2:3], cntc[0:NE, 1:2], cntc[0:NE, 0:1], ALU.add))
            link(V.tensor_scalar(cntc[0:NE, 3:4], cntc[0:NE, 1:2], float(SLOT), 1.0, ALU.mult, ALU.add))
            jrow = con[0:NE, C_J:C_J + NJ1]
            link(V.tensor_scalar(ge1[0:NE, :], jrow, cntc[0:NE, 1:2], None, ALU.is_ge))
            V.scalar_tensor_tensor(e1h[0:NE, :], jrow, cntc[0:NE, 2:3], ge1[0:NE, :], ALU.is_lt, ALU.mult).then_inc(once("e1h_ready")[0], 1)
            link(V.tensor_copy(maskT[0:NE, :], bank[4][0:NE, 0:T]))
            link(V.tensor_copy(gateT[0:NE, :], bank[0][0:NE, 0:T]))
            V.scalar_tensor_tensor(m1T[0:NE, :], bank[6][0:NE, 0:T], cntc[0:NE, 3:4], maskT[0:NE, :], ALU.add, ALU.mult).then_inc(once("m1_ready")[0], 1)
            dve.wait_ge(stage("route"), 3)
            link(V.tensor_copy(items[0:1, 1:1 + NJ1], bank[7][0:1, 8:8 + NJ1]))
            V.tensor_copy(items[0:1, 0:1], bank[7][0:1, 2:3]).then_inc(once("items_ready")[0], 1)
            dve.wait_ge(stage("route"), 4)
            for i, n in ((0, P), (1, P), (2, NSA)):
                link(V.tensor_tensor(rr[0:n, i, :], bank[1][0:n, NJ1 * i:NJ1 * (i + 1)], con[0:n, C_J64:C_J64 + NJ1], ALU.subtract))
                ins = V.tensor_copy(gg[0:n, i, :], bank[2][0:n, NJ1 * i:NJ1 * (i + 1)])
                if i < 2:
                    link(ins)
                else:
                    ins.then_inc(stage("rg_copied"), 1)
            dve.wait_ge(stage("rg_copied"), 1)
            dve.wait_ge(*once("items_ready"))
            moe_vector(dve, link)
            link(V.tensor_tensor(acc[:, :, NPR:T], acc[:, :, NPR:T], mod[:, 40:48, 1:9], ALU.mult))
            link(V.tensor_tensor(xT[:, :, NPR:T], xT[:, :, NPR:T], acc[:, :, NPR:T], ALU.add))
            for m in range(KD):
                V.scalar_tensor_tensor(xT[:, m, 0:NPR], acc[:, m, 0:NPR], mod[:, 40 + m, 0:1], xT[:, m, 0:NPR], ALU.mult, ALU.add).then_inc(stage("x2_ready"), 1)
            dve.wait_ge(stage("x2_ready"), KD)
            norm_mod(2, xT[:, :, :], yout[:, :, :], 56, 48, S_NFIN, mrs2[:, :], modA2[:, :, :])

        @block.gpsimd
        def _(pool):
            pool.wait_ge(h_ready, 1)
            pool.wait_ge(silu_done, CONVT + 1)
            pool.wait_ge(proj_evac, CONVT)
            pool.dma_start(t["o_convp"], convp[:, :, :]).then_inc(stored, 16)
            pool.dma_start(t["o_convs"], samp[:, :, :, :]).then_inc(stored, 16)
            pool.wait_ge(stage("egB_ready"), 1)
            for g in range(2):
                pool.wait_ge(slot_in[(SSM + g) % RING], arrive[SSM + g])
                S = ssm_view[g].rearrange("p h b v -> p (h b) v")
                nc.gpsimd.tensor_tensor(S, S, egB[:, 32 * g:32 * g + 32].unsqueeze(2).to_broadcast([P, 32, P]), ALU.mult).then_inc(stage("decayed"), 1)
            pool.wait_ge(stage("lt_done"), 4 * LEVELS)
            nc.gpsimd.memset(x32[:, :, :], 0.0).then_inc(once("x32_zero")[0], 1)
            pool.wait_ge(stage("gd_out"), 4)
            nc.gpsimd.memset(krow[:, :, :, :], 0.0).then_inc(once("krow_zero")[0], 1)
            pool.dma_start(t["o_ssmp"], Sst[:, :, :]).then_inc(stage("ssmp_stored"), 16)
            for i in range(2):
                pool.wait_ge(stage("snew"), 2 * i + 2)
                pool.dma_start(t["o_ssms"][i, :, :], ring[(SSM + i) % RING][:, :]).then_inc(stage(f"ssm_stored{i}"), 16)
            pool.wait_ge(*once("kpe_rot"))
            pool.dma_start(t["o_kpe"], kpeT[0:ROPE, :]).then_inc(stored, 16)
            pool.wait_ge(stage("lat_normed"), 2)
            pool.dma_start(t["o_lat"], latT[:, :, :]).then_inc(stored, 16)
            pool.wait_ge(stage("pa_ready"), 8)
            nc.gpsimd.memset(regC[:, 2376:4424], 0.0)
            nc.gpsimd.memset(regC[:, mlat:mlat + 512], 0.0).then_inc(once("att_zero")[0], 1)
            pool.wait_ge(stage("merged"), KD)
            nc.gpsimd.memset(acc[:, :, :], 0.0).then_inc(acc_added, 1)
            pool.wait_ge(stored, 64)
            pool.wait_ge(stage("ssm_stored0"), 16)
            pool.wait_ge(stage("ssm_stored1"), 16)
            pool.wait_ge(stage("ssmp_stored"), 16)


Q0, Z0, B0, CQ0, CKV0, KPE0, GA0, GB0 = 0, 3072, 4096, 4112, 4624, 5136, 5200, 6224


def wp_index(n):
    if n < SSM:
        return n
    return n - 2 - sum(c < n for c in KV_OF)


def lay_out(i):
    f = np.float32

    def cols(w, c0, n):
        w = w[:, c0:c0 + 512 * n].reshape(-1, P, n, 512)
        return w.transpose(2, 1, 0, 3).reshape(n, P, -1)

    def vec(v):
        return v.reshape(-1, P).T

    w_in = i["w_in"][0]
    w_uq = i["w_uq"][0].reshape(LORA, P, H, 192)
    half = np.zeros((P, 2048), f)
    uqr = w_uq[..., 128:].reshape(LORA, P, 512).transpose(1, 0, 2).reshape(P, 2048)
    uk = i["w_uk"][0].reshape(H, LORA, P, P)
    uv = i["w_uv"][0].reshape(H, LORA, P, P).transpose(2, 1, 0, 3).reshape(1, P, CH)
    wpre = np.concatenate([
        cols(i["w_ada"][0], 0, 4), cols(w_in, Q0, 6), cols(i["w_ada"][0], 2048, 8), cols(i["w_ada_final"], 0, 4),
        cols(w_in, Z0, 2),
        cols(w_in, CQ0, 1), cols(w_in, CKV0, 1),
        w_uq[..., :128].reshape(LORA, P, 1024).transpose(1, 0, 2).reshape(1, P, CH),
        np.concatenate([uqr, half], 1)[None],
        uv, uk.transpose(2, 1, 0, 3).reshape(1, P, CH),
        i["w_uk"][0].transpose(2, 0, 1).reshape(1, P, CH),
        cols(i["w_o_gdn"][0], 0, 2), cols(w_in, GA0, 2), cols(w_in, GB0, 2), uv, cols(i["w_o_mla"][0], 0, 2),
        cols(i["w_out"][0], 0, 2)], 0)
    n = np.arange(P)
    con = np.zeros((P, NCONST), f)
    con[:, C_ID:C_ID + P] = np.eye(P)
    con[:, C_ONE:C_ONE + P] = 1
    con[:, C_U:C_U + P] = n[:, None] <= n[None]
    con[:, C_STR:C_STR + P] = n[:, None] < n[None]
    con[:, C_PERM:C_PERM + P] = n[:, None] == (n[None] ^ 32)
    for lv in range(LEVELS):
        b = 1 << lv
        con[:, C_LEV + lv * P:C_LEV + (lv + 1) * P] = ((n[:, None] // (2 * b) == n[None] // (2 * b))
                                                     & (n[:, None] // b % 2 == 0) & (n[None] // b % 2 == 1))
    inv = f(10000.0) ** (-np.arange(32, dtype=f) / f(32))
    pos = np.concatenate([np.arange(NPR), np.full(NSA, PAGES * P)]).astype(f)
    ang = inv[n % 32][:, None] * pos[None]
    con[:, C_COS:C_COS + T] = np.cos(ang)
    con[:, C_SIN:C_SIN + T] = np.sin(ang) * np.where(n % 64 < 32, -1, 1)[:, None]
    low = np.where(n[None] <= n[:, None], 0, NEG)
    con[:, C_NEG:C_NEG + P] = low
    con[:, C_NEG + 256:C_NEG + 384] = low
    con[:, C_IOTA:C_IOTA + SLOT] = np.arange(SLOT)
    con[:, C_J:C_J + NJ1] = np.arange(NJ1)
    con[:, C_J64:C_J64 + NJ1] = SLOT * np.arange(NJ1) + 1
    con[:, C_E] = n
    con[:, C_EPS] = EPS
    con[:, C_COL:] = np.arange(4 * H - 1) == 2 * H - 1
    con[:, C_OWN:C_OWN + NSA] = n[:, None] % 32 == np.arange(NSA)[None]
    con[0:2, C_TWO:C_TWO + P] = np.arange(2)[:, None] == n[None] // 64
    con[:, C_B8:C_B8 + 16] = np.where(np.arange(16)[None] // 8 * 4 + n[:, None] // 32 == np.arange(16)[None] % 8, 0, NEG)
    small = np.empty((P, NSMALL), f)
    small[:, S_NMIX:S_NMIX + 8] = vec(i["norm_mix_w"])
    small[:, S_NFFN:S_NFFN + 8] = vec(i["norm_ffn_w"])
    small[:, S_NFIN:S_NFIN + 8] = vec(i["norm_final_w"])
    small[:, S_NQ:S_NQ + 4] = vec(i["q_norm_w"])
    small[:, S_NKV:S_NKV + 4] = vec(i["kv_norm_w"])
    small[:, S_NGDN:S_NGDN + 1] = vec(i["gdn_norm_w"])
    small[:, S_BADA:S_BADA + 64] = np.concatenate([vec(i["b_ada"]), vec(i["b_ada_final"])], 1)
    small[:, S_ALOG:S_ALOG + 8] = i["A_log"]
    small[:, S_DT:S_DT + 8] = i["dt_bias"]
    small[:, S_BR:S_BR + NE] = i["b_router"]
    small[:, S_CW:S_CW + CONVT * 4] = i["conv_w"][0].reshape(CONVT, P, 4).transpose(1, 0, 2).reshape(P, -1)
    kpe = w_in[:, KPE0:KPE0 + ROPE]
    small[:, S_WSM:S_WSM + KD * WSM] = np.concatenate([w_in[:, B0:B0 + 16], kpe, i["w_router"][0]],
                                                      1).reshape(KD, P, WSM).transpose(1, 0, 2).reshape(P, -1)
    c = np.concatenate([i["c_prompt"], i["c_sample"], np.zeros((23, D), f)], 0)
    small[:, S_CT:] = c.T.reshape(KD, P, 32).transpose(1, 0, 2).reshape(P, -1)
    x = np.concatenate([i["x_prompt"][0], i["x_sample"][:, 0]], 0)
    conv = np.zeros((P, CONVT, 4, NSA), f)
    conv[:, :, 0:3] = i["state_conv"][0].reshape(NSA, 3, CONVT, P).transpose(3, 2, 1, 0)
    kv = i["cache_kv"][0]
    return {
        "small": small,
        "biases": np.concatenate([i["b_gu"][0].reshape(NE, 2, 2, 512), i["b_dn"][0].reshape(NE, 1, 2, 512)],
                                 1).transpose(0, 2, 1, 3).reshape(NE, 2, -1),
        "con": con,
        "xT": x.T.reshape(KD, P, T).transpose(1, 0, 2),
        "convT": conv,
        "pages": i["page_table"].reshape(1, -1),
        "wpre": wpre,
        "ssm": i["state_ssm"][0].reshape(NSA, 2, 4, P, P).transpose(1, 3, 2, 0, 4).reshape(2, P, CH),
        "kvT": kv.reshape(NPHYS, P, LORA, P).transpose(0, 3, 2, 1).reshape(NPHYS, P, 512),
        "kv": kv,
        "peT": i["cache_pe"][0].transpose(0, 2, 1),
        "w_gu": i["w_gu"][0],
        "w_dn": i["w_dn"][0],
    }


OUTS = {
    "o_y": (P, KD, T), "o_lat": (P, LORA, T), "o_kpe": (ROPE, T), "o_ssmp": (P, 2, 512),
    "o_convp": (P, CONVT, 3), "o_ssms": (2, P, CH), "o_convs": (P, CONVT, 4, NSA),
}


def kernel(**inputs):
    import concourse.bacc as bacc
    from concourse.bass_utils import run_bass_kernel_spmd

    nc = bacc.Bacc("TRN2", target_bir_lowering=False, num_devices=1)
    arrays = {k: np.ascontiguousarray(v) for k, v in lay_out({k: np.asarray(v) for k, v in inputs.items()}).items()}
    t = {k: nc.dram_tensor(k, v.shape, mybir.dt.from_np(v.dtype), kind="ExternalInput").ap() for k, v in arrays.items()}
    for k, shape in OUTS.items():
        t[k] = nc.dram_tensor(k, shape, F32, kind="ExternalOutput").ap()
    build_program(nc, t)
    r = run_bass_kernel_spmd(nc, [arrays], core_ids=[0]).results[0]

    def rows(v):
        return v.transpose(2, 1, 0).reshape(v.shape[2], -1)
    y, lat, kpe = rows(r["o_y"]), rows(r["o_lat"]), r["o_kpe"].T
    ssmp = r["o_ssmp"].reshape(P, H, P).transpose(1, 0, 2)
    convp = r["o_convp"].transpose(2, 1, 0).reshape(1, 1, 3, -1)
    ssms = r["o_ssms"].reshape(2, P, 4, NSA, P).transpose(3, 0, 2, 1, 4).reshape(1, NSA, H, P, P)
    convs = r["o_convs"][:, :, 1:4, :].transpose(3, 2, 1, 0).reshape(1, NSA, 3, -1)
    c = np.ascontiguousarray
    return (c(y[None, :NPR]), c(y[NPR:, None]), c(lat[None, None, :NPR]), c(kpe[None, None, :NPR]), c(ssmp[None, None]),
            c(convp), c(lat[None, NPR:, None]), c(kpe[None, NPR:, None]), c(ssms), c(convs))
```
